# Optimizing a Trainium2 kernel written in Bass

```python
import math
import jax, jax.numpy as jnp
from jax import lax
import numpy as np

D_MODEL = 1024
BATCH = 1
SEQ = 1024
DEPTH = 1
DEC_BATCH = 8
DEC_SEQ = 4
PAST_LEN = 8192
PAGE_SIZE = 128

HEAD_DIM = 64
D_A = D_MODEL // 2
N_HEADS_A = D_A // HEAD_DIM
DILATED_PATTERNS = ((128, 1), (512, 4), (2048, 16))
MAX_WINDOW = max(w for w, _ in DILATED_PATTERNS)
BAND_BLOCK = 128
POOL_WINDOWS = (2, 4, 8, 16)
N_POOL_GROUPS = len(POOL_WINDOWS)
D_B = D_MODEL // 4
POOL_GROUP_DIM = D_B // N_POOL_GROUPS
POOL_BUF = max(POOL_WINDOWS) - 1
D_C = D_MODEL // 4
N_HEADS_C = D_C // HEAD_DIM
N_MEM = 256
D_MIX = D_A + D_B + D_C
D_IN = 3 * D_A + D_B + D_C
SPLITS = (D_A, 2 * D_A, 3 * D_A, 3 * D_A + D_B)
N_EXPERT_GROUPS = 4
EXPERTS_PER_GROUP = 8
TOP_K_INNER = 2
D_EXPERT = D_MODEL // 4
DN_ALPHA = (2.0 * DEPTH) ** 0.25
DN_BETA = (8.0 * DEPTH) ** -0.25
LN_EPS = 1e-5
ATTN_SCALE = HEAD_DIM ** -0.5

kernel_name = "hymba_dilated_pool_hmoe_step"

def alibi_slopes(n):
    return 2.0 ** (-8.0 * jnp.arange(1, n + 1, dtype=jnp.float32) / n)

def layer_norm(x, g, b):
    xf = x.astype(jnp.float32)
    mu = jnp.mean(xf, -1, keepdims=True)
    var = jnp.mean(jnp.square(xf - mu), -1, keepdims=True)
    return ((xf - mu) * lax.rsqrt(var + LN_EPS) * g.astype(jnp.float32) + b.astype(jnp.float32)).astype(x.dtype)

def _heads(t, h):
    return t.reshape(t.shape[:-1] + (h, HEAD_DIM))

def _to_strided(t, d):
    B, S = t.shape[:2]
    rest = t.shape[2:]
    t = jnp.swapaxes(t.reshape((B, S // d, d) + rest), 1, 2)
    return t.reshape((B * d, S // d) + rest)

def _from_strided(t, B, d):
    L = t.shape[1]
    rest = t.shape[2:]
    t = jnp.swapaxes(t.reshape((B, d, L) + rest), 1, 2)
    return t.reshape((B, L * d) + rest)

def _dilated_band_prompt(q, k, v, window, dilation, slopes):
    B = q.shape[0]
    n_steps = window // dilation
    blk = BAND_BLOCK
    qs, ks, vs = _to_strided(q, dilation), _to_strided(k, dilation), _to_strided(v, dilation)
    N, L, H, hd = qs.shape
    nb = -(-L // blk)
    Lp = nb * blk
    qb = jnp.pad(qs, ((0, 0), (0, Lp - L), (0, 0), (0, 0))).reshape(N, nb, blk, H, hd)

    def band(t):
        t = jnp.pad(t, ((0, 0), (blk, Lp - L), (0, 0), (0, 0))).reshape(N, nb + 1, blk, H, hd)
        return jnp.concatenate([t[:, :-1], t[:, 1:]], axis=2)

    kb, vb = band(ks), band(vs)
    s = jnp.einsum('nbqhd,nbkhd->nbhqk', qb, kb).astype(jnp.float32) * ATTN_SCALE
    steps = jnp.arange(blk)[:, None] + blk - jnp.arange(2 * blk)[None, :]
    key_pos = jnp.arange(nb)[:, None] * blk - blk + jnp.arange(2 * blk)[None, :]
    valid = ((steps >= 0) & (steps <= n_steps))[None] & (key_pos >= 0)[:, None, :]
    dist = (steps * dilation).astype(jnp.float32)
    s = s - slopes[:, None, None] * dist[None]
    s = jnp.where(valid[None, :, None], s, -jnp.inf)
    m = jnp.max(s, -1, keepdims=True)
    p = jnp.exp(s - m)
    den = jnp.sum(p, -1)
    o = jnp.einsum('nbhqk,nbkhd->nbqhd', p, vb.astype(jnp.float32)) / jnp.swapaxes(den, 2, 3)[..., None]
    lse = jnp.swapaxes(m[..., 0] + jnp.log(den), 2, 3)
    o = o.reshape(N, Lp, H, hd)[:, :L]
    lse = lse.reshape(N, Lp, H)[:, :L]
    return _from_strided(o, B, dilation), _from_strided(lse, B, dilation)

def _dilated_sample(q, kc, vc, wb, slopes):
    T = q.shape[1]
    outs, lses = [], []
    for window, dil in DILATED_PATTERNS:
        n_steps = window // dil
        i = jnp.arange(n_steps + 1)
        idx = wb + jnp.arange(T)[:, None] - i[None, :] * dil
        valid = idx >= 0
        idxc = jnp.maximum(idx, 0)
        kg, vg = kc[:, idxc], vc[:, idxc]
        s = jnp.einsum('bthd,btnhd->bhtn', q, kg).astype(jnp.float32) * ATTN_SCALE
        s = s - slopes[:, None, None] * (i * dil).astype(jnp.float32)[None, None, :]
        s = jnp.where(valid[None, None], s, -jnp.inf)
        m = jnp.max(s, -1, keepdims=True)
        p = jnp.exp(s - m)
        den = jnp.sum(p, -1)
        o = jnp.einsum('bhtn,btnhd->bthd', p, vg.astype(jnp.float32)) / jnp.swapaxes(den, 1, 2)[..., None]
        outs.append(o)
        lses.append(jnp.swapaxes(m[..., 0] + jnp.log(den), 1, 2))
    return _mix_dilations(outs, lses)

def _mix_dilations(outs, lses):
    w = jax.nn.softmax(jnp.stack(lses), axis=0)
    return jnp.sum(w[..., None] * jnp.stack(outs), axis=0)

def _multi_pool(u, pos, w_pool, pool_scale):
    N, L, _ = u.shape
    uf = u.astype(jnp.float32)
    c = jnp.cumsum(uf, axis=1)
    pooled = []
    for g, w in enumerate(POOL_WINDOWS):
        cg = c[..., g * POOL_GROUP_DIM:(g + 1) * POOL_GROUP_DIM]
        lag = jnp.pad(cg, ((0, 0), (w, 0), (0, 0)))[:, :L]
        cnt = jnp.minimum(w, pos + 1).astype(jnp.float32)
        pooled.append((cg - lag) / cnt[None, :, None])
    diff = jnp.stack(pooled, axis=2) - uf.reshape(N, L, N_POOL_GROUPS, POOL_GROUP_DIM)
    out = jnp.einsum('nlgc,gce->nlge', diff, w_pool.astype(jnp.float32)).reshape(N, L, D_B)
    return out * pool_scale.astype(jnp.float32)

def _mem_attention(q, km, vm):
    s = jnp.einsum('nlhd,nmhd->nhlm', q, km).astype(jnp.float32) * ATTN_SCALE
    p = jax.nn.softmax(s, axis=-1)
    return jnp.einsum('nhlm,nmhd->nlhd', p, vm.astype(jnp.float32))

def _merge(x, attn, pool, memo, w_o):
    lead = x.shape[:2]
    cat = jnp.concatenate([attn.reshape(lead + (D_A,)).astype(x.dtype), pool.astype(x.dtype),
                           memo.reshape(lead + (D_C,)).astype(x.dtype)], axis=-1)
    return cat @ w_o

def _mixer_prompt(x, mem, w_in, w_mem_kv, w_pool, pool_scale, w_o):
    B, S, _ = x.shape
    slopes = alibi_slopes(N_HEADS_A)
    q_a, k_a, v_a, u_b, q_c = jnp.split(x @ w_in, SPLITS, axis=-1)
    q_a, k_a, v_a = _heads(q_a, N_HEADS_A), _heads(k_a, N_HEADS_A), _heads(v_a, N_HEADS_A)
    outs, lses = [], []
    for window, dil in DILATED_PATTERNS:
        o, l = _dilated_band_prompt(q_a, k_a, v_a, window, dil, slopes)
        outs.append(o)
        lses.append(l)
    attn = _mix_dilations(outs, lses)
    pool = _multi_pool(u_b, jnp.arange(S), w_pool, pool_scale)
    km, vm = jnp.split(mem @ w_mem_kv, 2, axis=-1)
    km, vm = _heads(km, N_HEADS_C), _heads(vm, N_HEADS_C)
    memo = _mem_attention(_heads(q_c, N_HEADS_C), km, vm)
    y = _merge(x, attn, pool, memo, w_o)
    wbp = min(MAX_WINDOW, S)
    return y, k_a[:, S - wbp:], v_a[:, S - wbp:], u_b[:, S - POOL_BUF:], km, vm

def _mixer_sample(x, win_k, win_v, pool_buf, mem_k, mem_v, w_in, w_pool, pool_scale, w_o):
    T = x.shape[1]
    wb = win_k.shape[1]
    pb = pool_buf.shape[1]
    slopes = alibi_slopes(N_HEADS_A)
    q_a, k_a, v_a, u_b, q_c = jnp.split(x @ w_in, SPLITS, axis=-1)
    q_a, k_a, v_a = _heads(q_a, N_HEADS_A), _heads(k_a, N_HEADS_A), _heads(v_a, N_HEADS_A)
    kc = jnp.concatenate([win_k.astype(k_a.dtype), k_a], axis=1)
    vc = jnp.concatenate([win_v.astype(v_a.dtype), v_a], axis=1)
    attn = _dilated_sample(q_a, kc, vc, wb, slopes)
    useq = jnp.concatenate([pool_buf.astype(u_b.dtype), u_b], axis=1)
    pos = PAST_LEN - pb + jnp.arange(pb + T)
    pool = _multi_pool(useq, pos, w_pool, pool_scale)[:, pb:]
    memo = _mem_attention(_heads(q_c, N_HEADS_C), mem_k, mem_v)
    y = _merge(x, attn, pool, memo, w_o)
    return y, kc[:, T:], vc[:, T:], useq[:, T:]

def _hier_moe(x, w_r1, b_r1, w_r2, b_r2, w_gate, w_up, w_down):
    p1 = jax.nn.softmax((x @ w_r1).astype(jnp.float32) + b_r1.astype(jnp.float32), axis=-1)
    v1, g_sel = lax.top_k(p1, 1)
    l2 = jnp.einsum('nd,gde->nge', x, w_r2).astype(jnp.float32) + b_r2.astype(jnp.float32)
    l2_sel = jnp.take_along_axis(l2, g_sel[:, :, None], axis=1)[:, 0]
    v2, e_idx = lax.top_k(l2_sel, TOP_K_INNER)
    w2 = jax.nn.softmax(v2, axis=-1)
    inner = jnp.sum(w2[..., None] * jax.nn.one_hot(e_idx, EXPERTS_PER_GROUP, dtype=jnp.float32), axis=1)
    gate = v1[:, 0, None, None] * jax.nn.one_hot(g_sel[:, 0], N_EXPERT_GROUPS, dtype=jnp.float32)[:, :, None] * inner[:, None, :]
    y = jnp.zeros(x.shape, jnp.float32)
    for g in range(N_EXPERT_GROUPS):
        hg = jnp.einsum('nd,edf->nef', x, w_gate[g])
        hu = jnp.einsum('nd,edf->nef', x, w_up[g])
        a = jax.nn.silu(hg) * hu * gate[:, g, :, None].astype(x.dtype)
        y = y + jnp.einsum('nef,efd->nd', a, w_down[g]).astype(jnp.float32)
    return y.astype(x.dtype)

def _post_block(x, mix, ln1_g, ln1_b, ln2_g, ln2_b, w_r1, b_r1, w_r2, b_r2, w_gate, w_up, w_down):
    h1 = layer_norm(DN_ALPHA * x + mix, ln1_g, ln1_b)
    f = _hier_moe(h1.reshape(-1, h1.shape[-1]), w_r1, b_r1, w_r2, b_r2, w_gate, w_up, w_down).reshape(h1.shape)
    return layer_norm(DN_ALPHA * h1 + f, ln2_g, ln2_b)

def setup_inputs(seed: int = 0) -> dict:
    key = jax.random.key(seed)
    ks = jax.random.split(key, 24)
    wb = min(MAX_WINDOW, PAST_LEN)
    nrm = jax.random.normal
    f32 = jnp.float32
    return {
        "x_prompt": nrm(ks[0], (BATCH, SEQ, D_MODEL), f32),
        "x_sample": nrm(ks[1], (DEC_BATCH, DEC_SEQ, D_MODEL), f32),
        "cache_win_k": nrm(ks[2], (DEPTH, DEC_BATCH, wb, N_HEADS_A, HEAD_DIM), f32),
        "cache_win_v": nrm(ks[3], (DEPTH, DEC_BATCH, wb, N_HEADS_A, HEAD_DIM), f32),
        "state_pool": nrm(ks[4], (DEPTH, DEC_BATCH, POOL_BUF, D_B), f32),
        "cache_mem_k": nrm(ks[5], (DEPTH, DEC_BATCH, N_MEM, N_HEADS_C, HEAD_DIM), f32),
        "cache_mem_v": nrm(ks[6], (DEPTH, DEC_BATCH, N_MEM, N_HEADS_C, HEAD_DIM), f32),
        "mem_prompt": nrm(ks[7], (BATCH, N_MEM, D_MODEL), f32),
        "w_in": nrm(ks[8], (DEPTH, D_MODEL, D_IN), f32) * D_MODEL ** -0.5,
        "w_mem_kv": nrm(ks[9], (DEPTH, D_MODEL, 2 * D_C), f32) * D_MODEL ** -0.5,
        "w_pool": nrm(ks[10], (DEPTH, N_POOL_GROUPS, POOL_GROUP_DIM, POOL_GROUP_DIM), f32) * POOL_GROUP_DIM ** -0.5,
        "pool_scale": 1.0 + 0.1 * nrm(ks[11], (DEPTH, D_B), f32),
        "w_o": nrm(ks[12], (DEPTH, D_MIX, D_MODEL), f32) * (D_MIX ** -0.5 * DN_BETA),
        "ln1_g": 1.0 + 0.05 * nrm(ks[13], (DEPTH, D_MODEL), f32),
        "ln1_b": 0.02 * nrm(ks[14], (DEPTH, D_MODEL), f32),
        "ln2_g": 1.0 + 0.05 * nrm(ks[15], (DEPTH, D_MODEL), f32),
        "ln2_b": 0.02 * nrm(ks[16], (DEPTH, D_MODEL), f32),
        "w_r1": nrm(ks[17], (DEPTH, D_MODEL, N_EXPERT_GROUPS), f32) * D_MODEL ** -0.5,
        "b_r1": 0.01 * nrm(ks[18], (DEPTH, N_EXPERT_GROUPS), f32),
        "w_r2": nrm(ks[19], (DEPTH, N_EXPERT_GROUPS, D_MODEL, EXPERTS_PER_GROUP), f32) * D_MODEL ** -0.5,
        "b_r2": 0.01 * nrm(ks[20], (DEPTH, N_EXPERT_GROUPS, EXPERTS_PER_GROUP), f32),
        "w_gate": nrm(ks[21], (DEPTH, N_EXPERT_GROUPS, EXPERTS_PER_GROUP, D_MODEL, D_EXPERT), f32) * D_MODEL ** -0.5,
        "w_up": nrm(ks[22], (DEPTH, N_EXPERT_GROUPS, EXPERTS_PER_GROUP, D_MODEL, D_EXPERT), f32) * D_MODEL ** -0.5,
        "w_down": nrm(ks[23], (DEPTH, N_EXPERT_GROUPS, EXPERTS_PER_GROUP, D_EXPERT, D_MODEL), f32) * (D_EXPERT ** -0.5 * DN_BETA),
    }

def reference(x_prompt, x_sample, cache_win_k, cache_win_v, state_pool, cache_mem_k, cache_mem_v, mem_prompt,
              w_in, w_mem_kv, w_pool, pool_scale, w_o, ln1_g, ln1_b, ln2_g, ln2_b,
              w_r1, b_r1, w_r2, b_r2, w_gate, w_up, w_down):
    h_p, h_s = x_prompt, x_sample
    wk_p, wv_p, pl_p, mk_p, mv_p = [], [], [], [], []
    wk_s, wv_s, pl_s = [], [], []
    for l in range(DEPTH):
        mix_p, k_new, v_new, u_new, km, vm = _mixer_prompt(h_p, mem_prompt, w_in[l], w_mem_kv[l], w_pool[l], pool_scale[l], w_o[l])
        h_p = _post_block(h_p, mix_p, ln1_g[l], ln1_b[l], ln2_g[l], ln2_b[l], w_r1[l], b_r1[l], w_r2[l], b_r2[l], w_gate[l], w_up[l], w_down[l])
        wk_p.append(k_new); wv_p.append(v_new); pl_p.append(u_new); mk_p.append(km); mv_p.append(vm)
        mix_s, kbuf, vbuf, ubuf = _mixer_sample(h_s, cache_win_k[l], cache_win_v[l], state_pool[l], cache_mem_k[l], cache_mem_v[l], w_in[l], w_pool[l], pool_scale[l], w_o[l])
        h_s = _post_block(h_s, mix_s, ln1_g[l], ln1_b[l], ln2_g[l], ln2_b[l], w_r1[l], b_r1[l], w_r2[l], b_r2[l], w_gate[l], w_up[l], w_down[l])
        wk_s.append(kbuf); wv_s.append(vbuf); pl_s.append(ubuf)
    return (h_p, h_s, jnp.stack(wk_p), jnp.stack(wv_p), jnp.stack(pl_p), jnp.stack(mk_p), jnp.stack(mv_p),
            jnp.stack(wk_s), jnp.stack(wv_s), jnp.stack(pl_s))


_drawn_inputs = setup_inputs


def setup_inputs(seed=0):
    import zlib

    import numpy as np

    out = dict(_drawn_inputs(seed))
    spreads = {}
    factors = {'ln2_b': 2.858, 'b_r1': 7.765, 'b_r2': 13.933}
    for name, (base, spread) in spreads.items():
        noise = np.random.default_rng([zlib.crc32(name.encode()), seed]).standard_normal(out[name].shape)
        drawn = base * np.exp(spread * noise) if base else spread * noise
        out[name] = __import__('jax').numpy.asarray(drawn.astype(out[name].dtype))
    for name, factor in factors.items():
        out[name] = (out[name] * factor).astype(out[name].dtype)
    return out
```

```python
from contextlib import ExitStack

import concourse.bass as bass
import numpy as np
from concourse import mybir

F32 = mybir.dt.float32
U32 = mybir.dt.uint32
ALU = mybir.AluOpType
ACT = mybir.ActivationFunctionType
AX = mybir.AxisListType

P = 128
D = 1024
KT = D // P
SEQ = 1024
DB, DT = 8, 4
SMP = DB * DT
TOK = SEQ + SMP
CH = SEQ // P + 1
HD = 64
HA, HC = 8, 4
D_A, D_B, D_C = 512, 256, 256
N_MEM = 256
WB = 2048
PB = 15
PATTERNS = ((128, 1), (512, 4), (2048, 16))
NG, EPG = 4, 8
NE = NG * EPG
DE = 256
ALPHA = 2.0 ** 0.25
EPS = 1e-5
QS = -(HD ** -0.5)
MASKED = 1e30

FAR = [16 * j + t for j in range((WB - 512) // 16) for t in range(DT)]
NEAR = list(range(WB - 512, WB))
ROWS = FAR + NEAR
NK = len(ROWS)
KC = NK // 4
NVT = NK // P

CAP = 128
NPAIR = 2 * TOK
BLOCKS = NPAIR // CAP


def distance_bias(dist):
    dist = np.asarray(dist)
    c = np.zeros(dist.shape)
    for w, d in PATTERNS:
        c += (dist >= 0) & (dist <= w) & (dist % d == 0)
    return np.where(c > 0, -np.log(np.maximum(c, 1)), MASKED)


def shape_constants():
    slopes = 2.0 ** (-8.0 * np.arange(1, HA + 1) / HA)
    p, u = np.arange(P)[:, None], np.arange(SEQ)[None, :]
    dist = p + SEQ - P - u
    table = np.stack([distance_bias(dist) + s * np.maximum(dist, 0) for s in slopes])
    b, h, t = np.meshgrid(np.arange(4), np.arange(HA), np.arange(DT), indexing="ij")
    b, h, t = (x.reshape(P, 1) for x in (b, h, t))
    d_win = WB + t - np.array(ROWS)[None, :]
    win = distance_bias(d_win) + slopes[h] * d_win
    new = []
    for g in range(2):
        kb, kt = np.arange(SMP)[None, :] // DT, np.arange(SMP)[None, :] % DT
        dn = np.where(kb == 4 * g + b, t - kt, -1)
        new.append(distance_bias(dn) + slopes[h] * np.maximum(dn, 0))
    sample = np.concatenate([win] + new, axis=1)
    inv = np.zeros((P, 2, 17))
    for tile in range(2):
        for half in range(2):
            w = 2 ** (2 * tile + half + 1)
            inv[64 * half:64 * half + 64, tile, :16] = 1.0 / np.minimum(w, np.arange(16) + 1)
            inv[64 * half:64 * half + 64, tile, 16] = 1.0 / w
    tri = (np.arange(P)[:, None] < np.arange(P)[None, :]).astype(np.float32)
    iota = np.broadcast_to(np.arange(P), (P, P))
    small = np.concatenate([np.eye(P), tri, np.ones((P, P)), iota, inv.reshape(P, 34),
                            1.0 + np.arange(P)[:, None] + P * np.arange(CH)[None, :],
                            (np.arange(P)[:, None] + P * np.arange(CH)[None, :] < TOK)], axis=1)
    f = np.float32
    return {"c_table": table.astype(f), "c_sample": sample.astype(f), "c_small": small.astype(f)}


class Steps:

    def __init__(self, eng, sem):
        self.eng, self.sem, self.n = eng, sem, 0

    def __call__(self, ins):
        self.n += 1
        ins.then_inc(self.sem, 1)
        self.eng.wait_ge(self.sem, self.n)


def build(nc, I, O):
    ctx = ExitStack()
    with ctx:
        def sem(name):
            return ctx.enter_context(nc.semaphore(name))

        AR = ctx.enter_context(nc.sbuf_tensor("arena", [P, 51856], F32))
        PS = ctx.enter_context(nc.psum_tensor("psum", [P, 8 * 512], F32))
        CS = ctx.enter_context(nc.sbuf_tensor("consts", [P, 4 * P + 34 + 2 * CH], F32))
        ST = ctx.enter_context(nc.sbuf_tensor("stats", [P, 420], F32))
        h1_d = nc.dram_tensor("h1_d", [TOK, D], F32, kind="Internal").ap()
        pair_d = nc.dram_tensor("pair_d", [NPAIR, D], F32, kind="Internal").ap()

        def at(off, *dims):
            n = int(np.prod(dims))
            v = AR[:, off:off + n]
            if len(dims) == 2:
                v = v.rearrange("p (a b) -> p a b", a=dims[0])
            elif len(dims) == 3:
                v = v.rearrange("p (a b c) -> p a b c", a=dims[0], b=dims[1])
            elif len(dims) == 4:
                v = v.rearrange("p (a b c d) -> p a b c d", a=dims[0], b=dims[1], c=dims[2])
            return v

        def bank(n):
            return PS[:, 512 * n:512 * n + 512]

        ident, tri, ones, iota = (CS[:, P * n:P * n + P] for n in range(4))
        pool_inv = CS[:, 4 * P:4 * P + 34].rearrange("p (a b) -> p a b", a=2)
        tok1 = CS[:, 4 * P + 34:4 * P + 34 + CH]
        valid = CS[:, 4 * P + 34 + CH:4 * P + 34 + 2 * CH]

        QT, KTT, QC, UH = at(0, 4, TOK), at(4224, 4, TOK), at(8448, 2, TOK), 16
        V = at(10560, CH, D_A)
        KM, VM = at(15168, 2, N_MEM), at(15680, 2, D_C)
        UP = at(16192, 2, UH + SEQ)
        US = at(16192 + 2 * (UH + SEQ), 2, DB, PB + DT)
        USF = at(16192 + 2 * (UH + SEQ), 2 * DB, PB + DT)
        SS = at(16192, 2, 960)
        CAT = at(18576, KT, TOK)
        PA = AR[:, 18576 + 6 * TOK:18576 + 6 * TOK + 2 * (UH + SEQ)].rearrange("p (a b) -> p a b", a=2)
        PBUF = AR[:, 18576 + 2 * TOK:18576 + 2 * TOK + 2 * (UH + SEQ)].rearrange("p (a b) -> p a b", a=2)
        XT = at(27024, KT, TOK)
        WR = [at(35472 + 4096 * s, KT, 512) for s in range(3)]
        MT = at(47760, KT, N_MEM)
        RING = [27024, 27024 + 4096]
        SP = [at(35472 + 1024 * s, 1024) for s in range(4)]
        PTB = [at(39568 + 512 * s, 4, P) for s in range(4)]
        PTS = at(39568 + 2048, 2, 8, P)
        TB = [[at(43664 + 2048 * a + 1024 * b, 1024) for b in range(2)] for a in range(2)]
        QBD = at(47760, 2, 4, 4, 32)
        QBM = at(48784, 2, DB, 32)
        PMS, PTM = at(49296, N_MEM), at(49552, 2, P)
        SBIAS = at(49808, 960)
        OB = [at(50768 + P * s, P) for s in range(4)]
        KN = at(51280, 512)
        SA, SBF = at(41616, 2, DB, PB + DT), at(41616 + 304, 2, DB, PB + DT)
        WO = at(27024, KT, D)
        XR = [at(35472 + D * s, D) for s in range(2)]
        GB = at(37520, 2, D)
        H1 = at(0, CH, D)
        H1T = [at(9216 + D * s, KT, P) for s in range(2)]
        RB = [at(11264 + D * s, D) for s in range(2)]
        WRT = at(13312, KT, 36)
        LG = at(13600, CH, 36)
        SLOT = [39568, 45712, 18576, 24720]
        WG = [at(s, KT, DE) for s in SLOT]
        WU = [at(s + 2048, KT, DE) for s in SLOT]
        WD = [at(s + 4096, 2, D) for s in SLOT]
        XG = [at(30864 + D * s, D) for s in range(2)]
        XGT = [at(32912 + D * s, KT, P) for s in range(2)]
        SIL = [at(13312 + 2048 + 256 * s, 2, P) for s in range(2)]
        AT = [at(13312 + 2560 + 256 * s, 2, P) for s in range(2)]
        YS = [at(9216 + D * s, D) for s in range(2)]
        YP = [at(39568 + 2048 * s, 2, D) for s in range(3)]
        RF = [at(18576 + D * s, D) for s in range(3)]

        MN, DEN, RD = ST[:, 0:96], ST[:, 96:192], ST[:, 192:288]
        SMN, SDEN, SRD = ST[:, 288:291], ST[:, 291:294], ST[:, 294:297]
        BN = ST[:, 300:300 + 24].rearrange("p (c s) -> p c s", c=2)
        MV = ST[:, 330:330 + 4 * CH].rearrange("p (c s) -> p c s", c=CH)
        MV2 = ST[:, 370:370 + 4 * CH].rearrange("p (c s) -> p c s", c=CH)
        EPSC = ST[:, 297:298]
        PSC = ST[:, 298:300]
        WPL2 = ctx.enter_context(nc.sbuf_tensor("w_pool2", [P, 2, 64], F32))
        RT = ctx.enter_context(nc.sbuf_tensor("routing", [P, 72], F32))

        FLAG = at(35300, 1).bitcast(U32)
        CNT, NB = at(35301, NE), at(35333, NE)
        EB = at(35365, BLOCKS).bitcast(U32)
        OPOS, OVAL = at(15872 + 512, 2, CH), at(15872 + 530, 2, CH, 4)
        OLF, OLI = at(16500, 4), at(16504, 2).bitcast(U32)
        OPRE = [at(16510, NE), at(16542, NE)]
        OTMP = at(39568 + 6144, BLOCKS, NE)

        s_const, s_bias = sem("s_const"), sem("s_bias")
        s_xk = [sem(f"s_xk{k}") for k in range(KT)]
        s_w = [sem(f"s_w{g}") for g in range(5)]
        s_mem, s_state = sem("s_mem"), sem("s_state")
        s_proj = sem("s_proj")
        s_pe_d, s_pe_a = sem("s_pe_d"), sem("s_pe_a")
        s_copy = [sem(f"s_copy{i}") for i in range(2)]
        s_store = sem("s_store")
        s_halo, s_pool = sem("s_halo"), sem("s_pool")
        s_tb = [sem(f"s_tb{i}") for i in range(2)]
        s_ring = [sem(f"s_ring{i}") for i in range(2)]
        s_S, s_min, s_exp = sem("s_S"), sem("s_min"), sem("s_exp")
        s_T, s_Td, s_Ta, s_PV, s_O, s_OB = sem("s_T"), sem("s_Td"), sem("s_Ta"), sem("s_PV"), sem("s_O"), sem("s_OB")
        s_xp, s_xe, s_sexp, s_smin, s_srd = sem("s_xp"), sem("s_xe"), sem("s_sexp"), sem("s_smin"), sem("s_srd")
        s_dve, s_pl, s_ac = sem("s_dve"), sem("s_pl"), sem("s_ac")
        s_wo, s_gb, s_mix, s_r = sem("s_wo"), sem("s_gb"), sem("s_mix"), sem("s_r")
        s_x = [sem(f"s_x{i}") for i in range(2)]
        s_std, s_nrm, s_z, s_h1 = sem("s_std"), sem("s_nrm"), sem("s_z"), sem("s_h1")
        s_ht, s_hte, s_rt = sem("s_ht"), sem("s_hte"), sem("s_rt")
        s_h1d = sem("s_h1d")
        s_M, s_rank, s_oh, s_ohx, s_idx = sem("s_M"), sem("s_rank"), sem("s_oh"), sem("s_ohx"), sem("s_idx")
        s_rx, s_ra, s_ahh = sem("s_rx"), sem("s_ra"), sem("s_ahh")
        s_g = [sem(f"s_g{i}") for i in range(4)]
        s_wd = [sem(f"s_wd{i}") for i in range(4)]
        s_gx = [sem(f"s_gx{i}") for i in range(2)]
        s_col, s_past = sem("s_col"), sem("s_past")
        s_tp, s_xgt, s_gu, s_sil, s_at, s_y, s_ya, s_yd = (sem(n) for n in
                                                      ("s_tp", "s_xgt", "s_gu", "s_sil", "s_at", "s_y", "s_ya", "s_yd"))
        s_ys = [sem(f"s_ys{i}") for i in range(2)]
        s_gb2, s_ah = sem("s_gb2"), sem("s_ah")
        s_yp = [sem(f"s_yp{i}") for i in range(3)]
        s_f, s_f1, s_fz, s_fo, s_std2, s_nr2 = (sem(n) for n in ("s_f", "s_f1", "s_fz", "s_fo", "s_std2", "s_nr2"))
        s_out = [sem(f"s_out{i}") for i in range(3)]

        o_pos, o_eb, o_oh, o_ohx, o_idx, o_col = (sem(n) for n in ("o_pos", "o_eb", "o_oh", "o_ohx", "o_idx", "o_col"))
        o_free = sem("o_free")
        o_w, o_g, o_s = sem("o_w"), sem("o_g"), sem("o_s")
        o_tp, o_xgt, o_gu, o_sil, o_at, o_y, o_ya, o_yd = (sem(n) for n in
                                                           ("o_tp", "o_xgt", "o_gu", "o_sil", "o_at", "o_y", "o_ya", "o_yd"))

        block = ctx.enter_context(nc.Block())

        def overflow(eng):
            eng.wait_ge(s_idx, 1)
            return eng.If(eng.value_load(FLAG[0:1, 0:1], min_val=0, max_val=1) > 0)

        def rows(c):
            return P if c < CH - 1 else SMP

        W_G = {"q": 0, "k": 1, "v": 2, "u": 3, "m": 4}
        W_SLOT = [0, 1, 2, 0, 1]
        proj = []

        def proj_tile(dest3, wgrp, col):
            w = WR[W_SLOT[W_G[wgrp]]]
            return [(d, lambda k, c=col, w=w: w[:, k, c:c + P], lambda k, a=a, n=n: XT[:, k, a:a + n], W_G[wgrp], s, P, n)
                    for d, a, n, s in dest3]

        for m in range(4):
            proj += proj_tile([(QT[:, m, 0:512], 0, 512, QS), (QT[:, m, 512:1024], 512, 512, QS)], "q", m * P)
        for m in range(4):
            proj += proj_tile([(QT[:, m, SEQ:TOK], SEQ, SMP, QS)], "q", m * P)
        for m in range(4):
            proj += proj_tile([(KTT[:, m, a:a + n], a, n, 1.0) for a, n in ((0, 512), (512, 512), (SEQ, SMP))], "k", m * P)
        for c in range(CH):
            proj.append((V[0:rows(c), c, :], lambda k, c=c: XT[:, k, c * P:c * P + rows(c)],
                         lambda k: WR[2][:, k, :], W_G["v"], 1.0, rows(c), 512))
        for m in range(2):
            proj += proj_tile([(UP[:, m, UH:UH + 512], 0, 512, 1.0), (UP[:, m, UH + 512:UH + SEQ], 512, 512, 1.0),
                               (US[:, m, :, PB:PB + DT], SEQ, SMP, 1.0)], "u", m * P)
        for m in range(2):
            proj += proj_tile([(QC[:, m, a:a + n], a, n, QS) for a, n in ((0, 512), (512, 512), (SEQ, SMP))], "u", D_B + m * P)
        n_x = len(proj)
        for m in range(2):
            proj.append((KM[:, m, :], lambda k, m=m: WR[1][:, k, m * P:m * P + P], lambda k: MT[:, k, :], W_G["m"], 1.0, P, N_MEM))
        for m in range(2):
            proj.append((VM[:, m, :], lambda k, m=m: MT[:, k, m * P:m * P + P], lambda k: WR[1][:, k, 256:512], W_G["m"], 1.0, P, N_MEM))
        NPROJ = len(proj)
        last_of = {g: max(n for n, t in enumerate(proj) if t[3] == g) for g in range(5)}

        def proj_done(eng, n):
            eng.wait_ge(s_pe_d, n // 2 + 1)
            if n >= 1:
                eng.wait_ge(s_pe_a, (n + 1) // 2)

        units = [("w", hp, i) for hp in range(4) for i in range(8)] + [("c", hp, i) for hp in range(2) for i in range(8)]
        NU = len(units)
        items = []
        unit_items = []
        for u, (kind, hp, i) in enumerate(units):
            nb = i + 1 if kind == "w" else 2
            mine = []
            for s in range(2):
                for b0 in range(0, nb, 4):
                    mine.append(("T", u, s, list(range(b0, min(b0 + 4, nb))), nb))
            if u:
                mine.insert(1, ("OT", u - 1))
            if u == NU - 1:
                mine.append(("OT", u))
            unit_items.append(list(range(len(items), len(items) + len(mine))))
            items += mine
        NI = len(items)
        last_T = {}
        ot_at = {}
        pv_upto = []
        n_pv = 0
        for n, it in enumerate(items):
            if it[0] == "T":
                last_T[(it[1], it[2])] = n
                n_pv += 1
            else:
                ot_at[it[1]] = n
            pv_upto.append(n_pv)

        def item_done(eng, n):
            if n % 2 == 0:
                eng.wait_ge(s_Td, n // 2 + 1)
            else:
                eng.wait_ge(s_Ta, n // 2 + 1)

        extra = {u: [] for u in range(-1, NU)}
        extra[-1] = [("knew",)]
        for j in range(5):
            extra[j] = extra.get(j, []) + [("pool", j)]
        for s in range(8):
            extra[6 + 2 * s].append(("ss", s))
        extra[13].append(("st", 0, 0)); extra[13].append(("st", 0, 1))
        extra[21].append(("st", 1, 0)); extra[21].append(("st", 1, 1))
        for b in range(8):
            extra[22 + 2 * b].append(("pv", b))
        extra[38].append(("ms",))
        extra[39].append(("mt",))
        extra[40].append(("mpv",))
        xlist = [e for u in range(-1, NU) for e in extra[u]]
        xnum = {e: n for n, e in enumerate(xlist)}
        x_before = [sum(len(extra[w]) for w in range(-1, u)) for u in range(NU)]
        ring_user = [("ss", s) for s in range(8)] + [("pv", b) for b in range(8)] + [("ms",), ("mpv",)]
        ring_no = {e: n for n, e in enumerate(ring_user)}

        def ring_ready(eng, e):
            n = ring_no[e]
            eng.wait_ge(s_ring[n % 2], 16 * sum(4 if f[0] == "pv" else 1 for f in ring_user[n % 2:n + 1:2]))

        def load_table(sp, hp):
            if hp >= 2:
                sp.wait_ge(s_min, 2 * 8 * (hp - 1))
            elif hp == 0:
                proj_done(sp, last_of[2])
            for s in range(2):
                sp.dma_start(TB[hp % 2][s], I["c_table"][2 * hp + s]).then_inc(s_tb[hp % 2], 16)

        def ring_load(n, e):
            off = RING[n % 2]
            if e[0] == "ss":
                return [at(off, 4, 4 * KC)], [I["winkT"][e[1]].rearrange("p a n -> p a n")]
            if e[0] == "pv":
                v = I["cache_win_v"][e[1]]
                dst = at(off, NVT, 512)
                far = v[0:WB - 512, :].rearrange("(j r) n -> j (r n)", r=16)[:, 0:DT * 512]
                return ([dst[:, t, :] for t in range(3)] + [dst[:, 3:7, :]],
                        [far[32 * t:32 * t + 32, :].rearrange("j (r n) -> j r n", r=DT) for t in range(3)]
                        + [v[WB - 512:WB, :].rearrange("(t p) n -> p t n", p=P)])
            if e[0] == "ms":
                return [at(off, 2, DB * N_MEM)], [I["memkT"]]
            return [at(off, DB * 2, D_C)], [I["cache_mem_v"].rearrange("b (t p) n -> p (b t) n", p=P)]

        def load_gu(sp, e, j):
            for w, d in (("w_gate", WG), ("w_up", WU)):
                src = I[w][bass.ds(e, 1)].rearrange("o (k p) n -> p (o k) n", p=P)
                sp.dma_start(d[j], src).then_inc(s_g[j], 16)

        def load_dn(sp, e, j):
            src = I["w_down"][bass.ds(e, 1)].rearrange("o (k p) n -> p (o k) n", p=P)
            sp.dma_start(WD[j], src).then_inc(s_wd[j], 16)

        def load_expert(sp, e, j):
            load_gu(sp, e, j)
            load_dn(sp, e, j)

        R0 = 13600 + 324
        RM, RMP = at(R0, CH, NE), at(R0 + 288, CH, NE)
        RE = [at(R0 + 576, CH, NE), at(R0 + 864, CH, NE)]
        RL = at(R0 + 1152, CH, NE)
        RANK = at(17800, CH, NE)
        RX = at(R0 + 1440, CH, NE)
        RV = AR[:, 30864:30864 + 2 * CH * 96].rearrange("p (k c n) -> p k c n", k=2, c=CH)
        OH = [at(32912 + P * s, P) for s in range(4)]
        IDX = at(34960, 3 * NE).bitcast(U32)
        IDF = at(35056, 3 * NE)

        def transposed_out(eng, copy, n):
            it = items[n]
            b = bank(4 + n % 2)
            if it[0] == "T":
                if n >= 4:
                    eng.wait_ge(s_PV, pv_upto[n - 4])
                w = len(it[3])
                return copy(PTB[n % 4][:, 0:w, :].rearrange("p a b -> p (a b)"), b[:, 0:w * P])
            kind, hp, i = units[it[1]]
            if kind == "c" or hp >= 2:
                eng.wait_ge(s_xp, xnum[("pool", 4)] + 1)
            return copy(CAT[:, hp + (0 if kind == "w" else 6), i * P:i * P + P], b[:, 0:P])

        GI = [at(35296 + n, 1).bitcast(U32) for n in range(2)]
        SI = [at(35298 + n, 1).bitcast(U32) for n in range(2)]
        G1W = at(35152, 12 * CH)
        RX1 = at(35260, CH * 4)
        W2 = G1W[:, 0:CH]
        GS = IDF[:, 2 * NE:3 * NE]

        @block.sync
        def _(sp):
            xv = I["xT"].rearrange("(k p) n -> p k n", p=P)
            wv = I["w_in"].rearrange("(k p) n -> p k n", p=P)
            for k in range(KT):
                sp.dma_start(XT[:, k, :], xv[:, k, :]).then_inc(s_xk[k], 16)
                sp.dma_start(WR[0][:, k, :], wv[:, k, 0:512]).then_inc(s_xk[k], 16)
                if k == 1:
                    sp.dma_start(CS[:, :], I["c_small"]).then_inc(s_const, 16)
            sp.dma_start(WR[1], wv[:, :, 512:1024]).then_inc(s_w[1], 16)
            sp.dma_start(WR[2], wv[:, :, 1024:1536]).then_inc(s_w[2], 16)
            sp.dma_start(MT, I["memT"].rearrange("(k p) n -> p k n", p=P)).then_inc(s_mem, 16)
            sp.dma_start(SBIAS, I["c_sample"]).then_inc(s_bias, 16)
            sp.dma_start(USF[:, :, 0:PB], I["stateT"]).then_inc(s_state, 16)
            sp.dma_start(WPL2[:, :, :], I["w_pool"].rearrange("(m h) c e -> (h c) m e", h=2)).then_inc(s_state, 16)
            sp.dma_start(PSC, I["pool_scale"]).then_inc(s_state, 16)
            copies = [(t, b, r) for t in "kv" for b in range(DB) for r in range(2)]
            half = (WB - DT) // 2
            for n, (t, b, r) in enumerate(copies):
                if n == 5:
                    proj_done(sp, last_of[0])
                    sp.dma_start(WR[0], wv[:, :, 1536:2048]).then_inc(s_w[3], 16)
                if n == 14:
                    proj_done(sp, last_of[1])
                    sp.dma_start(WR[1], I["w_mem_kv"].rearrange("(k p) n -> p k n", p=P)).then_inc(s_w[4], 16)
                if n >= 2:
                    sp.wait_ge(s_copy[n % 2], 16 * (n // 2))
                sp.dma_start(O["win_" + t + "_s"][b, r * half:(r + 1) * half, :],
                             I["cache_win_" + t][b, DT + r * half:DT + (r + 1) * half, :]).then_inc(s_copy[n % 2], 16)
                if n == 26:
                    load_table(sp, 0)
            load_table(sp, 1)
            for n, e in enumerate(ring_user):
                if n == 0:
                    proj_done(sp, n_x - 1)
                if n >= 2:
                    sp.wait_ge(s_xp, xnum[ring_user[n - 2]] + 1)
                dst, srcs = ring_load(n, e)
                for d, s in zip(dst, srcs):
                    sp.dma_start(d, s).then_inc(s_ring[n % 2], 16)
                if n == 1:
                    proj_done(sp, NPROJ - 1)
                    sp.dma_start(O["kT"].rearrange("(m p) n -> p m n", p=P), KTT[:, :, 0:SEQ]).then_inc(s_store, 16)
                    sp.dma_start(O["v"].rearrange("(c p) n -> p c n", p=P), V[:, 0:CH - 1, :]).then_inc(s_store, 16)
                    sp.dma_start(O["kmT"].rearrange("(m p) n -> p m n", p=P), KM).then_inc(s_store, 16)
                    sp.dma_start(O["vm"].rearrange("(m p) n -> p m n", p=P), VM).then_inc(s_store, 16)
                    sp.dma_start(O["uT"].rearrange("(m p) n -> p m n", p=P), UP[:, :, UH + SEQ - PB:UH + SEQ]).then_inc(s_store, 16)
                    sp.wait_ge(s_state, 48)
                    sp.dma_start(O["poolT_s"], USF[:, :, DT:DT + PB]).then_inc(s_store, 16)
                    for b in range(DB):
                        sp.dma_start(O["win_v_s"][b, WB - DT:WB, :], V[DT * b:DT * b + DT, CH - 1, :]).then_inc(s_store, 16)
                    sp.wait_ge(s_xe, xnum[("knew",)] + 1)
                    for b in range(DB):
                        sp.dma_start(O["win_k_s"][b, WB - DT:WB, :], KN[DT * b:DT * b + DT, :]).then_inc(s_store, 16)
                if n == 4:
                    load_table(sp, 2)
                if n == 9:
                    load_table(sp, 3)
            sp.wait_ge(s_xp, len(xlist))
            wo = I["w_o"].rearrange("(k p) n -> p k n", p=P)
            sp.dma_start(WO[:, :, 0:512], wo[:, :, 0:512]).then_inc(s_wo, 16)
            sp.dma_start(WO[:, :, 512:1024], wo[:, :, 512:1024]).then_inc(s_wo, 16)
            item_done(sp, NI - 1)
            item_done(sp, NI - 2)
            sp.wait_ge(s_OB, 2 * NU)
            sp.wait_ge(s_store, 16 * (6 + 2 * DB))
            for v, n in (("ln1_g", 0), ("ln1_b", 1)):
                sp.dma_start(GB[:, n, :], I[v].unsqueeze(0).broadcast_to([P, D])).then_inc(s_gb, 16)
            sp.dma_start(WRT, I["w_r"].rearrange("(k p) e -> p k e", p=P)).then_inc(s_gb, 16)
            sp.dma_start(RT[:, 0:36], I["b_r"].unsqueeze(0).broadcast_to([P, 36])).then_inc(s_gb, 16)

            def store_h1(c):
                sp.wait_ge(s_h1, c + 1)
                sp.dma_start(h1_d[c * P:c * P + rows(c), :], H1[0:rows(c), c, :]).then_inc(s_h1d, 16)

            for c in range(CH):
                if c >= 2:
                    sp.wait_ge(s_r, c - 1)
                sp.dma_start(XR[c % 2][0:rows(c), :], I["x"][c * P:c * P + rows(c), :]).then_inc(s_x[c % 2], 16)
                if c == 3:
                    load_expert(sp, 0, 0)
                if c == 5:
                    load_expert(sp, 1, 1)
                if c >= 3:
                    store_h1(c - 3)
            for c in range(CH - 3, CH):
                store_h1(c)
            sp.wait_ge(s_mix, CH)
            load_expert(sp, 2, 2)
            load_expert(sp, 3, 3)
            with sp.Fori(1, NE // 4) as i:
                for j in range(4):
                    sp.wait_ge(s_gu, i * 4 + (j - 3))
                    load_gu(sp, i * 4 + j, j)
                    sp.wait_ge(s_y, i * 4 + (j - 3))
                    load_dn(sp, i * 4 + j, j)
            with overflow(sp):
                sp.wait_ge(s_y, NE)
                sp.wait_ge(o_eb, 1)
                with sp.Fori(0, BLOCKS) as b:
                    e = sp.value_load(EB[0:1, bass.ds(b, 1)], min_val=0, max_val=NE - 1)
                    sp.wait_ge(o_free, b + 1)
                    for w, d in (("w_gate", WG), ("w_up", WU), ("w_down", WD)):
                        sp.dma_start(d[0], I[w][bass.ds(e, 1)].rearrange("o (k p) n -> p (o k) n", p=P)).then_inc(o_w, 16)
                sp.wait_ge(o_s, 16 * BLOCKS)
            with sp.Else():
                sp.nop()
            for v, n in (("ln2_g", 0), ("ln2_b", 1)):
                sp.dma_start(GB[:, n, :], I[v].unsqueeze(0).broadcast_to([P, D])).then_inc(s_gb2, 16)
            sp.wait_ge(s_ys[0], 16 * (NE // 2))
            sp.wait_ge(s_ys[1], 16 * (NE // 2))
            pr = pair_d.rearrange("(k n) d -> n k d", k=2)

            def store_y(c):
                sp.wait_ge(s_fo, c + 1)
                sp.dma_start(O["y"][c * P:c * P + rows(c), :], RF[c % 3][0:rows(c), :]).then_inc(s_out[c % 3], 16)

            for c in range(CH):
                if c == 0:
                    sp.wait_ge(s_y, NE)
                if c >= 3:
                    sp.wait_ge(s_f, c - 2)
                sp.dma_start(YP[c % 3][0:rows(c), :, :], pr[c * P:c * P + rows(c), :, :]).then_inc(s_yp[c % 3], 16)
                if c >= 3:
                    store_y(c - 3)
            for c in range(CH - 3, CH):
                store_y(c)
            for i in range(3):
                sp.wait_ge(s_out[i], 16 * (CH // 3))
            for i in range(2):
                sp.wait_ge(s_copy[i], 16 * DB * 2)

        @block.tensor
        def _(pe):
            def mm(out, lhsT, rhs, start, stop):
                return nc.tensor.matmul(out, lhsT, rhs, start=start, stop=stop, skip_group_check=True)

            for k in range(KT):
                pe.wait_ge(s_xk[k], 32)
                for n in range(8):
                    _, lt, rh, _, _, m, w = proj[n]
                    last = mm(bank(n)[0:m, 0:w], lt(k), rh(k), k == 0, k == KT - 1)
                    if k == KT - 1:
                        last.then_inc(s_proj, 1)
            for n in range(8, NPROJ):
                _, lt, rh, g, _, m, w = proj[n]
                if g:
                    pe.wait_ge(s_w[g], 16)
                if g == 4:
                    pe.wait_ge(s_mem, 16)
                proj_done(pe, n - 8)
                for k in range(KT):
                    last = mm(bank(n % 8)[0:m, 0:w], lt(k), rh(k), k == 0, k == KT - 1)
                last.then_inc(s_proj, 1)
            proj_done(pe, NPROJ - 1)
            pe.wait_ge(s_const, 16)

            def scores(u):
                kind, hp, i = units[u]
                for s in range(2):
                    if u:
                        pu = units[u - 1]
                        if pu[0] == "w":
                            pe.wait_ge(s_min, 2 * (u - 1) + s + 1)
                        else:
                            pe.wait_ge(s_exp, 2 * (u - 1) + s + 1)
                for s in range(2):
                    h = slice(64 * s, 64 * s + 64)
                    q = (QT if kind == "w" else QC)[h, hp, i * P:i * P + P]
                    width = P * (i + 1) if kind == "w" else N_MEM
                    for a in range(0, width, 512):
                        w = min(512, width - a)
                        k = (KTT if kind == "w" else KM)[h, hp, a:a + w]
                        last = mm(PS[:, 1024 * s + a:1024 * s + a + w], q, k, True, True)
                    last.then_inc(s_S, 1)

            def transposes(n):
                it = items[n]
                if n >= 2:
                    item_done(pe, n - 2)
                b = bank(4 + n % 2)
                if it[0] == "T":
                    _, u, s, blocks, _ = it
                    pe.wait_ge(s_exp, 2 * u + s + 1)
                    for j, kb in enumerate(blocks):
                        last = nc.tensor.transpose(b[:, j * P:j * P + P], SP[(u % 2) * 2 + s][:, kb * P:kb * P + P], ident)
                else:
                    pe.wait_ge(s_OB, 2 * it[1] + 2)
                    last = nc.tensor.transpose(b[:, 0:P], OB[it[1] % 4], ident)
                last.then_inc(s_T, 1)

            def values(n):
                it = items[n]
                if it[0] == "OT":
                    return
                _, u, s, blocks, nb = it
                kind, hp, i = units[u]
                item_done(pe, n)
                if blocks[0] == 0 and u:
                    pe.wait_ge(s_OB, 2 * (u - 1) + s + 1)
                if blocks[0] == 0 and s == 0:
                    pe.wait_ge(s_xe, x_before[u])
                o = bank(6 + s)[:, 0:HD]
                for j, kb in enumerate(blocks):
                    c = (2 * hp + s) * HD
                    v = (V if kind == "w" else VM)[:, kb, c:c + HD]
                    last = mm(o, PTB[n % 4][:, j, :], v, kb == 0, kb == nb - 1)
                last.then_inc(s_PV, 1)

            def x_step(e, u):
                x = xnum[e]
                if x:
                    pe.wait_ge(s_xe, x)
                if u >= 0:
                    pe.wait_ge(s_OB, 2 * u + 1)
                bx = bank(6)
                if e[0] == "knew":
                    for m in range(4):
                        last = nc.tensor.transpose(bx[0:SMP, m * P:m * P + P], KTT[:, m, SEQ:TOK], ident)
                elif e[0] == "pool":
                    pe.wait_ge(s_pool, 1 if e[1] < 4 else 2)
                    if e[1] < 4:
                        t, hf = e[1] // 2, e[1] % 2
                        for g in range(2):
                            r = slice(64 * g, 64 * g + 64)
                            last = mm(bx[r, 0:512], WPL2[r, t, :], PA[r, t, UH + 512 * hf:UH + 512 * hf + 512], True, True)
                    else:
                        for t in range(2):
                            for g in range(2):
                                r = slice(64 * g, 64 * g + 64)
                                last = mm(bx[r, t * SMP:t * SMP + SMP], WPL2[r, t, :], SA[r, t, :, PB:PB + DT], True, True)
                elif e[0] == "ss":
                    g, kc = e[1] // 4, e[1] % 4
                    ring_ready(pe, e)
                    if e[1] == 0:
                        pe.wait_ge(s_srd, 1)
                    kt = at(RING[ring_no[e] % 2], 4, 4, KC)
                    for hp in range(4):
                        for b in range(4):
                            last = mm(bx[32 * b:32 * b + 32, 0:KC], QBD[:, g, hp, b, :], kt[:, hp, b, :], hp == 0, hp == 3)
                    if kc == 3:
                        for hp in range(4):
                            for b in range(4):
                                last = mm(bx[32 * b:32 * b + 32, KC:KC + SMP], QBD[:, g, hp, b, :], KTT[:, hp, SEQ:TOK], hp == 0, hp == 3)
                elif e[0] == "st":
                    _, g, hf = e
                    pe.wait_ge(s_srd, 2 + g)
                    for j in range(4):
                        t = 4 * hf + j
                        m = P if t < NVT else SMP
                        last = nc.tensor.transpose(bx[0:m, j * P:j * P + P], SS[:, g, t * P:t * P + m], ident)
                elif e[0] == "pv":
                    b = e[1]
                    g = b // 4
                    ring_ready(pe, e)
                    vt = at(RING[ring_no[e] % 2], NVT, 512)
                    for hp in range(4):
                        o = bx[:, 8 * hp:8 * hp + 8]
                        pc = 32 * (b % 4) + 8 * hp
                        for t in range(NVT):
                            mm(o, vt[:, t, hp * P:hp * P + P], PTS[:, g, t, pc:pc + 8], t == 0, False)
                        last = mm(o, V[0:SMP, CH - 1, hp * P:hp * P + P], PTS[0:SMP, g, NVT, pc:pc + 8], False, True)
                elif e[0] == "ms":
                    ring_ready(pe, e)
                    km = at(RING[ring_no[e] % 2], 2, DB, N_MEM)
                    for j in range(4):
                        for n in range(4):
                            hp, b = n // 2, 2 * j + n % 2
                            last = mm(bx[32 * j:32 * j + 32, 0:N_MEM], QBM[:, hp, b, :], km[:, hp, b, :], n == 0, n == 3)
                elif e[0] == "mt":
                    pe.wait_ge(s_srd, 4)
                    for t in range(2):
                        last = nc.tensor.transpose(bx[:, t * P:t * P + P], PMS[:, t * P:t * P + P], ident)
                else:
                    ring_ready(pe, e)
                    vm = at(RING[ring_no[e] % 2], DB, 2, D_C)
                    for b in range(DB):
                        for hp in range(2):
                            for t in range(2):
                                c = (2 * b + hp) * 8
                                last = mm(bx[:, c:c + 8], vm[:, b, t, hp * P:hp * P + P], PTM[:, t, 16 * b + 8 * hp:16 * b + 8 * hp + 8], t == 0, t == 1)
                last.then_inc(s_xp, 1)

            for e in extra[-1]:
                x_step(e, -1)
            scores(0)
            for u in range(NU):
                if u + 1 < NU:
                    scores(u + 1)
                for n in unit_items[u]:
                    if n == NI - 1:
                        values(n - 1)
                    transposes(n)
                    if 0 < n < NI - 1:
                        values(n - 1)
                for e in extra[u]:
                    x_step(e, u)
            item_done(pe, NI - 1)
            item_done(pe, NI - 2)
            pe.wait_ge(s_xe, len(xlist))
            pe.wait_ge(s_wo, 32)
            pe.wait_ge(s_exp, 2 * NU)

            def mix(c):
                if c >= 2:
                    pe.wait_ge(s_r, c - 1)
                m = rows(c)
                for n in range(2):
                    for k in range(KT):
                        last = mm(PS[0:m, 1024 * (c % 2) + 512 * n:1024 * (c % 2) + 512 * n + 512],
                                  CAT[:, k, c * P:c * P + m], WO[:, k, 512 * n:512 * n + 512], k == 0, k == KT - 1)
                last.then_inc(s_mix, 1)

            def h1_transposes(c):
                pe.wait_ge(s_h1, c + 1)
                m = rows(c)
                for hf in range(2):
                    if c >= 1:
                        pe.wait_ge(s_hte, 2 * (c - 1) + hf + 1)
                    for j in range(4):
                        k = 4 * hf + j
                        last = nc.tensor.transpose(bank(4 + hf)[:, j * P:j * P + m], H1[0:m, c, k * P:k * P + P], ident[0:m, 0:m])
                    last.then_inc(s_ht, 1)

            def router(c):
                m = rows(c)
                if c == 0:
                    pe.wait_ge(s_gb, 64)
                pe.wait_ge(s_hte, 2 * c + 2)
                for k in range(KT):
                    last = mm(bank(6)[0:m, 36 * c:36 * c + 36], H1T[c % 2][:, k, 0:m], WRT[:, k, :], k == 0, k == KT - 1)
                last.then_inc(s_rt, 1)

            for c in range(CH):
                mix(c)
                if c >= 1:
                    h1_transposes(c - 1)
                if c >= 2:
                    router(c - 2)
            h1_transposes(CH - 1)
            router(CH - 2)
            router(CH - 1)
            pe.wait_ge(s_M, 1)
            mm(bank(0)[:, 0:CH * NE], tri, RM.rearrange("p c e -> p (c e)"), True, False)
            mm(bank(0)[:, 0:CH * NE], ones, RMP.rearrange("p c e -> p (c e)"), False, True)
            mm(bank(0)[:, CH * NE:CH * NE + NE], ones, CNT, True, True).then_inc(s_rank, 1)
            for n in range(2 * CH):
                c, k = n // 2, n % 2
                pe.wait_ge(s_oh, n + 1)
                last = mm(bank(1)[:, 0:3 * NE], OH[n % 4], RV[:, k, c, :], n == 0, n == 2 * CH - 1)
                last.then_inc(s_ohx, 1)
            def gather_transposes(e, sl):
                for hf in range(2):
                    for j in range(4):
                        k = 4 * hf + j
                        last = nc.tensor.transpose(bank(hf)[:, j * P:j * P + P], XG[sl][:, k * P:k * P + P], ident)
                    last.then_inc(s_tp, 1)

            def gate_up(j):
                b = bank(2 + j % 2)
                for n in range(4):
                    w = (WG, WU)[n // 2][j]
                    for k in range(KT):
                        last = mm(b[:, n * P:n * P + P], w[:, k, (n % 2) * P:(n % 2) * P + P], XGT[j % 2][:, k, :], k == 0, k == KT - 1)
                last.then_inc(s_gu, 1)

            def down(j):
                for n in range(2):
                    for f in range(2):
                        last = mm(PS[:, 2048 + 1024 * (j % 2) + 512 * n:2048 + 1024 * (j % 2) + 512 * n + 512],
                                  AT[j % 2][:, f, :], WD[j][:, f, 512 * n:512 * n + 512], f == 0, f == 1)
                last.then_inc(s_y, 1)

            pe.wait_ge(s_idx, 1)
            pe.wait_ge(s_gx[0], 16)
            gather_transposes(0, 0)

            def expert(i, j, first, last):
                e = i * 4 + j
                pe.wait_ge(s_g[j], i * 32 + 32)
                pe.wait_ge(s_xgt, e * 2 + 2)
                if not first:
                    pe.wait_ge(s_at, e - 1)
                gate_up(j)
                if not last:
                    pe.wait_ge(s_gx[(j + 1) % 2], (e + 1 - (j + 1) % 2) * 8 + 16)
                    gather_transposes(e + 1, (j + 1) % 2)
                pe.wait_ge(s_at, e + 1)
                pe.wait_ge(s_wd[j], i * 16 + 16)
                if not first:
                    pe.wait_ge(s_ya, e - 1)
                    pe.wait_ge(s_yd, e - 1)
                down(j)

            for j in range(4):
                expert(0, j, j < 2, False)
            with pe.Fori(1, NE // 4 - 1) as i:
                for j in range(4):
                    expert(i, j, False, False)
            for j in range(4):
                expert(NE // 4 - 1, j, False, j == 3)
            with overflow(pe):
                pe.wait_ge(s_yd, NE)
                pe.wait_ge(s_ya, NE)
                with pe.Fori(0, BLOCKS) as b:
                    for n in range(2 * CH):
                        pe.wait_ge(o_oh, b * 2 * CH + (n + 1))
                        mm(bank(1)[:, 0:4], OH[n % 4], OVAL[:, n % 2, n // 2, :], n == 0, n == 2 * CH - 1).then_inc(o_ohx, 1)
                    pe.wait_ge(o_g, b * 16 + 16)
                    for hf in range(2):
                        for j in range(4):
                            k = 4 * hf + j
                            last = nc.tensor.transpose(bank(hf)[:, j * P:j * P + P], XG[0][:, k * P:k * P + P], ident)
                        last.then_inc(o_tp, 1)
                    pe.wait_ge(o_w, b * 48 + 48)
                    pe.wait_ge(o_xgt, b * 2 + 2)
                    for n in range(4):
                        w = (WG, WU)[n // 2][0]
                        for k in range(KT):
                            last = mm(bank(2)[:, n * P:n * P + P], w[:, k, (n % 2) * P:(n % 2) * P + P], XGT[0][:, k, :], k == 0, k == KT - 1)
                    last.then_inc(o_gu, 1)
                    pe.wait_ge(o_at, b + 1)
                    for n in range(2):
                        for f in range(2):
                            last = mm(bank(4 + n), AT[0][:, f, :], WD[0][:, f, 512 * n:512 * n + 512], f == 0, f == 1)
                    last.then_inc(o_y, 1)
            with pe.Else():
                pe.nop()

        @block.scalar
        def _(act):
            for n in range(1, NPROJ, 2):
                d, _, _, _, scale, m, w = proj[n]
                act.wait_ge(s_proj, n + 1)
                src = bank(n % 8)[0:m, 0:w]
                if len(d.shape) == 3:
                    src = src.rearrange("p (b t) -> p b t", t=DT)
                nc.scalar.activation(d, src, ACT.Copy, scale=scale).then_inc(s_pe_a, 1)

            def evac(n):
                it = items[n]
                if n % 2 == 0:
                    return
                act.wait_ge(s_T, n + 1)
                transposed_out(act, nc.scalar.copy, n).then_inc(s_Ta, 1)

            def exps(u, s):
                kind, hp, i = units[u]
                w = P * (i + 1) if kind == "w" else N_MEM
                x = 2 * u + s
                act.wait_ge(s_min, x + 1)
                sp = SP[(u % 2) * 2 + s]
                if kind == "c" and u >= 2:
                    act.wait_ge(s_T, last_T[(u - 2, s)] + 1)
                src = sp[:, 0:w] if kind == "w" else PS[:, 1024 * s:1024 * s + w]
                nc.scalar.activation(sp[:, 0:w], src, ACT.Exp, scale=-1.0, bias=MN[:, x:x + 1],
                                     accum_out=DEN[:, x:x + 1]).then_inc(s_exp, 1)

            def x_act(e):
                if e in (("ss", 3), ("ss", 7)):
                    g = e[1] // 4
                    act.wait_ge(s_smin, g + 1)
                    nc.scalar.activation(SS[:, g, 0:NK + SMP], SS[:, g, 0:NK + SMP], ACT.Exp, scale=-1.0,
                                         bias=SMN[:, g:g + 1], accum_out=SDEN[:, g:g + 1]).then_inc(s_sexp, 1)
                if e == ("ms",):
                    act.wait_ge(s_smin, 3)
                    nc.scalar.activation(PMS, bank(6)[:, 0:N_MEM], ACT.Exp, scale=-1.0,
                                         bias=SMN[:, 2:3], accum_out=SDEN[:, 2:3]).then_inc(s_sexp, 1)

            exps(0, 0)
            exps(0, 1)
            for u in range(NU):
                mine = unit_items[u]
                for j, n in enumerate(mine):
                    evac(n)
                    if u + 1 < NU and j == min(1, len(mine) - 1):
                        exps(u + 1, 0)
                    if u + 1 < NU and j == min(3, len(mine) - 1):
                        exps(u + 1, 1)
                for e in extra[u]:
                    x_act(e)
            def h1t_copy(c):
                m = rows(c)
                for hf in range(2):
                    act.wait_ge(s_ht, 2 * c + hf + 1)
                    if c >= 2:
                        act.wait_ge(s_rt, c - 1)
                    nc.scalar.copy(H1T[c % 2][:, 4 * hf:4 * hf + 4, 0:m],
                                   bank(4 + hf).rearrange("p (j n) -> p j n", j=4)[:, :, 0:m]).then_inc(s_hte, 1)

            for c in range(CH):
                m = rows(c)
                act.wait_ge(s_r, c + 1)
                nc.scalar.activation(MV[0:m, c, 2:3], MV[0:m, c, 1:2], ACT.Sqrt, bias=EPSC[0:m, :]).then_inc(s_std, 1)
                act.wait_ge(s_nrm, c + 1)
                if c == 0:
                    act.wait_ge(s_store, 16 * (6 + 2 * DB))
                nc.scalar.activation(H1[0:m, c, :], RB[c % 2][0:m, :], ACT.Identity, scale=MV[0:m, c, 2:3],
                                     bias=MV[0:m, c, 3:4]).then_inc(s_z, 1)
                if c >= 1:
                    h1t_copy(c - 1)
            h1t_copy(CH - 1)
            act.wait_ge(s_rx, 1)
            nc.scalar.activation(RX1, RX1, ACT.Exp).then_inc(s_ra, 1)
            act.wait_ge(s_rx, 2)
            nc.scalar.activation(W2, W2, ACT.Exp).then_inc(s_ra, 1)

            def expert(i, j, first):
                e = i * 4 + j
                for hf in range(2):
                    act.wait_ge(s_tp, e * 2 + (hf + 1))
                    if not first:
                        act.wait_ge(s_gu, e - 1)
                    nc.scalar.copy(XGT[j % 2][:, 4 * hf:4 * hf + 4, :],
                                   bank(hf).rearrange("p (j n) -> p j n", j=4)).then_inc(s_xgt, 1)

            def silu(i, j, first):
                e = i * 4 + j
                act.wait_ge(s_gu, e + 1)
                if not first:
                    act.wait_ge(s_at, e - 1)
                nc.scalar.activation(SIL[j % 2].rearrange("p a n -> p (a n)"), bank(2 + j % 2)[:, 0:256], ACT.Silu).then_inc(s_sil, 1)

            def y_half(i, j, first):
                e = i * 4 + j
                act.wait_ge(s_y, e + 1)
                if not first:
                    act.wait_ge(s_ys[j % 2], (e - j % 2) * 8)
                nc.scalar.activation(YS[j % 2][:, 0:512], PS[:, 2048 + 1024 * (j % 2):2048 + 1024 * (j % 2) + 512], ACT.Copy,
                                     scale=GS[:, bass.ds(e, 1)]).then_inc(s_ya, 1)

            act.wait_ge(s_idx, 1)
            expert(0, 0, True)
            def turn(i, j, first, last):
                silu(i, j, first)
                if not last:
                    expert(i + (j + 1) // 4, (j + 1) % 4, first and j == 0)
                y_half(i, j, first)
            for j in range(4):
                turn(0, j, j < 2, False)
            with act.Fori(1, NE // 4 - 1) as i:
                for j in range(4):
                    turn(i, j, False, False)
            for j in range(4):
                turn(NE // 4 - 1, j, False, j == 3)
            with overflow(act):
                with act.Fori(0, BLOCKS) as b:
                    for hf in range(2):
                        act.wait_ge(o_tp, b * 2 + (hf + 1))
                        nc.scalar.copy(XGT[0][:, 4 * hf:4 * hf + 4, :], bank(hf).rearrange("p (j n) -> p j n", j=4)).then_inc(o_xgt, 1)
                    act.wait_ge(o_gu, b + 1)
                    nc.scalar.activation(SIL[0].rearrange("p a n -> p (a n)"), bank(2)[:, 0:256], ACT.Silu).then_inc(o_sil, 1)
                    act.wait_ge(o_y, b + 1)
                    nc.scalar.activation(YS[0][:, 0:512], bank(4), ACT.Copy, scale=OLF[:, 2:3]).then_inc(o_ya, 1)
            with act.Else():
                act.nop()
            for c in range(CH):
                m = rows(c)
                act.wait_ge(s_f, c + 1)
                nc.scalar.activation(MV2[0:m, c, 2:3], MV2[0:m, c, 1:2], ACT.Sqrt, bias=EPSC[0:m, :]).then_inc(s_std2, 1)
                act.wait_ge(s_nr2, c + 1)
                nc.scalar.activation(RF[c % 3][0:m, :], RF[c % 3][0:m, :], ACT.Identity, scale=MV2[0:m, c, 2:3],
                                     bias=MV2[0:m, c, 3:4]).then_inc(s_fz, 1)

        @block.vector
        def _(dve):
            step = Steps(dve, s_dve)
            V_ = nc.vector
            step(V_.memset(EPSC, EPS))
            step(V_.memset(UP[:, :, 0:UH], 0.0))
            for n in range(0, NPROJ, 2):
                d, _, _, _, scale, m, w = proj[n]
                dve.wait_ge(s_proj, n + 1)
                src = bank(n % 8)[0:m, 0:w]
                if len(d.shape) == 3:
                    src = src.rearrange("p (b t) -> p b t", t=DT)
                V_.tensor_scalar(d, src, scale, None, ALU.mult).then_inc(s_pe_d, 1)
            proj_done(dve, NPROJ - 1)
            step(V_.memset(at(47760, 1536), 0.0))
            for g in range(2):
                for hp in range(4):
                    for s in range(2):
                        r = slice(64 * s, 64 * s + 64)
                        last = V_.tensor_copy(QBD[r, g, hp, :, (2 * hp + s) * DT:(2 * hp + s) * DT + DT],
                                              QT[r, hp, SEQ + 16 * g:SEQ + 16 * g + 16].rearrange("p (b t) -> p b t", t=DT))
            for hp in range(2):
                for s in range(2):
                    for o in range(2):
                        r = slice(64 * s, 64 * s + 64)
                        c = o * 16 + (2 * hp + s) * DT
                        last = V_.tensor_copy(QBM[r, hp, :, c:c + DT].rearrange("p (b o) t -> p b o t", o=2)[:, :, o, :],
                                              QC[r, hp, SEQ:TOK].rearrange("p (b o t) -> p b o t", o=2, t=DT)[:, :, o, :])
            last.then_inc(s_srd, 1)

            def mins(u, s):
                kind, hp, i = units[u]
                x = 2 * u + s
                dve.wait_ge(s_S, x + 1)
                ps = PS[:, 1024 * s:1024 * s + 1024]
                if kind == "w":
                    if i == 0:
                        dve.wait_ge(s_tb[hp % 2], 32 * (hp // 2 + 1))
                    if u >= 2:
                        dve.wait_ge(s_T, last_T[(u - 2, s)] + 1)
                    w = P * (i + 1)
                    V_.tensor_tensor_reduce(SP[(u % 2) * 2 + s][:, 0:w], ps[:, 0:w], TB[hp % 2][s][:, SEQ - w:SEQ],
                                            1.0, 3e38, ALU.add, ALU.min, MN[:, x:x + 1]).then_inc(s_min, 1)
                else:
                    V_.tensor_reduce(MN[:, x:x + 1], ps[:, 0:N_MEM], AX.X, ALU.min).then_inc(s_min, 1)

            def evac(n):
                if n % 2 == 0:
                    dve.wait_ge(s_T, n + 1)
                    transposed_out(dve, V_.tensor_copy, n).then_inc(s_Td, 1)

            def o_out(u, s):
                x = 2 * u + s
                dve.wait_ge(s_exp, x + 1)
                step(V_.reciprocal(RD[:, x:x + 1], DEN[:, x:x + 1]))
                dve.wait_ge(s_PV, pv_upto[last_T[(u, s)]])
                if u >= 4:
                    dve.wait_ge(s_T, ot_at[u - 4] + 1)
                V_.tensor_scalar(OB[u % 4][:, 64 * s:64 * s + 64], bank(6 + s)[:, 0:HD], RD[:, x:x + 1], None,
                                 ALU.mult).then_inc(s_OB, 1)

            def normalise(g, w, p):
                dve.wait_ge(s_sexp, g + 1)
                step(V_.reciprocal(SRD[:, g:g + 1], SDEN[:, g:g + 1]))
                V_.tensor_scalar(p[:, 0:w], p[:, 0:w], SRD[:, g:g + 1], None, ALU.mult).then_inc(s_srd, 1)

            def x_out(e):
                x = xnum[e]
                dve.wait_ge(s_xp, x + 1)
                bx = bank(6)
                if e[0] == "knew":
                    V_.tensor_copy(KN[0:SMP, :], bx[0:SMP, :]).then_inc(s_xe, 1)
                elif e[0] == "pool":
                    if e[1] < 4:
                        t, hf = e[1] // 2, e[1] % 2
                        V_.tensor_scalar(CAT[:, 4 + t, 512 * hf:512 * hf + 512], bx, PSC[:, t:t + 1], None, ALU.mult).then_inc(s_xe, 1)
                    else:
                        step(V_.tensor_scalar(CAT[:, 4, SEQ:TOK], bx[:, 0:SMP], PSC[:, 0:1], None, ALU.mult))
                        V_.tensor_scalar(CAT[:, 5, SEQ:TOK], bx[:, SMP:2 * SMP], PSC[:, 1:2], None, ALU.mult).then_inc(s_xe, 1)
                elif e[0] == "ss":
                    g, kc = e[1] // 4, e[1] % 4
                    if e[1] == 0:
                        dve.wait_ge(s_bias, 16)
                        dve.wait_ge(s_pool, 2)
                        dve.wait_ge(s_store, 16 * (6 + 2 * DB))
                    if kc < 3:
                        V_.tensor_tensor(SS[:, g, kc * KC:kc * KC + KC], bx[:, 0:KC], SBIAS[:, kc * KC:kc * KC + KC], ALU.add).then_inc(s_xe, 1)
                    else:
                        step(V_.tensor_tensor(SS[:, g, 3 * KC:4 * KC], bx[:, 0:KC], SBIAS[:, 3 * KC:4 * KC], ALU.add))
                        V_.tensor_tensor(SS[:, g, NK:NK + SMP], bx[:, KC:KC + SMP], SBIAS[:, NK + SMP * g:NK + SMP * g + SMP], ALU.add).then_inc(s_xe, 1)
                        dve.wait_ge(s_xe, x + 1)
                        V_.tensor_reduce(SMN[:, g:g + 1], SS[:, g, 0:NK + SMP], AX.X, ALU.min).then_inc(s_smin, 1)
                        pending.append((g, NK + SMP, SS[:, g, :]))
                elif e[0] == "st":
                    _, g, hf = e
                    if hf == 0:
                        V_.tensor_copy(PTS[:, g, 0:4, :].rearrange("p a b -> p (a b)"), bx).then_inc(s_xe, 1)
                    else:
                        step(V_.tensor_copy(PTS[:, g, 4:7, :].rearrange("p a b -> p (a b)"), bx[:, 0:3 * P]))
                        V_.tensor_copy(PTS[0:SMP, g, 7, :], bx[0:SMP, 3 * P:4 * P]).then_inc(s_xe, 1)
                elif e[0] == "pv":
                    b = e[1]
                    o = bx[:, 0:32].rearrange("p (a c) -> p a c", a=4)
                    step(V_.tensor_copy(CAT[0:64, 0:4, SEQ + DT * b:SEQ + DT * b + DT], o[0:64, :, 0:DT]))
                    V_.tensor_copy(CAT[64:128, 0:4, SEQ + DT * b:SEQ + DT * b + DT], o[64:128, :, DT:2 * DT]).then_inc(s_xe, 1)
                elif e[0] == "ms":
                    V_.tensor_reduce(SMN[:, 2:3], bx[:, 0:N_MEM], AX.X, ALU.min).then_inc(s_smin, 1)
                    normalise(2, N_MEM, PMS)
                    dve.wait_ge(s_srd, 4)
                    dve.sem_inc(s_xe, 1)
                elif e[0] == "mt":
                    V_.tensor_copy(PTM.rearrange("p a b -> p (a b)"), bx[:, 0:2 * P]).then_inc(s_xe, 1)
                else:
                    o = bx[:, 0:P].rearrange("p (b a c) -> p b a c", b=DB, a=2)
                    for hp in range(2):
                        for s in range(2):
                            last = V_.tensor_copy(CAT[64 * s:64 * s + 64, 6 + hp, SEQ:TOK].rearrange("p (b t) -> p b t", t=DT),
                                                  o[64 * s:64 * s + 64, :, hp, DT * s:DT * s + DT])
                            if hp + s < 2:
                                step(last)
                    last.then_inc(s_xe, 1)

            pending = []
            for e in extra[-1]:
                x_out(e)
            mins(0, 0)
            mins(0, 1)
            for u in range(NU):
                for e in pending:
                    normalise(*e)
                pending.clear()
                for j, n in enumerate(unit_items[u]):
                    if n == NI - 1:
                        o_out(u, 1)
                    evac(n)
                    before = items[n - 1] if n else ("OT",)
                    if before[0] == "T" and last_T[before[1:3]] == n - 1 and n < NI - 1:
                        o_out(*before[1:3])
                    if u + 1 < NU and j < 2:
                        mins(u + 1, j)
                for e in extra[u]:
                    x_out(e)
            for c in range(CH):
                m = rows(c)
                dve.wait_ge(s_mix, c + 1)
                dve.wait_ge(s_x[c % 2], 16 * (c // 2 + 1))
                if c >= 2:
                    dve.wait_ge(s_z, c - 1)
                step(V_.scalar_tensor_tensor(RB[c % 2][0:m, :], XR[c % 2][0:m, :], ALPHA,
                                             PS[0:m, 1024 * (c % 2):1024 * (c % 2) + 1024], ALU.mult, ALU.add))
                for hf in range(2):
                    last = V_.bn_stats(BN[0:m, 0, 6 * hf:6 * hf + 6], RB[c % 2][0:m, 512 * hf:512 * hf + 512])
                step(last)
                V_.bn_aggr(MV[0:m, c, 0:2], BN[0:m, 0, :]).then_inc(s_r, 1)
                dve.wait_ge(s_std, c + 1)
                step(V_.reciprocal(MV[0:m, c, 2:3], MV[0:m, c, 2:3]))
                V_.scalar_tensor_tensor(MV[0:m, c, 3:4], MV[0:m, c, 0:1], -1.0, MV[0:m, c, 2:3], ALU.mult, ALU.mult).then_inc(s_nrm, 1)
                dve.wait_ge(s_nrm, c + 1)
            step(V_.memset(LG, 0.0))
            dve.wait_ge(s_rt, CH)
            step(V_.tensor_copy(LG[:, 0:8, :].rearrange("p c e -> p (c e)"), bank(6)[:, 0:288]))
            step(V_.tensor_copy(LG[0:SMP, 8, :], bank(6)[0:SMP, 288:324]))
            dve.wait_ge(s_gb, 64)
            step(V_.tensor_tensor(LG, LG, RT[:, 0:36].unsqueeze(1).broadcast_to([P, CH, 36]), ALU.add))
            L1 = LG[:, :, 0:NG]
            rx1 = RX1.rearrange("p (c e) -> p c e", c=CH)
            m1, p1, v1, v2, r1, r2 = (G1W[:, CH * n:CH * n + CH] for n in range(1, 7))
            g4 = [at(R0 + 1728, CH, 4), at(R0 + 1764, CH, 4)]

            def wide(x, n):
                return x.unsqueeze(2).broadcast_to([P, CH, n])

            def first_max(out, vals, top, n, scratch):
                down_ = CS[:, 3 * P:3 * P + n].unsqueeze(1).broadcast_to([P, CH, n])
                step(V_.tensor_reduce(top, vals, AX.X, ALU.max))
                step(V_.tensor_tensor(scratch, vals, wide(top, n), ALU.is_equal))
                step(V_.tensor_scalar(out, scratch, -1000.0, 1000.0, ALU.mult, ALU.add))
                step(V_.tensor_tensor(out, out, down_, ALU.add))
                step(V_.tensor_reduce(p1, out, AX.X, ALU.min))
                step(V_.tensor_tensor(out, out, wide(p1, n), ALU.is_equal))

            first_max(g4[0], L1, m1, NG, g4[1])
            step(V_.tensor_tensor(rx1, L1, wide(m1, NG), ALU.subtract))
            dve.sem_inc(s_rx, 1)
            step(V_.tensor_scalar(g4[0], g4[0], 1.0, MASKED, ALU.subtract, ALU.mult))
            step(V_.tensor_tensor(RL.rearrange("p c (g e) -> p c g e", g=NG), LG[:, :, NG:36].rearrange("p c (g e) -> p c g e", g=NG),
                                  g4[0].unsqueeze(3).broadcast_to([P, CH, NG, EPG]), ALU.add))
            first_max(RE[0], RL, v1, NE, RX)
            step(V_.tensor_scalar(RX, RE[0], -2.0 * MASKED, None, ALU.mult))
            step(V_.tensor_tensor(RL, RL, RX, ALU.add))
            first_max(RE[1], RL, v2, NE, RX)
            for k in range(2):
                step(V_.tensor_tensor(RE[k], RE[k], wide(valid, NE), ALU.mult))
            step(V_.tensor_tensor(RM, RE[0], RE[1], ALU.add))
            step(V_.memset(RMP[:, 0, :], 0.0))
            for c in range(1, CH):
                step(V_.tensor_tensor(RMP[:, c, :], RMP[:, c - 1, :], RM[:, c - 1, :], ALU.add))
            step(V_.tensor_tensor(CNT, RMP[:, CH - 1, :], RM[:, CH - 1, :], ALU.add))
            dve.sem_inc(s_M, 1)
            step(V_.tensor_tensor(W2, v2, v1, ALU.subtract))
            dve.sem_inc(s_rx, 1)
            dve.wait_ge(s_ra, 1)
            step(V_.tensor_reduce(p1, rx1, AX.X, ALU.add))
            step(V_.reciprocal(p1, p1))
            dve.wait_ge(s_ra, 2)
            step(V_.tensor_scalar(v1, W2, 1.0, None, ALU.add))
            step(V_.reciprocal(v1, v1))
            step(V_.tensor_tensor(v1, v1, p1, ALU.mult))
            step(V_.tensor_tensor(v2, v1, W2, ALU.mult))
            for k in range(2):
                step(V_.tensor_tensor(RV[:, k, :, 0:NE], RE[k], wide(tok1, NE), ALU.mult))
                step(V_.scalar_tensor_tensor(RV[:, k, :, NE:2 * NE], RE[k], float(k * TOK), RV[:, k, :, 0:NE], ALU.mult, ALU.add))
                step(V_.tensor_tensor(RV[:, k, :, 2 * NE:3 * NE], RE[k], wide((v1, v2)[k], NE), ALU.mult))
            dve.wait_ge(s_rank, 1)
            step(V_.tensor_copy(RANK.rearrange("p c e -> p (c e)"), bank(0)[:, 0:CH * NE]))
            for k in range(2):
                step(V_.tensor_tensor(RX, RE[k], bank(0)[:, 0:CH * NE].rearrange("p (c e) -> p c e", c=CH), ALU.mult))
                step(V_.tensor_reduce((r1, r2)[k], RX, AX.X, ALU.add))
            step(V_.tensor_copy(CNT, bank(0)[:, CH * NE:CH * NE + NE]))
            step(V_.tensor_reduce(NB[:, 0:1], CNT, AX.X, ALU.max))
            step(V_.tensor_scalar(FLAG, NB[:, 0:1], float(CAP), None, ALU.is_gt))
            if CAP < P:
                for x in (r1, r2):
                    step(V_.tensor_scalar(m1, x, float(CAP), 1e6, ALU.is_ge, ALU.mult))
                    step(V_.tensor_tensor(x, x, m1, ALU.add))
            for n in range(2 * CH):
                c, k = n // 2, n % 2
                if n >= 4:
                    dve.wait_ge(s_ohx, n - 3)
                V_.tensor_scalar(OH[n % 4], iota, (r1, r2)[k][:, c:c + 1], None, ALU.is_equal).then_inc(s_oh, 1)
            dve.wait_ge(s_ohx, 2 * CH)
            step(V_.tensor_copy(IDF[:, :], bank(1)[:, 0:3 * NE]))
            step(V_.tensor_scalar(RX[:, 0:2, :].rearrange("p a b -> p (a b)"), IDF[:, 0:2 * NE], 0.0, 1e6, ALU.is_equal, ALU.mult))
            step(V_.scalar_tensor_tensor(IDF[:, 0:2 * NE], IDF[:, 0:2 * NE], -1.0, RX[:, 0:2, :].rearrange("p a b -> p (a b)"), ALU.add, ALU.add))
            step(V_.tensor_copy(IDX[:, 0:2 * NE], IDF[:, 0:2 * NE]))
            for s in range(2):
                step(V_.memset(XG[s], 0.0))
            dve.sem_inc(s_idx, 1)

            def turn(i, j, first):
                e = i * 4 + j
                dve.wait_ge(s_sil, e + 1)
                if not first:
                    dve.wait_ge(s_y, e - 1)
                V_.tensor_tensor(AT[j % 2].rearrange("p a n -> p (a n)"), SIL[j % 2].rearrange("p a n -> p (a n)"),
                                 bank(2 + j % 2)[:, 256:512], ALU.mult).then_inc(s_at, 1)
                dve.wait_ge(s_y, e + 1)
                if not first:
                    dve.wait_ge(s_ys[j % 2], (e - j % 2) * 8)
                V_.tensor_scalar(YS[j % 2][:, 512:1024], PS[:, 2048 + 1024 * (j % 2) + 512:2048 + 1024 * (j % 2) + 1024],
                                 GS[:, bass.ds(e, 1)], None, ALU.mult).then_inc(s_yd, 1)

            for j in range(4):
                turn(0, j, j < 2)
            with dve.Fori(1, NE // 4) as i:
                for j in range(4):
                    turn(i, j, False)
            with overflow(dve):
                dve.wait_ge(s_ys[0], 8 * NE)
                dve.wait_ge(s_ys[1], 8 * NE)
                n_o = [0]

                def ostep(ins):
                    n_o[0] += 1
                    ins.then_inc(o_pos, 1)
                    dve.wait_ge(o_pos, n_o[0])

                ostep(V_.memset(NB, 0.0))
                for j in range(1, -(-TOK // CAP)):
                    ostep(V_.scalar_tensor_tensor(NB, CNT, float(j * CAP), NB, ALU.is_gt, ALU.add))
                ostep(V_.tensor_copy(OPRE[0], NB))
                for j in range(5):
                    a, b = OPRE[j % 2], OPRE[(j + 1) % 2]
                    ostep(V_.tensor_copy(b[:, 0:2 ** j], a[:, 0:2 ** j]))
                    ostep(V_.tensor_tensor(b[:, 2 ** j:NE], a[:, 2 ** j:NE], a[:, 0:NE - 2 ** j], ALU.add))
                ostep(V_.tensor_tensor(OTMP, OPRE[1].unsqueeze(1).broadcast_to([P, BLOCKS, NE]),
                                       iota[:, 0:BLOCKS].unsqueeze(2).broadcast_to([P, BLOCKS, NE]), ALU.is_le))
                ostep(V_.tensor_reduce(RX[:, 0, 0:BLOCKS] if BLOCKS <= NE else RX.rearrange("p c e -> p (c e)")[:, 0:BLOCKS], OTMP, AX.X, ALU.add))
                ostep(V_.tensor_scalar(EB, RX.rearrange("p c e -> p (c e)")[:, 0:BLOCKS], float(NE - 1), None, ALU.min))
                dve.sem_inc(o_eb, 1)
                dve.sem_inc(o_free, 1)
                ostep(V_.tensor_tensor(OPRE[0], OPRE[1], NB, ALU.subtract))
                for k in range(2):
                    ostep(V_.tensor_tensor(RX, RE[k], OPRE[0].unsqueeze(1).broadcast_to([P, CH, NE]), ALU.mult))
                    ostep(V_.tensor_reduce(m1, RX, AX.X, ALU.add))
                    ostep(V_.tensor_tensor(RX, RE[k], RANK, ALU.mult))
                    ostep(V_.tensor_reduce(p1, RX, AX.X, ALU.add))
                    ostep(V_.scalar_tensor_tensor(OPOS[:, k, :], m1, float(CAP), p1, ALU.mult, ALU.add))
                    ostep(V_.tensor_scalar(p1, p1, float(CAP), -1e6, ALU.is_lt, ALU.mult))
                    ostep(V_.tensor_tensor(OPOS[:, k, :], OPOS[:, k, :], p1, ALU.add))
                    ostep(V_.tensor_tensor(OVAL[:, k, :, 0], tok1, valid, ALU.mult))
                    ostep(V_.scalar_tensor_tensor(OVAL[:, k, :, 1], valid, float(k * TOK), OVAL[:, k, :, 0], ALU.mult, ALU.add))
                    ostep(V_.tensor_tensor(OVAL[:, k, :, 2], (v1, v2)[k], valid, ALU.mult))
                    ostep(V_.memset(OVAL[:, k, :, 3], 0.0))
                per_block = 5
                with dve.Fori(0, BLOCKS) as b:
                    def bstep(ins, n):
                        ins.then_inc(o_pos, 1)
                        dve.wait_ge(o_pos, b * per_block + (n_o[0] + n))

                    dve.wait_ge(o_free, b + 1)
                    bstep(V_.tensor_scalar(OPOS, OPOS, float(CAP), None, ALU.subtract), 1)
                    for n in range(2 * CH):
                        if n >= 4:
                            dve.wait_ge(o_ohx, b * 2 * CH + (n - 3))
                        V_.tensor_scalar(OH[n % 4], iota, OPOS[:, n % 2, n // 2:n // 2 + 1], None, ALU.is_equal).then_inc(o_oh, 1)
                    dve.wait_ge(o_ohx, b * 2 * CH + 2 * CH)
                    bstep(V_.tensor_copy(OLF, bank(1)[:, 0:4]), 2)
                    bstep(V_.tensor_scalar(OPRE[0][:, 0:2], OLF[:, 0:2], 0.0, 1e6, ALU.is_equal, ALU.mult), 3)
                    bstep(V_.scalar_tensor_tensor(OPRE[0][:, 0:2], OLF[:, 0:2], -1.0, OPRE[0][:, 0:2], ALU.add, ALU.add), 4)
                    bstep(V_.tensor_copy(OLI, OPRE[0][:, 0:2]), 5)
                    dve.sem_inc(o_idx, 1)
                    dve.wait_ge(o_sil, b + 1)
                    V_.tensor_tensor(AT[0].rearrange("p a n -> p (a n)"), SIL[0].rearrange("p a n -> p (a n)"),
                                     bank(2)[:, 256:512], ALU.mult).then_inc(o_at, 1)
                    dve.wait_ge(o_ya, b + 1)
                    V_.tensor_scalar(YS[0][:, 512:1024], bank(5), OLF[:, 2:3], None, ALU.mult).then_inc(o_yd, 1)
            with dve.Else():
                dve.nop()
            for c in range(CH):
                m = rows(c)
                dve.wait_ge(s_f1, c + 1)
                for hf in range(2):
                    last = V_.bn_stats(BN[0:m, 1, 6 * hf:6 * hf + 6], RF[c % 3][0:m, 512 * hf:512 * hf + 512])
                step(last)
                V_.bn_aggr(MV2[0:m, c, 0:2], BN[0:m, 1, :]).then_inc(s_f, 1)
                dve.wait_ge(s_std2, c + 1)
                step(V_.reciprocal(MV2[0:m, c, 2:3], MV2[0:m, c, 2:3]))
                V_.scalar_tensor_tensor(MV2[0:m, c, 3:4], MV2[0:m, c, 0:1], -1.0, MV2[0:m, c, 2:3], ALU.mult, ALU.mult).then_inc(s_nr2, 1)
                dve.wait_ge(s_nr2, c + 1)
                dve.wait_ge(s_fz, c + 1)
                if c == 0:
                    dve.wait_ge(s_gb2, 32)
                step(V_.tensor_tensor(RF[c % 3][0:m, :], RF[c % 3][0:m, :], GB[0:m, 0, :], ALU.mult))
                V_.tensor_tensor(RF[c % 3][0:m, :], RF[c % 3][0:m, :], GB[0:m, 1, :], ALU.add).then_inc(s_fo, 1)

        @block.gpsimd
        def _(pool):
            step = Steps(pool, s_pl)
            G = nc.gpsimd
            proj_done(pool, NPROJ - 1)
            pool.wait_ge(s_state, 48)
            pool.wait_ge(s_dve, 2)
            pool.wait_ge(s_const, 16)

            def sums(u, a, b, n, ap):
                step(G.tensor_tensor(ap(a, 0, 1, n), ap(u, 0, 1, n), ap(u, 0, 0, n - 1), ALU.add))
                step(G.tensor_tensor(ap(b, 0, 3, n), ap(a, 0, 3, n), ap(a, 0, 1, n - 2), ALU.add))
                step(G.tensor_tensor(ap(a, 1, 7, n), ap(b, 1, 7, n), ap(b, 1, 3, n - 4), ALU.add))
                step(G.tensor_tensor(ap(b, 1, 15, n), ap(a, 1, 15, n), ap(a, 1, 7, n - 8), ALU.add))

            def prompt_ap(x, t0, lo, hi):
                return x[:, t0:2, lo:hi]

            def sample_ap(x, t0, lo, hi):
                return x[:, t0, :, lo:hi] if t0 else x[:, :, :, lo:hi]

            sums(UP, PA, PBUF, UH + SEQ, prompt_ap)
            for t in range(2):
                for g in range(2):
                    r = slice(64 * g, 64 * g + 64)
                    src = (PA, PBUF)[g]
                    step(G.tensor_tensor(PA[r, t, UH:UH + 16], src[r, t, UH:UH + 16], pool_inv[r, t, 0:16], ALU.mult))
                    step(G.tensor_scalar(PA[r, t, UH + 16:UH + SEQ], src[r, t, UH + 16:UH + SEQ], pool_inv[r, t, 16:17], None, ALU.mult))
            G.tensor_tensor(PA[:, :, UH:UH + SEQ], PA[:, :, UH:UH + SEQ], UP[:, :, UH:UH + SEQ], ALU.subtract).then_inc(s_pool, 1)
            sums(US, SA, SBF, PB + DT, sample_ap)
            for t in range(2):
                for g in range(2):
                    r = slice(64 * g, 64 * g + 64)
                    src = (SA, SBF)[g]
                    step(G.tensor_scalar(SA[r, t, :, PB:PB + DT], src[r, t, :, PB:PB + DT], pool_inv[r, t, 16:17], None, ALU.mult))
            G.tensor_tensor(SA[:, :, :, PB:PB + DT], SA[:, :, :, PB:PB + DT], US[:, :, :, PB:PB + DT], ALU.subtract).then_inc(s_pool, 1)
            for c in range(CH):
                m = rows(c)
                pool.wait_ge(s_z, c + 1)
                if c == 0:
                    pool.wait_ge(s_gb, 64)
                step(G.tensor_tensor(H1[0:m, c, :], H1[0:m, c, :], GB[0:m, 0, :], ALU.mult))
                G.tensor_tensor(H1[0:m, c, :], H1[0:m, c, :], GB[0:m, 1, :], ALU.add).then_inc(s_h1, 1)
            pool.wait_ge(s_idx, 1)
            pool.wait_ge(s_h1d, 16 * CH)

            def await_(sem_, count):
                pool.wait_ge(sem_, count)
                pool.sem_inc(s_past, 1)

            def column(dst, src, count):
                G.tensor_copy(dst, src).then_inc(s_col, 1)
                await_(s_col, count)

            last_token, last_pair = pool.to_reg(TOK - 1), pool.to_reg(NPAIR - 1)

            def gather(e, sl, count):
                column(GI[sl], e, count)
                G.indirect_dma_start(XG[sl], None, h1_d, bass.IndirectOffsetOnAxis(ap=GI[sl], axis=0),
                                     bounds_check=last_token, oob_is_err=False).then_inc(s_gx[sl], 16)

            def scatter(e, sl, count):
                column(SI[sl], e, count)
                G.indirect_dma_start(pair_d, bass.IndirectOffsetOnAxis(ap=SI[sl], axis=0), YS[sl], None,
                                     bounds_check=last_pair, oob_is_err=False).then_inc(s_ys[sl], 16)

            gather(IDX[:, 0:1], 0, 1)
            gather(IDX[:, 1:2], 1, 2)
            for c in range(CH):
                step(G.tensor_scalar(H1[0:rows(c), c, :], H1[0:rows(c), c, :], ALPHA, None, ALU.mult))

            def turn(i, j, last):
                e = i * 4 + j
                to_gather = IDX[:, bass.ds(e + 2, 1)] if last else IDX[:, bass.ds(pool.snap(e + 2), 1)] if not isinstance(i, int) else IDX[:, e + 2:e + 3]
                to_scatter = IDX[:, bass.ds(pool.snap(e + NE), 1)] if not isinstance(i, int) else IDX[:, NE + e:NE + e + 1]
                if not last:
                    pool.wait_ge(s_tp, e * 2 + 2)
                    gather(to_gather, j % 2, e * 2 + 3)
                pool.wait_ge(s_ya, e + 1)
                pool.wait_ge(s_yd, e + 1)
                scatter(to_scatter, j % 2, e * 2 + 4 if not last else NE + e + 1)

            with pool.Fori(0, NE // 4 - 1) as i:
                for j in range(4):
                    turn(i, j, False)
            for j in range(4):
                turn(NE // 4 - 1, j, j >= 2)
            with overflow(pool):
                with pool.Fori(0, BLOCKS) as b:
                    await_(o_idx, b + 1)
                    G.indirect_dma_start(XG[0], None, h1_d, bass.IndirectOffsetOnAxis(ap=OLI[:, 0:1], axis=0),
                                         bounds_check=last_token, oob_is_err=False).then_inc(o_g, 16)
                    await_(o_yd, b + 1)
                    G.indirect_dma_start(pair_d, bass.IndirectOffsetOnAxis(ap=OLI[:, 1:2], axis=0), YS[0], None,
                                         bounds_check=last_pair, oob_is_err=False).then_inc(o_s, 16)
                    pool.wait_ge(o_s, b * 16 + 16)
                    pool.sem_inc(o_free, 1)
            with pool.Else():
                pool.nop()
            pool.wait_ge(s_y, NE)
            for c in range(CH):
                m = rows(c)
                pool.wait_ge(s_yp[c % 3], 16 * (c // 3 + 1))
                if c >= 3:
                    pool.wait_ge(s_out[c % 3], 16 * (c // 3))
                step(G.tensor_tensor(RF[c % 3][0:m, :], YP[c % 3][0:m, 0, :], YP[c % 3][0:m, 1, :], ALU.add))
                G.tensor_tensor(RF[c % 3][0:m, :], RF[c % 3][0:m, :], H1[0:m, c, :], ALU.add).then_inc(s_f1, 1)


_OUT = {"y": (TOK, D), "kT": (D_A, SEQ), "v": (SEQ, D_A), "uT": (D_B, PB), "kmT": (D_C, N_MEM), "vm": (N_MEM, D_C),
        "win_k_s": (DB, WB, D_A), "win_v_s": (DB, WB, D_A), "poolT_s": (P, 2 * DB, PB)}


def laid_out(i):
    a = {n: np.asarray(v) for n, v in i.items()}
    x = np.concatenate([a["x_prompt"].reshape(SEQ, D), a["x_sample"].reshape(SMP, D)])
    wk = a["cache_win_k"][0][:, ROWS].reshape(2, 4, 4, KC, 4, 2, HD)
    wk = wk.transpose(0, 3 - 1, 5, 6, 4, 1, 3).reshape(8, P, 4, 4 * KC)
    mk = a["cache_mem_k"][0].reshape(DB, N_MEM, 2, 2, HD).transpose(3, 4, 2, 0, 1).reshape(P, 2, DB * N_MEM)
    out = {
        "x": x, "xT": x.T, "memT": a["mem_prompt"][0].T, "stateT": a["state_pool"][0].transpose(2, 0, 1).reshape(2, P, DB, PB).transpose(1, 0, 2, 3).reshape(P, 2 * DB, PB),
        "winkT": wk, "memkT": mk,
        "cache_win_k": a["cache_win_k"].reshape(DB, WB, D_A), "cache_win_v": a["cache_win_v"].reshape(DB, WB, D_A),
        "cache_mem_v": a["cache_mem_v"].reshape(DB, N_MEM, D_C),
        "w_in": a["w_in"][0], "w_mem_kv": a["w_mem_kv"][0], "w_pool": a["w_pool"][0], "pool_scale": a["pool_scale"][0].reshape(2, P).T,
        "w_o": a["w_o"][0], "w_r": np.concatenate([a["w_r1"][0], a["w_r2"][0].transpose(1, 0, 2).reshape(D, NE)], axis=1),
        "b_r": np.concatenate([a["b_r1"][0], a["b_r2"][0].reshape(NE)]),
        "w_gate": a["w_gate"].reshape(NE, D, DE), "w_up": a["w_up"].reshape(NE, D, DE), "w_down": a["w_down"].reshape(NE, DE, D),
        **{n: a[n][0] for n in ("ln1_g", "ln1_b", "ln2_g", "ln2_b")}, **shape_constants(),
    }
    return {n: np.ascontiguousarray(v) for n, v in out.items()}


def results(r):
    y = r["y"]
    heads = lambda t, n: t.reshape(1, 1, -1, n, HD)
    return (y[:SEQ].reshape(1, SEQ, D), y[SEQ:].reshape(DB, DT, D),
            heads(np.ascontiguousarray(r["kT"].T), HA), heads(r["v"], HA),
            np.ascontiguousarray(r["uT"].T).reshape(1, 1, PB, D_B),
            heads(np.ascontiguousarray(r["kmT"].T), HC), heads(r["vm"], HC),
            r["win_k_s"].reshape(1, DB, WB, HA, HD), r["win_v_s"].reshape(1, DB, WB, HA, HD),
            np.ascontiguousarray(r["poolT_s"].reshape(P, 2, DB, PB).transpose(2, 3, 1, 0)).reshape(1, DB, PB, D_B))


def kernel(**inputs):
    import concourse.bacc as _bacc
    from concourse.bass_utils import run_bass_kernel_spmd as _run

    nc = _bacc.Bacc("TRN2", target_bir_lowering=False, num_devices=1)
    arrays = laid_out(inputs)
    ins = {n: nc.dram_tensor(n, a.shape, F32, kind="ExternalInput").ap() for n, a in arrays.items()}
    outs = {n: nc.dram_tensor("out_" + n, s, F32, kind="ExternalOutput").ap() for n, s in _OUT.items()}
    build(nc, ins, outs)
    r = _run(nc, [arrays], core_ids=[0])
    return results({n: r.results[0]["out_" + n] for n in _OUT})
```

```python
from contextlib import ExitStack

import concourse.bass as bass
import numpy as np
from concourse import mybir

F32 = mybir.dt.float32
U32 = mybir.dt.uint32
ALU = mybir.AluOpType
ACT = mybir.ActivationFunctionType
AX = mybir.AxisListType

P = 128
D = 1024
KT = D // P
SEQ = 1024
DB, DT = 8, 4
SMP = DB * DT
TOK = SEQ + SMP
CH = SEQ // P + 1
HD = 64
HA, HC = 8, 4
D_A, D_B, D_C = 512, 256, 256
N_MEM = 256
WB = 2048
PB = 15
PATTERNS = ((128, 1), (512, 4), (2048, 16))
NG, EPG = 4, 8
NE = NG * EPG
DE = 256
ALPHA = 2.0 ** 0.25
EPS = 1e-5
QS = -(HD ** -0.5)
MASKED = 1e30

FAR = [16 * j + t for j in range((WB - 512) // 16) for t in range(DT)]
NEAR = list(range(WB - 512, WB))
ROWS = FAR + NEAR
NK = len(ROWS)
KC = NK // 4
NVT = NK // P

CAP = 128
NPAIR = 2 * TOK
BLOCKS = NPAIR // CAP


def distance_bias(dist):
    dist = np.asarray(dist)
    c = np.zeros(dist.shape)
    for w, d in PATTERNS:
        c += (dist >= 0) & (dist <= w) & (dist % d == 0)
    return np.where(c > 0, -np.log(np.maximum(c, 1)), MASKED)


def shape_constants():
    slopes = 2.0 ** (-8.0 * np.arange(1, HA + 1) / HA)
    p, u = np.arange(P)[:, None], np.arange(SEQ)[None, :]
    dist = p + SEQ - P - u
    table = np.stack([distance_bias(dist) + s * np.maximum(dist, 0) for s in slopes])
    b, h, t = np.meshgrid(np.arange(4), np.arange(HA), np.arange(DT), indexing="ij")
    b, h, t = (x.reshape(P, 1) for x in (b, h, t))
    d_win = WB + t - np.array(ROWS)[None, :]
    win = distance_bias(d_win) + slopes[h] * d_win
    new = []
    for g in range(2):
        kb, kt = np.arange(SMP)[None, :] // DT, np.arange(SMP)[None, :] % DT
        dn = np.where(kb == 4 * g + b, t - kt, -1)
        new.append(distance_bias(dn) + slopes[h] * np.maximum(dn, 0))
    sample = np.concatenate([win] + new, axis=1)
    inv = np.zeros((P, 2, 17))
    for tile in range(2):
        for half in range(2):
            w = 2 ** (2 * tile + half + 1)
            inv[64 * half:64 * half + 64, tile, :16] = 1.0 / np.minimum(w, np.arange(16) + 1)
            inv[64 * half:64 * half + 64, tile, 16] = 1.0 / w
    tri = (np.arange(P)[:, None] < np.arange(P)[None, :]).astype(np.float32)
    iota = np.broadcast_to(np.arange(P), (P, P))
    small = np.concatenate([np.eye(P), tri, np.ones((P, P)), iota, inv.reshape(P, 34),
                            1.0 + np.arange(P)[:, None] + P * np.arange(CH)[None, :],
                            (np.arange(P)[:, None] + P * np.arange(CH)[None, :] < TOK)], axis=1)
    f = np.float32
    return {"c_table": table.astype(f), "c_sample": sample.astype(f), "c_small": small.astype(f)}


class Steps:

    def __init__(self, eng, sem):
        self.eng, self.sem, self.n = eng, sem, 0

    def __call__(self, ins):
        self.n += 1
        ins.then_inc(self.sem, 1)
        self.eng.wait_ge(self.sem, self.n)


def build(nc, I, O):
    ctx = ExitStack()
    with ctx:
        def sem(name):
            return ctx.enter_context(nc.semaphore(name))

        AR = ctx.enter_context(nc.sbuf_tensor("arena", [P, 51920], F32))
        PS = ctx.enter_context(nc.psum_tensor("psum", [P, 8 * 512], F32))
        CS = ctx.enter_context(nc.sbuf_tensor("consts", [P, 4 * P + 34 + 2 * CH], F32))
        ST = ctx.enter_context(nc.sbuf_tensor("stats", [P, 420], F32))
        h1_d = nc.dram_tensor("h1_d", [TOK, D], F32, kind="Internal").ap()
        pair_d = nc.dram_tensor("pair_d", [NPAIR, D], F32, kind="Internal").ap()

        def at(off, *dims):
            n = int(np.prod(dims))
            v = AR[:, off:off + n]
            if len(dims) == 2:
                v = v.rearrange("p (a b) -> p a b", a=dims[0])
            elif len(dims) == 3:
                v = v.rearrange("p (a b c) -> p a b c", a=dims[0], b=dims[1])
            elif len(dims) == 4:
                v = v.rearrange("p (a b c d) -> p a b c d", a=dims[0], b=dims[1], c=dims[2])
            return v

        def bank(n):
            return PS[:, 512 * n:512 * n + 512]

        ident, tri, ones, iota = (CS[:, P * n:P * n + P] for n in range(4))
        pool_inv = CS[:, 4 * P:4 * P + 34].rearrange("p (a b) -> p a b", a=2)
        tok1 = CS[:, 4 * P + 34:4 * P + 34 + CH]
        valid = CS[:, 4 * P + 34 + CH:4 * P + 34 + 2 * CH]

        QT, KTT, QC, UH = at(0, 4, TOK), at(4224, 4, TOK), at(8448, 2, TOK), 16
        V = at(10560, CH, D_A)
        KM, VM = at(15168, 2, N_MEM), at(15680, 2, D_C)
        UP = at(16192, 2, UH + SEQ)
        US = at(16192 + 2 * (UH + SEQ), 2, DB, PB + DT)
        USF = at(16192 + 2 * (UH + SEQ), 2 * DB, PB + DT)
        SS = at(16192, 2, 960)
        CAT = at(18576, KT, TOK)
        PA = AR[:, 18576 + 6 * TOK:18576 + 6 * TOK + 2 * (UH + SEQ)].rearrange("p (a b) -> p a b", a=2)
        PBUF = AR[:, 18576 + 2 * TOK:18576 + 2 * TOK + 2 * (UH + SEQ)].rearrange("p (a b) -> p a b", a=2)
        XT = at(27024, KT, TOK)
        WR = [at(35472 + 4096 * s, KT, 512) for s in range(3)]
        MT = at(47760, KT, N_MEM)
        RING = [27024, 27024 + 4096]
        SP = [at(x, 1024) for x in (35472, 36496, 37520, 38544, 41616, 42640)]
        PTB = [at(39568 + 512 * s, 4, P) for s in range(4)]
        PTS = at(18576 + 6 * TOK, 2, 8, P)
        TB = [[at(43664 + 2048 * a + 1024 * b, 1024) for b in range(2)] for a in range(2)]
        QBD = at(47760, 2, 4, 4, 32)
        QBM = at(48784, 2, DB, 32)
        PMS, PTM = at(49296, N_MEM), at(49552, 2, P)
        SBIAS = at(49808, 960)
        DG = [at(50768 + 2 * P * s, 2, P) for s in range(2)]
        KN = at(51280, 512)
        INV = at(51792, P)
        OA = at(51280, 512)
        SA, SBF = at(27024 + 3584, 2, DB, PB + DT), at(31120 + 3584, 2, DB, PB + DT)
        WO = at(27024, KT, D)
        XR = [at(35472 + D * s, D) for s in range(2)]
        GB = at(37520, 2, D)
        H1 = at(0, CH, D)
        H1T = [at(9216 + D * s, KT, P) for s in range(2)]
        RB = [at(11264 + D * s, D) for s in range(2)]
        WRT = at(13312, KT, 36)
        LG = at(13600, CH, 36)
        SLOT = [39568, 45712, 18576, 24720]
        WG = [at(s, KT, DE) for s in SLOT]
        WU = [at(s + 2048, KT, DE) for s in SLOT]
        WD = [at(s + 4096, 2, D) for s in SLOT]
        XG = [at(30864 + D * s, D) for s in range(2)]
        XGT = [at(32912 + D * s, KT, P) for s in range(2)]
        SIL = [at(13312 + 2048 + 256 * s, 2, P) for s in range(2)]
        AT = [at(13312 + 2560 + 256 * s, 2, P) for s in range(2)]
        YS = [at(9216 + D * s, D) for s in range(2)]
        YP = [at(39568 + 2048 * s, 2, D) for s in range(3)]
        RF = [at(18576 + D * s, D) for s in range(3)]

        MN, DEN, RD = ST[:, 0:96], ST[:, 96:192], ST[:, 192:288]
        SMN, SDEN, SRD = ST[:, 288:291], ST[:, 291:294], ST[:, 294:297]
        BN = ST[:, 300:300 + 24].rearrange("p (c s) -> p c s", c=2)
        MV = ST[:, 330:330 + 4 * CH].rearrange("p (c s) -> p c s", c=CH)
        MV2 = ST[:, 370:370 + 4 * CH].rearrange("p (c s) -> p c s", c=CH)
        EPSC = ST[:, 297:298]
        PSC = ST[:, 298:300]
        WPL2 = ctx.enter_context(nc.sbuf_tensor("w_pool2", [P, 2, 64], F32))
        RT = ctx.enter_context(nc.sbuf_tensor("routing", [P, 72], F32))

        FLAG = at(35300, 1).bitcast(U32)
        CNT, NB = at(35301, NE), at(35333, NE)
        EB = at(35365, BLOCKS).bitcast(U32)
        OPOS, OVAL = at(15872 + 512, 2, CH), at(15872 + 530, 2, CH, 4)
        OLF, OLI = at(16500, 4), at(16504, 2).bitcast(U32)
        OPRE = [at(16510, NE), at(16542, NE)]
        OTMP = at(39568 + 6144, BLOCKS, NE)

        s_const, s_bias = sem("s_const"), sem("s_bias")
        s_xk = [sem(f"s_xk{k}") for k in range(KT)]
        s_w = [sem(f"s_w{g}") for g in range(5)]
        s_mem, s_state = sem("s_mem"), sem("s_state")
        s_proj = sem("s_proj")
        s_pe_d, s_pe_a = sem("s_pe_d"), sem("s_pe_a")
        s_copy = [sem(f"s_copy{i}") for i in range(2)]
        s_store = sem("s_store")
        s_halo, s_pool = sem("s_halo"), sem("s_pool")
        s_tb = [sem(f"s_tb{i}") for i in range(2)]
        s_ring = [sem(f"s_ring{i}") for i in range(2)]
        s_S, s_min, s_exp = sem("s_S"), sem("s_min"), sem("s_exp")
        s_rd, s_dg, s_inv = sem("s_rd"), sem("s_dg"), sem("s_inv")
        s_T, s_Td, s_Ta, s_PV, s_O, s_OB = sem("s_T"), sem("s_Td"), sem("s_Ta"), sem("s_PV"), sem("s_O"), sem("s_OB")
        s_xp, s_xe, s_sexp, s_smin, s_srd = sem("s_xp"), sem("s_xe"), sem("s_sexp"), sem("s_smin"), sem("s_srd")
        s_dve, s_pl, s_ac = sem("s_dve"), sem("s_pl"), sem("s_ac")
        s_wo, s_gb, s_mix, s_r = sem("s_wo"), sem("s_gb"), sem("s_mix"), sem("s_r")
        s_x = [sem(f"s_x{i}") for i in range(2)]
        s_std, s_nrm, s_z, s_h1 = sem("s_std"), sem("s_nrm"), sem("s_z"), sem("s_h1")
        s_ht, s_hte, s_rt = sem("s_ht"), sem("s_hte"), sem("s_rt")
        s_h1d = sem("s_h1d")
        s_M, s_rank, s_oh, s_ohx, s_idx = sem("s_M"), sem("s_rank"), sem("s_oh"), sem("s_ohx"), sem("s_idx")
        s_rx, s_ra, s_ahh = sem("s_rx"), sem("s_ra"), sem("s_ahh")
        s_g = [sem(f"s_g{i}") for i in range(4)]
        s_wd = [sem(f"s_wd{i}") for i in range(4)]
        s_gx = [sem(f"s_gx{i}") for i in range(2)]
        s_col, s_past = sem("s_col"), sem("s_past")
        s_tp, s_xgt, s_gu, s_sil, s_at, s_y, s_ya, s_yd = (sem(n) for n in
                                                      ("s_tp", "s_xgt", "s_gu", "s_sil", "s_at", "s_y", "s_ya", "s_yd"))
        s_ys = [sem(f"s_ys{i}") for i in range(2)]
        s_gb2, s_ah = sem("s_gb2"), sem("s_ah")
        s_yp = [sem(f"s_yp{i}") for i in range(3)]
        s_f, s_f1, s_fz, s_fo, s_std2, s_nr2 = (sem(n) for n in ("s_f", "s_f1", "s_fz", "s_fo", "s_std2", "s_nr2"))
        s_out = [sem(f"s_out{i}") for i in range(3)]

        o_pos, o_eb, o_oh, o_ohx, o_idx, o_col = (sem(n) for n in ("o_pos", "o_eb", "o_oh", "o_ohx", "o_idx", "o_col"))
        o_free = sem("o_free")
        o_w, o_g, o_s = sem("o_w"), sem("o_g"), sem("o_s")
        o_tp, o_xgt, o_gu, o_sil, o_at, o_y, o_ya, o_yd = (sem(n) for n in
                                                           ("o_tp", "o_xgt", "o_gu", "o_sil", "o_at", "o_y", "o_ya", "o_yd"))

        block = ctx.enter_context(nc.Block())

        def overflow(eng):
            eng.wait_ge(s_idx, 1)
            return eng.If(eng.value_load(FLAG[0:1, 0:1], min_val=0, max_val=1) > 0)

        def rows(c):
            return P if c < CH - 1 else SMP

        W_G = {"q": 0, "k": 1, "v": 2, "u": 3, "m": 4}
        W_SLOT = [0, 1, 2, 0, 1]
        proj = []

        def proj_tile(dest3, wgrp, col):
            w = WR[W_SLOT[W_G[wgrp]]]
            return [(d, lambda k, c=col, w=w: w[:, k, c:c + P], lambda k, a=a, n=n: XT[:, k, a:a + n], W_G[wgrp], s, P, n)
                    for d, a, n, s in dest3]

        for m in range(4):
            proj += proj_tile([(QT[:, m, 0:512], 0, 512, QS), (QT[:, m, 512:1024], 512, 512, QS)], "q", m * P)
        for m in range(4):
            proj += proj_tile([(QT[:, m, SEQ:TOK], SEQ, SMP, QS)], "q", m * P)
        for m in range(4):
            proj += proj_tile([(KTT[:, m, a:a + n], a, n, 1.0) for a, n in ((0, 512), (512, 512), (SEQ, SMP))], "k", m * P)
        for c in range(CH):
            proj.append((V[0:rows(c), c, :], lambda k, c=c: XT[:, k, c * P:c * P + rows(c)],
                         lambda k: WR[2][:, k, :], W_G["v"], 1.0, rows(c), 512))
        for m in range(2):
            proj += proj_tile([(UP[:, m, UH:UH + 512], 0, 512, 1.0), (UP[:, m, UH + 512:UH + SEQ], 512, 512, 1.0),
                               (US[:, m, :, PB:PB + DT], SEQ, SMP, 1.0)], "u", m * P)
        n_u = len(proj)
        for m in range(2):
            proj += proj_tile([(QC[:, m, a:a + n], a, n, QS) for a, n in ((0, 512), (512, 512), (SEQ, SMP))], "u", D_B + m * P)
        n_x = len(proj)
        for m in range(2):
            proj.append((KM[:, m, :], lambda k, m=m: WR[1][:, k, m * P:m * P + P], lambda k: MT[:, k, :], W_G["m"], 1.0, P, N_MEM))
        for m in range(2):
            proj.append((VM[:, m, :], lambda k, m=m: MT[:, k, m * P:m * P + P], lambda k: WR[1][:, k, 256:512], W_G["m"], 1.0, P, N_MEM))
        NPROJ = len(proj)
        last_of = {g: max(n for n, t in enumerate(proj) if t[3] == g) for g in range(5)}

        def proj_done(eng, n):
            eng.wait_ge(s_pe_d, n // 2 + 1)
            if n >= 1:
                eng.wait_ge(s_pe_a, (n + 1) // 2)

        units = [("w", hp, i) for hp in range(4) for i in range(8)] + [("c", hp, i) for hp in range(2) for i in range(8)]
        NU = len(units)
        items = []
        unit_items = []
        for u, (kind, hp, i) in enumerate(units):
            nb = i + 1 if kind == "w" else 2
            unit_items.append(list(range(len(items), len(items) + (nb + 1) // 2)))
            items += [(u, list(range(b0, min(b0 + 2, nb))), nb) for b0 in range(0, nb, 2)]
        NI = len(items)

        def item_done(eng, n):
            if n % 2 == 0:
                eng.wait_ge(s_Td, n // 2 + 1)
            else:
                eng.wait_ge(s_Ta, n // 2 + 1)

        extra = {u: [] for u in range(-1, NU)}
        extra[-1] = [("knew",)]
        sample_steps = ([("pool", j) for j in range(5)] + [("ss", s) for s in range(6)] + [("st", 0, 0), ("st", 0, 1)]
                        + [("ss", 6), ("ss", 7), ("pv", 0, 0), ("pv", 0, 1), ("st", 1, 0), ("st", 1, 1)]
                        + [("pv", 0, 2), ("pv", 0, 3), ("ot", 0)] + [("pv", 1, p) for p in range(4)] + [("ot", 1)])
        for j, e in enumerate(sample_steps):
            extra[32 - len(sample_steps) + j].append(e)
        extra[34].append(("ms",))
        extra[36].append(("mt",))
        extra[38].append(("mpv",))
        xlist = [e for u in range(-1, NU) for e in extra[u]]
        xnum = {e: n for n, e in enumerate(xlist)}
        xbank = {e: 6 + (u + 1) % 2 for u in range(-1, NU) for e in extra[u]}
        x_before = [sum(len(extra[w]) for w in range(-1, u)) for u in range(NU)]
        ring_user = [e for e in xlist if e[0] in ("ss", "pv", "ms", "mpv")]
        ring_no = {e: n for n, e in enumerate(ring_user)}

        def ring_dmas(e):
            return sum(4 if t < 3 else 1 for t in pv_tiles(e[2])) if e[0] == "pv" else 1

        def pv_tiles(p):
            return range(2 * p, min(2 * p + 2, NVT))

        def ring_ready(eng, e):
            n = ring_no[e]
            eng.wait_ge(s_ring[n % 2], 16 * sum(ring_dmas(f) for f in ring_user[n % 2:n + 1:2]))

        def score_at(u, s):
            return 1024 * s + (512 * (u % 2) if units[u][0] == "c" else 0)

        def load_table(sp, hp):
            if hp >= 2:
                sp.wait_ge(s_min, 2 * 8 * (hp - 1))
            elif hp == 0:
                proj_done(sp, last_of[2])
            for s in range(2):
                sp.dma_start(TB[hp % 2][s], I["c_table"][2 * hp + s]).then_inc(s_tb[hp % 2], 16)

        def ring_load(n, e):
            off = RING[n % 2]
            if e[0] == "ss":
                return [at(off, 4, 4 * KC)], [I["winkT"][e[1]].rearrange("p a n -> p a n")]
            if e[0] == "pv":
                dst = at(off, 2, 4, 512)
                to, srcs = [], []
                for t in pv_tiles(e[2]):
                    if t < 3:
                        for b in range(4):
                            far = I["cache_win_v"][4 * e[1] + b][0:WB - 512, :].rearrange("(j r) n -> j (r n)", r=16)[:, 0:DT * 512]
                            to.append(dst[:, t % 2, b, :])
                            srcs.append(far[32 * t:32 * t + 32, :].rearrange("j (r n) -> j r n", r=DT))
                    else:
                        r0 = WB - 512 + P * (t - 3)
                        to.append(dst[:, t % 2, :, :])
                        srcs.append(I["cache_win_v"][4 * e[1]:4 * e[1] + 4, r0:r0 + P, :].rearrange("b p n -> p b n"))
                return to, srcs
            if e[0] == "ms":
                return [at(off, 2, DB * N_MEM)], [I["memkT"]]
            return [at(off, DB * 2, D_C)], [I["cache_mem_v"].rearrange("b (t p) n -> p (b t) n", p=P)]

        def load_gu(sp, e, j):
            for w, d in (("w_gate", WG), ("w_up", WU)):
                src = I[w][bass.ds(e, 1)].rearrange("o (k p) n -> p (o k) n", p=P)
                sp.dma_start(d[j], src).then_inc(s_g[j], 16)

        def load_dn(sp, e, j):
            src = I["w_down"][bass.ds(e, 1)].rearrange("o (k p) n -> p (o k) n", p=P)
            sp.dma_start(WD[j], src).then_inc(s_wd[j], 16)

        def load_expert(sp, e, j):
            load_gu(sp, e, j)
            load_dn(sp, e, j)

        R0 = 13600 + 324
        RM, RMP = at(R0, CH, NE), at(R0 + 288, CH, NE)
        RE = [at(R0 + 576, CH, NE), at(R0 + 864, CH, NE)]
        RL = at(R0 + 1152, CH, NE)
        RANK = at(17800, CH, NE)
        RX = at(R0 + 1440, CH, NE)
        RV = AR[:, 30864:30864 + 2 * CH * 96].rearrange("p (k c n) -> p k c n", k=2, c=CH)
        OH = [at(32912 + P * s, P) for s in range(4)]
        IDX = at(34960, 3 * NE).bitcast(U32)
        IDF = at(35056, 3 * NE)

        def transposed_out(eng, copy, n):
            if n >= 4:
                eng.wait_ge(s_PV, n - 3)
            w = 2 * P * len(items[n][1])
            return copy(PTB[n % 4].rearrange("p a b -> p (a b)")[:, 0:w], bank(4 + n % 2)[:, 0:w])

        GI = [at(35296 + n, 1).bitcast(U32) for n in range(2)]
        SI = [at(35298 + n, 1).bitcast(U32) for n in range(2)]
        G1W = at(35152, 12 * CH)
        RX1 = at(35260, CH * 4)
        W2 = G1W[:, 0:CH]
        GS = IDF[:, 2 * NE:3 * NE]

        @block.sync
        def _(sp):
            xv = I["xT"].rearrange("(k p) n -> p k n", p=P)
            wv = I["w_in"].rearrange("(k p) n -> p k n", p=P)
            for k in range(KT):
                sp.dma_start(XT[:, k, :], xv[:, k, :]).then_inc(s_xk[k], 16)
                sp.dma_start(WR[0][:, k, :], wv[:, k, 0:512]).then_inc(s_xk[k], 16)
                if k == 1:
                    sp.dma_start(CS[:, :], I["c_small"]).then_inc(s_const, 16)
            sp.dma_start(WR[1], wv[:, :, 512:1024]).then_inc(s_w[1], 16)
            sp.dma_start(WR[2], wv[:, :, 1024:1536]).then_inc(s_w[2], 16)
            sp.dma_start(MT, I["memT"].rearrange("(k p) n -> p k n", p=P)).then_inc(s_mem, 16)
            sp.dma_start(SBIAS, I["c_sample"]).then_inc(s_bias, 16)
            sp.dma_start(USF[:, :, 0:PB], I["stateT"]).then_inc(s_state, 16)
            sp.dma_start(WPL2[:, :, :], I["w_pool"].rearrange("(m h) c e -> (h c) m e", h=2)).then_inc(s_state, 16)
            sp.dma_start(PSC, I["pool_scale"]).then_inc(s_state, 16)
            copies = [(t, b, r) for t in "kv" for b in range(DB) for r in range(2)]
            half = (WB - DT) // 2
            for n, (t, b, r) in enumerate(copies):
                if n == 5:
                    proj_done(sp, last_of[0])
                    sp.dma_start(WR[0], wv[:, :, 1536:2048]).then_inc(s_w[3], 16)
                if n == 14:
                    proj_done(sp, last_of[1])
                    sp.dma_start(WR[1], I["w_mem_kv"].rearrange("(k p) n -> p k n", p=P)).then_inc(s_w[4], 16)
                if n >= 2:
                    sp.wait_ge(s_copy[n % 2], 16 * (n // 2))
                sp.dma_start(O["win_" + t + "_s"][b, r * half:(r + 1) * half, :],
                             I["cache_win_" + t][b, DT + r * half:DT + (r + 1) * half, :]).then_inc(s_copy[n % 2], 16)
                if n == 26:
                    load_table(sp, 0)
            load_table(sp, 1)
            for n, e in enumerate(ring_user):
                if n == 0:
                    proj_done(sp, n_x - 1)
                if n == 2:
                    load_table(sp, 2)
                if n == 7:
                    load_table(sp, 3)
                if n >= 2:
                    sp.wait_ge(s_xp, xnum[ring_user[n - 2]] + 1)
                dst, srcs = ring_load(n, e)
                for d, s in zip(dst, srcs):
                    sp.dma_start(d, s).then_inc(s_ring[n % 2], 16)
                if n == 1:
                    proj_done(sp, NPROJ - 1)
                    sp.dma_start(O["kT"].rearrange("(m p) n -> p m n", p=P), KTT[:, :, 0:SEQ]).then_inc(s_store, 16)
                    sp.dma_start(O["v"].rearrange("(c p) n -> p c n", p=P), V[:, 0:CH - 1, :]).then_inc(s_store, 16)
                    sp.dma_start(O["kmT"].rearrange("(m p) n -> p m n", p=P), KM).then_inc(s_store, 16)
                    sp.dma_start(O["vm"].rearrange("(m p) n -> p m n", p=P), VM).then_inc(s_store, 16)
                    sp.dma_start(O["uT"].rearrange("(m p) n -> p m n", p=P), UP[:, :, UH + SEQ - PB:UH + SEQ]).then_inc(s_store, 16)
                    sp.wait_ge(s_state, 48)
                    sp.dma_start(O["poolT_s"], USF[:, :, DT:DT + PB]).then_inc(s_store, 16)
                    for b in range(DB):
                        sp.dma_start(O["win_v_s"][b, WB - DT:WB, :], V[DT * b:DT * b + DT, CH - 1, :]).then_inc(s_store, 16)
                    sp.wait_ge(s_xe, xnum[("knew",)] + 1)
                    for b in range(DB):
                        sp.dma_start(O["win_k_s"][b, WB - DT:WB, :], KN[DT * b:DT * b + DT, :]).then_inc(s_store, 16)
            sp.wait_ge(s_xp, len(xlist))
            wo = I["w_o"].rearrange("(k p) n -> p k n", p=P)
            sp.dma_start(WO[:, :, 0:512], wo[:, :, 0:512]).then_inc(s_wo, 16)
            sp.dma_start(WO[:, :, 512:1024], wo[:, :, 512:1024]).then_inc(s_wo, 16)
            item_done(sp, NI - 1)
            item_done(sp, NI - 2)
            sp.wait_ge(s_OB, NU)
            sp.wait_ge(s_store, 16 * (6 + 2 * DB))
            for v, n in (("ln1_g", 0), ("ln1_b", 1)):
                sp.dma_start(GB[:, n, :], I[v].unsqueeze(0).broadcast_to([P, D])).then_inc(s_gb, 16)
            sp.dma_start(WRT, I["w_r"].rearrange("(k p) e -> p k e", p=P)).then_inc(s_gb, 16)
            sp.dma_start(RT[:, 0:36], I["b_r"].unsqueeze(0).broadcast_to([P, 36])).then_inc(s_gb, 16)

            def store_h1(c):
                sp.wait_ge(s_h1, c + 1)
                sp.dma_start(h1_d[c * P:c * P + rows(c), :], H1[0:rows(c), c, :]).then_inc(s_h1d, 16)

            for c in range(CH):
                if c >= 2:
                    sp.wait_ge(s_r, c - 1)
                sp.dma_start(XR[c % 2][0:rows(c), :], I["x"][c * P:c * P + rows(c), :]).then_inc(s_x[c % 2], 16)
                if c == 3:
                    load_expert(sp, 0, 0)
                if c == 5:
                    load_expert(sp, 1, 1)
                if c >= 3:
                    store_h1(c - 3)
            for c in range(CH - 3, CH):
                store_h1(c)
            sp.wait_ge(s_mix, CH)
            load_expert(sp, 2, 2)
            load_expert(sp, 3, 3)
            with sp.Fori(1, NE // 4) as i:
                for j in range(4):
                    sp.wait_ge(s_gu, i * 4 + (j - 3))
                    load_gu(sp, i * 4 + j, j)
                    sp.wait_ge(s_y, i * 4 + (j - 3))
                    load_dn(sp, i * 4 + j, j)
            with overflow(sp):
                sp.wait_ge(s_y, NE)
                sp.wait_ge(o_eb, 1)
                with sp.Fori(0, BLOCKS) as b:
                    e = sp.value_load(EB[0:1, bass.ds(b, 1)], min_val=0, max_val=NE - 1)
                    sp.wait_ge(o_free, b + 1)
                    for w, d in (("w_gate", WG), ("w_up", WU), ("w_down", WD)):
                        sp.dma_start(d[0], I[w][bass.ds(e, 1)].rearrange("o (k p) n -> p (o k) n", p=P)).then_inc(o_w, 16)
                sp.wait_ge(o_s, 16 * BLOCKS)
            with sp.Else():
                sp.nop()
            for v, n in (("ln2_g", 0), ("ln2_b", 1)):
                sp.dma_start(GB[:, n, :], I[v].unsqueeze(0).broadcast_to([P, D])).then_inc(s_gb2, 16)
            sp.wait_ge(s_ys[0], 16 * (NE // 2))
            sp.wait_ge(s_ys[1], 16 * (NE // 2))
            pr = pair_d.rearrange("(k n) d -> n k d", k=2)

            def store_y(c):
                sp.wait_ge(s_fo, c + 1)
                sp.dma_start(O["y"][c * P:c * P + rows(c), :], RF[c % 3][0:rows(c), :]).then_inc(s_out[c % 3], 16)

            for c in range(CH):
                if c == 0:
                    sp.wait_ge(s_y, NE)
                if c >= 3:
                    sp.wait_ge(s_f, c - 2)
                sp.dma_start(YP[c % 3][0:rows(c), :, :], pr[c * P:c * P + rows(c), :, :]).then_inc(s_yp[c % 3], 16)
                if c >= 3:
                    store_y(c - 3)
            for c in range(CH - 3, CH):
                store_y(c)
            for i in range(3):
                sp.wait_ge(s_out[i], 16 * (CH // 3))
            for i in range(2):
                sp.wait_ge(s_copy[i], 16 * DB * 2)

        @block.tensor
        def _(pe):
            def mm(out, lhsT, rhs, start, stop):
                return nc.tensor.matmul(out, lhsT, rhs, start=start, stop=stop, skip_group_check=True)

            for k in range(KT):
                pe.wait_ge(s_xk[k], 32)
                for n in range(8):
                    _, lt, rh, _, _, m, w = proj[n]
                    last = mm(bank(n)[0:m, 0:w], lt(k), rh(k), k == 0, k == KT - 1)
                    if k == KT - 1:
                        last.then_inc(s_proj, 1)
            for n in range(8, NPROJ):
                _, lt, rh, g, _, m, w = proj[n]
                if g:
                    pe.wait_ge(s_w[g], 16)
                if g == 4:
                    pe.wait_ge(s_mem, 16)
                proj_done(pe, n - 8)
                for k in range(KT):
                    last = mm(bank(n % 8)[0:m, 0:w], lt(k), rh(k), k == 0, k == KT - 1)
                last.then_inc(s_proj, 1)
            proj_done(pe, NPROJ - 1)
            pe.wait_ge(s_const, 16)

            def scores(u):
                kind, hp, i = units[u]
                if u and units[u - 1][0] == "w":
                    pe.wait_ge(s_min, 2 * u)
                if kind == "c" and units[u - 2][0] == "c":
                    pe.wait_ge(s_exp, 2 * (u - 1))
                width = P * (i + 1) if kind == "w" else N_MEM
                for a in range(0, width, 512):
                    w = min(512, width - a)
                    for s in range(2):
                        h = slice(64 * s, 64 * s + 64)
                        q = (QT if kind == "w" else QC)[h, hp, i * P:i * P + P]
                        k = (KTT if kind == "w" else KM)[h, hp, a:a + w]
                        o = score_at(u, s) + a
                        last = mm(PS[:, o:o + w], q, k, True, True)
                        if a + w == width:
                            last.then_inc(s_S, 1)

            def transposes(n):
                u, blocks, _ = items[n]
                if n >= 2:
                    item_done(pe, n - 2)
                if blocks[0] == 0:
                    pe.wait_ge(s_exp, 2 * u + 2)
                b = bank(4 + n % 2)
                for j, kb in enumerate(blocks):
                    for s in range(2):
                        last = nc.tensor.transpose(b[:, (2 * j + s) * P:(2 * j + s) * P + P], SP[(u % 3) * 2 + s][:, kb * P:kb * P + P], ident)
                last.then_inc(s_T, 1)

            def values(n):
                u, blocks, nb = items[n]
                kind, hp, i = units[u]
                item_done(pe, n)
                if blocks[0] == 0:
                    if u >= 2:
                        pe.wait_ge(s_OB, u - 1)
                    pe.wait_ge(s_xe, x_before[u])
                b = bank(6 + u % 2)
                for j, kb in enumerate(blocks):
                    for s in range(2):
                        c = (2 * hp + s) * HD
                        v = (V if kind == "w" else VM)[:, kb, c:c + HD]
                        last = mm(b[64 * s:64 * s + 64, 0:P], v, PTB[n % 4][:, 2 * j + s, :], kb == 0, kb == nb - 1)
                last.then_inc(s_PV, 1)
                if blocks[-1] == nb - 1:
                    pe.wait_ge(s_dg, u + 1)
                    for s in range(2):
                        last = mm(b[64 * s:64 * s + 64, P:2 * P], ones[:, 0:HD], DG[u % 2][:, s, :], True, True)
                    last.then_inc(s_O, 1)

            def x_step(e, u):
                x = xnum[e]
                if x:
                    pe.wait_ge(s_xe, x)
                if u >= 1:
                    pe.wait_ge(s_OB, u)
                bx = bank(xbank[e])
                if e[0] == "knew":
                    for m in range(4):
                        last = nc.tensor.transpose(bx[0:SMP, m * P:m * P + P], KTT[:, m, SEQ:TOK], ident)
                elif e[0] == "pool":
                    pe.wait_ge(s_pool, 1 if e[1] < 4 else 2)
                    if e[1] < 4:
                        t, hf = e[1] // 2, e[1] % 2
                        for g in range(2):
                            r = slice(64 * g, 64 * g + 64)
                            last = mm(bx[r, 0:512], WPL2[r, t, :], PA[r, t, UH + 512 * hf:UH + 512 * hf + 512], True, True)
                    else:
                        for t in range(2):
                            for g in range(2):
                                r = slice(64 * g, 64 * g + 64)
                                last = mm(bx[r, t * SMP:t * SMP + SMP], WPL2[r, t, :], SA[r, t, :, PB:PB + DT], True, True)
                elif e[0] == "ss":
                    g, kc = e[1] // 4, e[1] % 4
                    ring_ready(pe, e)
                    if e[1] == 0:
                        pe.wait_ge(s_srd, 1)
                    kt = at(RING[ring_no[e] % 2], 4, 4, KC)
                    for hp in range(4):
                        for b in range(4):
                            last = mm(bx[32 * b:32 * b + 32, 0:KC], QBD[:, g, hp, b, :], kt[:, hp, b, :], hp == 0, hp == 3)
                    if kc == 3:
                        for hp in range(4):
                            for b in range(4):
                                last = mm(bx[32 * b:32 * b + 32, KC:KC + SMP], QBD[:, g, hp, b, :], KTT[:, hp, SEQ:TOK], hp == 0, hp == 3)
                elif e[0] == "st":
                    _, g, hf = e
                    pe.wait_ge(s_srd, 2 + g)
                    for j in range(4):
                        t = 4 * hf + j
                        m = P if t < NVT else SMP
                        last = nc.tensor.transpose(bx[0:m, j * P:j * P + P], SS[:, g, t * P:t * P + m], ident)
                elif e[0] == "pv":
                    _, g, p = e
                    ring_ready(pe, e)
                    vt = at(RING[ring_no[e] % 2], 2, 4, 512)
                    for t in pv_tiles(p):
                        for b in range(4):
                            last = mm(bx[32 * b:32 * b + 32, :], PTS[:, g, t, 32 * b:32 * b + 32], vt[:, t % 2, b, :],
                                      t == 2 * p, p < 3 and t == 2 * p + 1)
                    if p == 3:
                        for b in range(4):
                            last = mm(bx[32 * b:32 * b + 32, :], PTS[0:SMP, g, NVT, 32 * b:32 * b + 32], V[0:SMP, CH - 1, :], False, True)
                elif e[0] == "ot":
                    for hp in range(4):
                        last = nc.tensor.transpose(bx[:, hp * P:hp * P + P], OA[:, hp * P:hp * P + P], ident)
                elif e[0] == "ms":
                    ring_ready(pe, e)
                    km = at(RING[ring_no[e] % 2], 2, DB, N_MEM)
                    for j in range(4):
                        for n in range(4):
                            hp, b = n // 2, 2 * j + n % 2
                            last = mm(bx[32 * j:32 * j + 32, 0:N_MEM], QBM[:, hp, b, :], km[:, hp, b, :], n == 0, n == 3)
                elif e[0] == "mt":
                    pe.wait_ge(s_srd, 4)
                    for t in range(2):
                        last = nc.tensor.transpose(bx[:, t * P:t * P + P], PMS[:, t * P:t * P + P], ident)
                else:
                    ring_ready(pe, e)
                    vm = at(RING[ring_no[e] % 2], DB, 2, D_C)
                    for b in range(DB):
                        for hp in range(2):
                            for t in range(2):
                                c = (2 * b + hp) * 8
                                last = mm(bx[:, c:c + 8], vm[:, b, t, hp * P:hp * P + P], PTM[:, t, 16 * b + 8 * hp:16 * b + 8 * hp + 8], t == 0, t == 1)
                last.then_inc(s_xp, 1)

            for e in extra[-1]:
                x_step(e, -1)
            scores(0)
            scores(1)
            for u in range(NU):
                if u + 2 < NU:
                    scores(u + 2)
                for n in unit_items[u]:
                    transposes(n)
                    if n:
                        values(n - 1)
                for e in extra[u]:
                    x_step(e, u)
            values(NI - 1)
            item_done(pe, NI - 1)
            item_done(pe, NI - 2)
            pe.wait_ge(s_xe, len(xlist))
            pe.wait_ge(s_wo, 32)
            pe.wait_ge(s_exp, 2 * NU)

            def mix(c):
                if c >= 2:
                    pe.wait_ge(s_r, c - 1)
                m = rows(c)
                for n in range(2):
                    for k in range(KT):
                        last = mm(PS[0:m, 1024 * (c % 2) + 512 * n:1024 * (c % 2) + 512 * n + 512],
                                  CAT[:, k, c * P:c * P + m], WO[:, k, 512 * n:512 * n + 512], k == 0, k == KT - 1)
                last.then_inc(s_mix, 1)

            def h1_transposes(c):
                pe.wait_ge(s_h1, c + 1)
                m = rows(c)
                for hf in range(2):
                    if c >= 1:
                        pe.wait_ge(s_hte, 2 * (c - 1) + hf + 1)
                    for j in range(4):
                        k = 4 * hf + j
                        last = nc.tensor.transpose(bank(4 + hf)[:, j * P:j * P + m], H1[0:m, c, k * P:k * P + P], ident[0:m, 0:m])
                    last.then_inc(s_ht, 1)

            def router(c):
                m = rows(c)
                if c == 0:
                    pe.wait_ge(s_gb, 64)
                pe.wait_ge(s_hte, 2 * c + 2)
                for k in range(KT):
                    last = mm(bank(6)[0:m, 36 * c:36 * c + 36], H1T[c % 2][:, k, 0:m], WRT[:, k, :], k == 0, k == KT - 1)
                last.then_inc(s_rt, 1)

            for c in range(CH):
                mix(c)
                if c >= 1:
                    h1_transposes(c - 1)
                if c >= 2:
                    router(c - 2)
            h1_transposes(CH - 1)
            router(CH - 2)
            router(CH - 1)
            pe.wait_ge(s_M, 1)
            mm(bank(0)[:, 0:CH * NE], tri, RM.rearrange("p c e -> p (c e)"), True, False)
            mm(bank(0)[:, 0:CH * NE], ones, RMP.rearrange("p c e -> p (c e)"), False, True)
            mm(bank(0)[:, CH * NE:CH * NE + NE], ones, CNT, True, True).then_inc(s_rank, 1)
            for n in range(2 * CH):
                c, k = n // 2, n % 2
                pe.wait_ge(s_oh, n + 1)
                last = mm(bank(1)[:, 0:3 * NE], OH[n % 4], RV[:, k, c, :], n == 0, n == 2 * CH - 1)
                last.then_inc(s_ohx, 1)
            def gather_transposes(e, sl):
                for hf in range(2):
                    for j in range(4):
                        k = 4 * hf + j
                        last = nc.tensor.transpose(bank(hf)[:, j * P:j * P + P], XG[sl][:, k * P:k * P + P], ident)
                    last.then_inc(s_tp, 1)

            def gate_up(j):
                b = bank(2 + j % 2)
                for n in range(4):
                    w = (WG, WU)[n // 2][j]
                    for k in range(KT):
                        last = mm(b[:, n * P:n * P + P], w[:, k, (n % 2) * P:(n % 2) * P + P], XGT[j % 2][:, k, :], k == 0, k == KT - 1)
                last.then_inc(s_gu, 1)

            def down(j):
                for n in range(2):
                    for f in range(2):
                        last = mm(PS[:, 2048 + 1024 * (j % 2) + 512 * n:2048 + 1024 * (j % 2) + 512 * n + 512],
                                  AT[j % 2][:, f, :], WD[j][:, f, 512 * n:512 * n + 512], f == 0, f == 1)
                last.then_inc(s_y, 1)

            pe.wait_ge(s_idx, 1)
            pe.wait_ge(s_gx[0], 16)
            gather_transposes(0, 0)

            def expert(i, j, first, last):
                e = i * 4 + j
                pe.wait_ge(s_g[j], i * 32 + 32)
                pe.wait_ge(s_xgt, e * 2 + 2)
                if not first:
                    pe.wait_ge(s_at, e - 1)
                gate_up(j)
                if not last:
                    pe.wait_ge(s_gx[(j + 1) % 2], (e + 1 - (j + 1) % 2) * 8 + 16)
                    gather_transposes(e + 1, (j + 1) % 2)
                pe.wait_ge(s_at, e + 1)
                pe.wait_ge(s_wd[j], i * 16 + 16)
                if not first:
                    pe.wait_ge(s_ya, e - 1)
                    pe.wait_ge(s_yd, e - 1)
                down(j)

            for j in range(4):
                expert(0, j, j < 2, False)
            with pe.Fori(1, NE // 4 - 1) as i:
                for j in range(4):
                    expert(i, j, False, False)
            for j in range(4):
                expert(NE // 4 - 1, j, False, j == 3)
            with overflow(pe):
                pe.wait_ge(s_yd, NE)
                pe.wait_ge(s_ya, NE)
                with pe.Fori(0, BLOCKS) as b:
                    for n in range(2 * CH):
                        pe.wait_ge(o_oh, b * 2 * CH + (n + 1))
                        mm(bank(1)[:, 0:4], OH[n % 4], OVAL[:, n % 2, n // 2, :], n == 0, n == 2 * CH - 1).then_inc(o_ohx, 1)
                    pe.wait_ge(o_g, b * 16 + 16)
                    for hf in range(2):
                        for j in range(4):
                            k = 4 * hf + j
                            last = nc.tensor.transpose(bank(hf)[:, j * P:j * P + P], XG[0][:, k * P:k * P + P], ident)
                        last.then_inc(o_tp, 1)
                    pe.wait_ge(o_w, b * 48 + 48)
                    pe.wait_ge(o_xgt, b * 2 + 2)
                    for n in range(4):
                        w = (WG, WU)[n // 2][0]
                        for k in range(KT):
                            last = mm(bank(2)[:, n * P:n * P + P], w[:, k, (n % 2) * P:(n % 2) * P + P], XGT[0][:, k, :], k == 0, k == KT - 1)
                    last.then_inc(o_gu, 1)
                    pe.wait_ge(o_at, b + 1)
                    for n in range(2):
                        for f in range(2):
                            last = mm(bank(4 + n), AT[0][:, f, :], WD[0][:, f, 512 * n:512 * n + 512], f == 0, f == 1)
                    last.then_inc(o_y, 1)
            with pe.Else():
                pe.nop()

        @block.scalar
        def _(act):
            for n in range(1, NPROJ, 2):
                d, _, _, _, scale, m, w = proj[n]
                act.wait_ge(s_proj, n + 1)
                src = bank(n % 8)[0:m, 0:w]
                if len(d.shape) == 3:
                    src = src.rearrange("p (b t) -> p b t", t=DT)
                nc.scalar.activation(d, src, ACT.Copy, scale=scale).then_inc(s_pe_a, 1)

            def evac(n):
                if n % 2:
                    act.wait_ge(s_T, n + 1)
                    transposed_out(act, nc.scalar.copy, n).then_inc(s_Ta, 1)

            def exps(u, s):
                kind, hp, i = units[u]
                w = P * (i + 1) if kind == "w" else N_MEM
                x = 2 * u + s
                act.wait_ge(s_min, x + 1)
                sp = SP[(u % 3) * 2 + s]
                if kind == "c":
                    act.wait_ge(s_T, unit_items[u - 3][-1] + 1)
                src = sp[:, 0:w] if kind == "w" else PS[:, score_at(u, s):score_at(u, s) + w]
                nc.scalar.activation(sp[:, 0:w], src, ACT.Exp, scale=-1.0, bias=MN[:, x:x + 1],
                                     accum_out=DEN[:, x:x + 1]).then_inc(s_exp, 1)

            def x_act(e):
                if e in (("ss", 3), ("ss", 7)):
                    g = e[1] // 4
                    act.wait_ge(s_smin, g + 1)
                    nc.scalar.activation(SS[:, g, 0:NK + SMP], SS[:, g, 0:NK + SMP], ACT.Exp, scale=-1.0,
                                         bias=SMN[:, g:g + 1], accum_out=SDEN[:, g:g + 1]).then_inc(s_sexp, 1)
                if e == ("ms",):
                    act.wait_ge(s_smin, 3)
                    nc.scalar.activation(PMS, bank(xbank[e])[:, 0:N_MEM], ACT.Exp, scale=-1.0,
                                         bias=SMN[:, 2:3], accum_out=SDEN[:, 2:3]).then_inc(s_sexp, 1)

            def spread(u):
                act.wait_ge(s_O, u + 1)
                if u:
                    act.wait_ge(s_OB, u)
                nc.scalar.copy(INV, bank(6 + u % 2)[:, P:2 * P]).then_inc(s_inv, 1)

            exps(0, 0)
            exps(0, 1)
            for u in range(NU):
                mine = unit_items[u]
                for j, n in enumerate(mine):
                    evac(n)
                    for s in range(2):
                        if u + 1 < NU and j == min(2 * s, len(mine) - 1):
                            exps(u + 1, s)
                    if j == min(1, len(mine) - 1) and u:
                        spread(u - 1)
                for e in extra[u]:
                    x_act(e)
            spread(NU - 1)
            def h1t_copy(c):
                m = rows(c)
                for hf in range(2):
                    act.wait_ge(s_ht, 2 * c + hf + 1)
                    if c >= 2:
                        act.wait_ge(s_rt, c - 1)
                    nc.scalar.copy(H1T[c % 2][:, 4 * hf:4 * hf + 4, 0:m],
                                   bank(4 + hf).rearrange("p (j n) -> p j n", j=4)[:, :, 0:m]).then_inc(s_hte, 1)

            for c in range(CH):
                m = rows(c)
                act.wait_ge(s_r, c + 1)
                nc.scalar.activation(MV[0:m, c, 2:3], MV[0:m, c, 1:2], ACT.Sqrt, bias=EPSC[0:m, :]).then_inc(s_std, 1)
                act.wait_ge(s_nrm, c + 1)
                if c == 0:
                    act.wait_ge(s_store, 16 * (6 + 2 * DB))
                nc.scalar.activation(H1[0:m, c, :], RB[c % 2][0:m, :], ACT.Identity, scale=MV[0:m, c, 2:3],
                                     bias=MV[0:m, c, 3:4]).then_inc(s_z, 1)
                if c >= 1:
                    h1t_copy(c - 1)
            h1t_copy(CH - 1)
            act.wait_ge(s_rx, 1)
            nc.scalar.activation(RX1, RX1, ACT.Exp).then_inc(s_ra, 1)
            act.wait_ge(s_rx, 2)
            nc.scalar.activation(W2, W2, ACT.Exp).then_inc(s_ra, 1)

            def expert(i, j, first):
                e = i * 4 + j
                for hf in range(2):
                    act.wait_ge(s_tp, e * 2 + (hf + 1))
                    if not first:
                        act.wait_ge(s_gu, e - 1)
                    nc.scalar.copy(XGT[j % 2][:, 4 * hf:4 * hf + 4, :],
                                   bank(hf).rearrange("p (j n) -> p j n", j=4)).then_inc(s_xgt, 1)

            def silu(i, j, first):
                e = i * 4 + j
                act.wait_ge(s_gu, e + 1)
                if not first:
                    act.wait_ge(s_at, e - 1)
                nc.scalar.activation(SIL[j % 2].rearrange("p a n -> p (a n)"), bank(2 + j % 2)[:, 0:256], ACT.Silu).then_inc(s_sil, 1)

            def y_half(i, j, first):
                e = i * 4 + j
                act.wait_ge(s_y, e + 1)
                if not first:
                    act.wait_ge(s_ys[j % 2], (e - j % 2) * 8)
                nc.scalar.activation(YS[j % 2][:, 0:512], PS[:, 2048 + 1024 * (j % 2):2048 + 1024 * (j % 2) + 512], ACT.Copy,
                                     scale=GS[:, bass.ds(e, 1)]).then_inc(s_ya, 1)

            act.wait_ge(s_idx, 1)
            expert(0, 0, True)
            def turn(i, j, first, last):
                silu(i, j, first)
                if not last:
                    expert(i + (j + 1) // 4, (j + 1) % 4, first and j == 0)
                y_half(i, j, first)
            for j in range(4):
                turn(0, j, j < 2, False)
            with act.Fori(1, NE // 4 - 1) as i:
                for j in range(4):
                    turn(i, j, False, False)
            for j in range(4):
                turn(NE // 4 - 1, j, False, j == 3)
            with overflow(act):
                with act.Fori(0, BLOCKS) as b:
                    for hf in range(2):
                        act.wait_ge(o_tp, b * 2 + (hf + 1))
                        nc.scalar.copy(XGT[0][:, 4 * hf:4 * hf + 4, :], bank(hf).rearrange("p (j n) -> p j n", j=4)).then_inc(o_xgt, 1)
                    act.wait_ge(o_gu, b + 1)
                    nc.scalar.activation(SIL[0].rearrange("p a n -> p (a n)"), bank(2)[:, 0:256], ACT.Silu).then_inc(o_sil, 1)
                    act.wait_ge(o_y, b + 1)
                    nc.scalar.activation(YS[0][:, 0:512], bank(4), ACT.Copy, scale=OLF[:, 2:3]).then_inc(o_ya, 1)
            with act.Else():
                act.nop()
            for c in range(CH):
                m = rows(c)
                act.wait_ge(s_f, c + 1)
                nc.scalar.activation(MV2[0:m, c, 2:3], MV2[0:m, c, 1:2], ACT.Sqrt, bias=EPSC[0:m, :]).then_inc(s_std2, 1)
                act.wait_ge(s_nr2, c + 1)
                nc.scalar.activation(RF[c % 3][0:m, :], RF[c % 3][0:m, :], ACT.Identity, scale=MV2[0:m, c, 2:3],
                                     bias=MV2[0:m, c, 3:4]).then_inc(s_fz, 1)

        @block.vector
        def _(dve):
            step = Steps(dve, s_dve)
            V_ = nc.vector
            step(V_.memset(EPSC, EPS))
            step(V_.memset(UP[:, :, 0:UH], 0.0))
            for n in range(0, NPROJ, 2):
                d, _, _, _, scale, m, w = proj[n]
                dve.wait_ge(s_proj, n + 1)
                src = bank(n % 8)[0:m, 0:w]
                if len(d.shape) == 3:
                    src = src.rearrange("p (b t) -> p b t", t=DT)
                V_.tensor_scalar(d, src, scale, None, ALU.mult).then_inc(s_pe_d, 1)
            proj_done(dve, NPROJ - 1)

            def sample_queries():
                step(V_.memset(at(47760, 1536), 0.0))
                for g in range(2):
                    for hp in range(4):
                        for s in range(2):
                            r = slice(64 * s, 64 * s + 64)
                            last = V_.tensor_copy(QBD[r, g, hp, :, (2 * hp + s) * DT:(2 * hp + s) * DT + DT],
                                                  QT[r, hp, SEQ + 16 * g:SEQ + 16 * g + 16].rearrange("p (b t) -> p b t", t=DT))
                for hp in range(2):
                    for s in range(2):
                        for o in range(2):
                            r = slice(64 * s, 64 * s + 64)
                            c = o * 16 + (2 * hp + s) * DT
                            last = V_.tensor_copy(QBM[r, hp, :, c:c + DT].rearrange("p (b o) t -> p b o t", o=2)[:, :, o, :],
                                                  QC[r, hp, SEQ:TOK].rearrange("p (b o t) -> p b o t", o=2, t=DT)[:, :, o, :])
                last.then_inc(s_srd, 1)

            def mins(u, s):
                kind, hp, i = units[u]
                x = 2 * u + s
                dve.wait_ge(s_S, x + 1)
                ps = PS[:, score_at(u, s):]
                if kind == "w":
                    if i == 0:
                        dve.wait_ge(s_tb[hp % 2], 32 * (hp // 2 + 1))
                    if u >= 3 and s == 0:
                        dve.wait_ge(s_T, unit_items[u - 3][-1] + 1)
                    w = P * (i + 1)
                    V_.tensor_tensor_reduce(SP[(u % 3) * 2 + s][:, 0:w], ps[:, 0:w], TB[hp % 2][s][:, SEQ - w:SEQ],
                                            1.0, 3e38, ALU.add, ALU.min, MN[:, x:x + 1]).then_inc(s_min, 1)
                else:
                    V_.tensor_reduce(MN[:, x:x + 1], ps[:, 0:N_MEM], AX.X, ALU.min).then_inc(s_min, 1)

            def evac(n):
                if n % 2 == 0:
                    dve.wait_ge(s_T, n + 1)
                    transposed_out(dve, V_.tensor_copy, n).then_inc(s_Td, 1)

            def inverse(u):
                dve.wait_ge(s_exp, 2 * u + 2)
                V_.reciprocal(RD[:, 2 * u:2 * u + 2], DEN[:, 2 * u:2 * u + 2]).then_inc(s_rd, 1)

            def o_out(u):
                kind, hp, i = units[u]
                dve.wait_ge(s_inv, u + 1)
                if (kind, hp, i) in (("w", 2, 0), ("c", 0, 0)):
                    dve.wait_ge(s_xp, xnum[("pool", 4) if kind == "w" else ("pv", 1, 3)] + 1)
                b = bank(6 + u % 2)
                V_.tensor_tensor(CAT[:, hp + (0 if kind == "w" else 6), i * P:i * P + P], b[:, 0:P], INV,
                                 ALU.mult).then_inc(s_OB, 1)

            def normalise(g, w, p):
                dve.wait_ge(s_sexp, g + 1)
                step(V_.reciprocal(SRD[:, g:g + 1], SDEN[:, g:g + 1]))
                V_.tensor_scalar(p[:, 0:w], p[:, 0:w], SRD[:, g:g + 1], None, ALU.mult).then_inc(s_srd, 1)

            def x_out(e):
                x = xnum[e]
                dve.wait_ge(s_xp, x + 1)
                bx = bank(xbank[e])
                if e[0] == "knew":
                    V_.tensor_copy(KN[0:SMP, :], bx[0:SMP, :]).then_inc(s_xe, 1)
                elif e[0] == "pool":
                    if e[1] < 4:
                        t, hf = e[1] // 2, e[1] % 2
                        V_.tensor_scalar(CAT[:, 4 + t, 512 * hf:512 * hf + 512], bx, PSC[:, t:t + 1], None, ALU.mult).then_inc(s_xe, 1)
                    else:
                        step(V_.tensor_scalar(CAT[:, 4, SEQ:TOK], bx[:, 0:SMP], PSC[:, 0:1], None, ALU.mult))
                        V_.tensor_scalar(CAT[:, 5, SEQ:TOK], bx[:, SMP:2 * SMP], PSC[:, 1:2], None, ALU.mult).then_inc(s_xe, 1)
                elif e[0] == "ss":
                    g, kc = e[1] // 4, e[1] % 4
                    if e[1] == 0:
                        dve.wait_ge(s_bias, 16)
                        dve.wait_ge(s_pool, 2)
                        dve.wait_ge(s_store, 16 * (6 + 2 * DB))
                    if kc < 3:
                        V_.tensor_tensor(SS[:, g, kc * KC:kc * KC + KC], bx[:, 0:KC], SBIAS[:, kc * KC:kc * KC + KC], ALU.add).then_inc(s_xe, 1)
                    else:
                        step(V_.tensor_tensor(SS[:, g, 3 * KC:4 * KC], bx[:, 0:KC], SBIAS[:, 3 * KC:4 * KC], ALU.add))
                        V_.tensor_tensor(SS[:, g, NK:NK + SMP], bx[:, KC:KC + SMP], SBIAS[:, NK + SMP * g:NK + SMP * g + SMP], ALU.add).then_inc(s_xe, 1)
                        dve.wait_ge(s_xe, x + 1)
                        V_.tensor_reduce(SMN[:, g:g + 1], SS[:, g, 0:NK + SMP], AX.X, ALU.min).then_inc(s_smin, 1)
                        pending.append((g, NK + SMP, SS[:, g, :]))
                elif e[0] == "st":
                    _, g, hf = e
                    if hf == 0:
                        V_.tensor_copy(PTS[:, g, 0:4, :].rearrange("p a b -> p (a b)"), bx).then_inc(s_xe, 1)
                    else:
                        step(V_.tensor_copy(PTS[:, g, 4:7, :].rearrange("p a b -> p (a b)"), bx[:, 0:3 * P]))
                        V_.tensor_copy(PTS[0:SMP, g, 7, :], bx[0:SMP, 3 * P:4 * P]).then_inc(s_xe, 1)
                elif e[0] == "pv":
                    if e[2] == 0:
                        V_.tensor_copy(OA, bx).then_inc(s_xe, 1)
                    else:
                        V_.tensor_tensor(OA, OA, bx, ALU.add).then_inc(s_xe, 1)
                elif e[0] == "ot":
                    g = e[1]
                    for hp in range(4):
                        for s in range(2):
                            r = slice(64 * s, 64 * s + 64)
                            last = V_.tensor_copy(CAT[r, hp, SEQ + 16 * g:SEQ + 16 * g + 16].rearrange("p (b t) -> p b t", t=DT),
                                                  bx[r, hp * P:hp * P + P].rearrange("p (b h t) -> p b h t", b=4, t=DT)[:, :, 2 * hp + s, :])
                    last.then_inc(s_xe, 1)
                elif e[0] == "ms":
                    V_.tensor_reduce(SMN[:, 2:3], bx[:, 0:N_MEM], AX.X, ALU.min).then_inc(s_smin, 1)
                    normalise(2, N_MEM, PMS)
                    dve.wait_ge(s_srd, 4)
                    dve.sem_inc(s_xe, 1)
                elif e[0] == "mt":
                    V_.tensor_copy(PTM.rearrange("p a b -> p (a b)"), bx[:, 0:2 * P]).then_inc(s_xe, 1)
                else:
                    o = bx[:, 0:P].rearrange("p (b a c) -> p b a c", b=DB, a=2)
                    for hp in range(2):
                        for s in range(2):
                            last = V_.tensor_copy(CAT[64 * s:64 * s + 64, 6 + hp, SEQ:TOK].rearrange("p (b t) -> p b t", t=DT),
                                                  o[64 * s:64 * s + 64, :, hp, DT * s:DT * s + DT])
                            if hp + s < 2:
                                step(last)
                    last.then_inc(s_xe, 1)

            pending = []
            for e in extra[-1]:
                x_out(e)
            for u in range(2):
                for s in range(2):
                    mins(u, s)
            for u in range(NU):
                for e in pending:
                    normalise(*e)
                pending.clear()
                mine = unit_items[u]
                for j, n in enumerate(mine):
                    evac(n)
                    if j == 0:
                        inverse(u)
                    for s in range(2):
                        if u + 2 < NU and j == min(2 * s, len(mine) - 1):
                            mins(u + 2, s)
                    if j == min(1, len(mine) - 1) and u:
                        o_out(u - 1)
                if u == 3:
                    sample_queries()
                for e in extra[u]:
                    x_out(e)
            o_out(NU - 1)
            for c in range(CH):
                m = rows(c)
                dve.wait_ge(s_mix, c + 1)
                dve.wait_ge(s_x[c % 2], 16 * (c // 2 + 1))
                if c >= 2:
                    dve.wait_ge(s_z, c - 1)
                step(V_.scalar_tensor_tensor(RB[c % 2][0:m, :], XR[c % 2][0:m, :], ALPHA,
                                             PS[0:m, 1024 * (c % 2):1024 * (c % 2) + 1024], ALU.mult, ALU.add))
                for hf in range(2):
                    last = V_.bn_stats(BN[0:m, 0, 6 * hf:6 * hf + 6], RB[c % 2][0:m, 512 * hf:512 * hf + 512])
                step(last)
                V_.bn_aggr(MV[0:m, c, 0:2], BN[0:m, 0, :]).then_inc(s_r, 1)
                dve.wait_ge(s_std, c + 1)
                step(V_.reciprocal(MV[0:m, c, 2:3], MV[0:m, c, 2:3]))
                V_.scalar_tensor_tensor(MV[0:m, c, 3:4], MV[0:m, c, 0:1], -1.0, MV[0:m, c, 2:3], ALU.mult, ALU.mult).then_inc(s_nrm, 1)
                dve.wait_ge(s_nrm, c + 1)
            step(V_.memset(LG, 0.0))
            dve.wait_ge(s_rt, CH)
            step(V_.tensor_copy(LG[:, 0:8, :].rearrange("p c e -> p (c e)"), bank(6)[:, 0:288]))
            step(V_.tensor_copy(LG[0:SMP, 8, :], bank(6)[0:SMP, 288:324]))
            dve.wait_ge(s_gb, 64)
            step(V_.tensor_tensor(LG, LG, RT[:, 0:36].unsqueeze(1).broadcast_to([P, CH, 36]), ALU.add))
            L1 = LG[:, :, 0:NG]
            rx1 = RX1.rearrange("p (c e) -> p c e", c=CH)
            m1, p1, v1, v2, r1, r2 = (G1W[:, CH * n:CH * n + CH] for n in range(1, 7))
            g4 = [at(R0 + 1728, CH, 4), at(R0 + 1764, CH, 4)]

            def wide(x, n):
                return x.unsqueeze(2).broadcast_to([P, CH, n])

            def first_max(out, vals, top, n, scratch):
                down_ = CS[:, 3 * P:3 * P + n].unsqueeze(1).broadcast_to([P, CH, n])
                step(V_.tensor_reduce(top, vals, AX.X, ALU.max))
                step(V_.tensor_tensor(scratch, vals, wide(top, n), ALU.is_equal))
                step(V_.tensor_scalar(out, scratch, -1000.0, 1000.0, ALU.mult, ALU.add))
                step(V_.tensor_tensor(out, out, down_, ALU.add))
                step(V_.tensor_reduce(p1, out, AX.X, ALU.min))
                step(V_.tensor_tensor(out, out, wide(p1, n), ALU.is_equal))

            first_max(g4[0], L1, m1, NG, g4[1])
            step(V_.tensor_tensor(rx1, L1, wide(m1, NG), ALU.subtract))
            dve.sem_inc(s_rx, 1)
            step(V_.tensor_scalar(g4[0], g4[0], 1.0, MASKED, ALU.subtract, ALU.mult))
            step(V_.tensor_tensor(RL.rearrange("p c (g e) -> p c g e", g=NG), LG[:, :, NG:36].rearrange("p c (g e) -> p c g e", g=NG),
                                  g4[0].unsqueeze(3).broadcast_to([P, CH, NG, EPG]), ALU.add))
            first_max(RE[0], RL, v1, NE, RX)
            step(V_.tensor_scalar(RX, RE[0], -2.0 * MASKED, None, ALU.mult))
            step(V_.tensor_tensor(RL, RL, RX, ALU.add))
            first_max(RE[1], RL, v2, NE, RX)
            for k in range(2):
                step(V_.tensor_tensor(RE[k], RE[k], wide(valid, NE), ALU.mult))
            step(V_.tensor_tensor(RM, RE[0], RE[1], ALU.add))
            step(V_.memset(RMP[:, 0, :], 0.0))
            for c in range(1, CH):
                step(V_.tensor_tensor(RMP[:, c, :], RMP[:, c - 1, :], RM[:, c - 1, :], ALU.add))
            step(V_.tensor_tensor(CNT, RMP[:, CH - 1, :], RM[:, CH - 1, :], ALU.add))
            dve.sem_inc(s_M, 1)
            step(V_.tensor_tensor(W2, v2, v1, ALU.subtract))
            dve.sem_inc(s_rx, 1)
            dve.wait_ge(s_ra, 1)
            step(V_.tensor_reduce(p1, rx1, AX.X, ALU.add))
            step(V_.reciprocal(p1, p1))
            dve.wait_ge(s_ra, 2)
            step(V_.tensor_scalar(v1, W2, 1.0, None, ALU.add))
            step(V_.reciprocal(v1, v1))
            step(V_.tensor_tensor(v1, v1, p1, ALU.mult))
            step(V_.tensor_tensor(v2, v1, W2, ALU.mult))
            for k in range(2):
                step(V_.tensor_tensor(RV[:, k, :, 0:NE], RE[k], wide(tok1, NE), ALU.mult))
                step(V_.scalar_tensor_tensor(RV[:, k, :, NE:2 * NE], RE[k], float(k * TOK), RV[:, k, :, 0:NE], ALU.mult, ALU.add))
                step(V_.tensor_tensor(RV[:, k, :, 2 * NE:3 * NE], RE[k], wide((v1, v2)[k], NE), ALU.mult))
            dve.wait_ge(s_rank, 1)
            step(V_.tensor_copy(RANK.rearrange("p c e -> p (c e)"), bank(0)[:, 0:CH * NE]))
            for k in range(2):
                step(V_.tensor_tensor(RX, RE[k], bank(0)[:, 0:CH * NE].rearrange("p (c e) -> p c e", c=CH), ALU.mult))
                step(V_.tensor_reduce((r1, r2)[k], RX, AX.X, ALU.add))
            step(V_.tensor_copy(CNT, bank(0)[:, CH * NE:CH * NE + NE]))
            step(V_.tensor_reduce(NB[:, 0:1], CNT, AX.X, ALU.max))
            step(V_.tensor_scalar(FLAG, NB[:, 0:1], float(CAP), None, ALU.is_gt))
            if CAP < P:
                for x in (r1, r2):
                    step(V_.tensor_scalar(m1, x, float(CAP), 1e6, ALU.is_ge, ALU.mult))
                    step(V_.tensor_tensor(x, x, m1, ALU.add))
            for n in range(2 * CH):
                c, k = n // 2, n % 2
                if n >= 4:
                    dve.wait_ge(s_ohx, n - 3)
                V_.tensor_scalar(OH[n % 4], iota, (r1, r2)[k][:, c:c + 1], None, ALU.is_equal).then_inc(s_oh, 1)
            dve.wait_ge(s_ohx, 2 * CH)
            step(V_.tensor_copy(IDF[:, :], bank(1)[:, 0:3 * NE]))
            step(V_.tensor_scalar(RX[:, 0:2, :].rearrange("p a b -> p (a b)"), IDF[:, 0:2 * NE], 0.0, 1e6, ALU.is_equal, ALU.mult))
            step(V_.scalar_tensor_tensor(IDF[:, 0:2 * NE], IDF[:, 0:2 * NE], -1.0, RX[:, 0:2, :].rearrange("p a b -> p (a b)"), ALU.add, ALU.add))
            step(V_.tensor_copy(IDX[:, 0:2 * NE], IDF[:, 0:2 * NE]))
            for s in range(2):
                step(V_.memset(XG[s], 0.0))
            dve.sem_inc(s_idx, 1)

            def turn(i, j, first):
                e = i * 4 + j
                dve.wait_ge(s_sil, e + 1)
                if not first:
                    dve.wait_ge(s_y, e - 1)
                V_.tensor_tensor(AT[j % 2].rearrange("p a n -> p (a n)"), SIL[j % 2].rearrange("p a n -> p (a n)"),
                                 bank(2 + j % 2)[:, 256:512], ALU.mult).then_inc(s_at, 1)
                dve.wait_ge(s_y, e + 1)
                if not first:
                    dve.wait_ge(s_ys[j % 2], (e - j % 2) * 8)
                V_.tensor_scalar(YS[j % 2][:, 512:1024], PS[:, 2048 + 1024 * (j % 2) + 512:2048 + 1024 * (j % 2) + 1024],
                                 GS[:, bass.ds(e, 1)], None, ALU.mult).then_inc(s_yd, 1)

            for j in range(4):
                turn(0, j, j < 2)
            with dve.Fori(1, NE // 4) as i:
                for j in range(4):
                    turn(i, j, False)
            with overflow(dve):
                dve.wait_ge(s_ys[0], 8 * NE)
                dve.wait_ge(s_ys[1], 8 * NE)
                n_o = [0]

                def ostep(ins):
                    n_o[0] += 1
                    ins.then_inc(o_pos, 1)
                    dve.wait_ge(o_pos, n_o[0])

                ostep(V_.memset(NB, 0.0))
                for j in range(1, -(-TOK // CAP)):
                    ostep(V_.scalar_tensor_tensor(NB, CNT, float(j * CAP), NB, ALU.is_gt, ALU.add))
                ostep(V_.tensor_copy(OPRE[0], NB))
                for j in range(5):
                    a, b = OPRE[j % 2], OPRE[(j + 1) % 2]
                    ostep(V_.tensor_copy(b[:, 0:2 ** j], a[:, 0:2 ** j]))
                    ostep(V_.tensor_tensor(b[:, 2 ** j:NE], a[:, 2 ** j:NE], a[:, 0:NE - 2 ** j], ALU.add))
                ostep(V_.tensor_tensor(OTMP, OPRE[1].unsqueeze(1).broadcast_to([P, BLOCKS, NE]),
                                       iota[:, 0:BLOCKS].unsqueeze(2).broadcast_to([P, BLOCKS, NE]), ALU.is_le))
                ostep(V_.tensor_reduce(RX[:, 0, 0:BLOCKS] if BLOCKS <= NE else RX.rearrange("p c e -> p (c e)")[:, 0:BLOCKS], OTMP, AX.X, ALU.add))
                ostep(V_.tensor_scalar(EB, RX.rearrange("p c e -> p (c e)")[:, 0:BLOCKS], float(NE - 1), None, ALU.min))
                dve.sem_inc(o_eb, 1)
                dve.sem_inc(o_free, 1)
                ostep(V_.tensor_tensor(OPRE[0], OPRE[1], NB, ALU.subtract))
                for k in range(2):
                    ostep(V_.tensor_tensor(RX, RE[k], OPRE[0].unsqueeze(1).broadcast_to([P, CH, NE]), ALU.mult))
                    ostep(V_.tensor_reduce(m1, RX, AX.X, ALU.add))
                    ostep(V_.tensor_tensor(RX, RE[k], RANK, ALU.mult))
                    ostep(V_.tensor_reduce(p1, RX, AX.X, ALU.add))
                    ostep(V_.scalar_tensor_tensor(OPOS[:, k, :], m1, float(CAP), p1, ALU.mult, ALU.add))
                    ostep(V_.tensor_scalar(p1, p1, float(CAP), -1e6, ALU.is_lt, ALU.mult))
                    ostep(V_.tensor_tensor(OPOS[:, k, :], OPOS[:, k, :], p1, ALU.add))
                    ostep(V_.tensor_tensor(OVAL[:, k, :, 0], tok1, valid, ALU.mult))
                    ostep(V_.scalar_tensor_tensor(OVAL[:, k, :, 1], valid, float(k * TOK), OVAL[:, k, :, 0], ALU.mult, ALU.add))
                    ostep(V_.tensor_tensor(OVAL[:, k, :, 2], (v1, v2)[k], valid, ALU.mult))
                    ostep(V_.memset(OVAL[:, k, :, 3], 0.0))
                per_block = 5
                with dve.Fori(0, BLOCKS) as b:
                    def bstep(ins, n):
                        ins.then_inc(o_pos, 1)
                        dve.wait_ge(o_pos, b * per_block + (n_o[0] + n))

                    dve.wait_ge(o_free, b + 1)
                    bstep(V_.tensor_scalar(OPOS, OPOS, float(CAP), None, ALU.subtract), 1)
                    for n in range(2 * CH):
                        if n >= 4:
                            dve.wait_ge(o_ohx, b * 2 * CH + (n - 3))
                        V_.tensor_scalar(OH[n % 4], iota, OPOS[:, n % 2, n // 2:n // 2 + 1], None, ALU.is_equal).then_inc(o_oh, 1)
                    dve.wait_ge(o_ohx, b * 2 * CH + 2 * CH)
                    bstep(V_.tensor_copy(OLF, bank(1)[:, 0:4]), 2)
                    bstep(V_.tensor_scalar(OPRE[0][:, 0:2], OLF[:, 0:2], 0.0, 1e6, ALU.is_equal, ALU.mult), 3)
                    bstep(V_.scalar_tensor_tensor(OPRE[0][:, 0:2], OLF[:, 0:2], -1.0, OPRE[0][:, 0:2], ALU.add, ALU.add), 4)
                    bstep(V_.tensor_copy(OLI, OPRE[0][:, 0:2]), 5)
                    dve.sem_inc(o_idx, 1)
                    dve.wait_ge(o_sil, b + 1)
                    V_.tensor_tensor(AT[0].rearrange("p a n -> p (a n)"), SIL[0].rearrange("p a n -> p (a n)"),
                                     bank(2)[:, 256:512], ALU.mult).then_inc(o_at, 1)
                    dve.wait_ge(o_ya, b + 1)
                    V_.tensor_scalar(YS[0][:, 512:1024], bank(5), OLF[:, 2:3], None, ALU.mult).then_inc(o_yd, 1)
            with dve.Else():
                dve.nop()
            for c in range(CH):
                m = rows(c)
                dve.wait_ge(s_f1, c + 1)
                for hf in range(2):
                    last = V_.bn_stats(BN[0:m, 1, 6 * hf:6 * hf + 6], RF[c % 3][0:m, 512 * hf:512 * hf + 512])
                step(last)
                V_.bn_aggr(MV2[0:m, c, 0:2], BN[0:m, 1, :]).then_inc(s_f, 1)
                dve.wait_ge(s_std2, c + 1)
                step(V_.reciprocal(MV2[0:m, c, 2:3], MV2[0:m, c, 2:3]))
                V_.scalar_tensor_tensor(MV2[0:m, c, 3:4], MV2[0:m, c, 0:1], -1.0, MV2[0:m, c, 2:3], ALU.mult, ALU.mult).then_inc(s_nr2, 1)
                dve.wait_ge(s_nr2, c + 1)
                dve.wait_ge(s_fz, c + 1)
                if c == 0:
                    dve.wait_ge(s_gb2, 32)
                step(V_.tensor_tensor(RF[c % 3][0:m, :], RF[c % 3][0:m, :], GB[0:m, 0, :], ALU.mult))
                V_.tensor_tensor(RF[c % 3][0:m, :], RF[c % 3][0:m, :], GB[0:m, 1, :], ALU.add).then_inc(s_fo, 1)

        @block.gpsimd
        def _(pool):
            step = Steps(pool, s_pl)
            G = nc.gpsimd
            proj_done(pool, n_u - 1)
            pool.wait_ge(s_state, 48)
            pool.wait_ge(s_dve, 2)
            pool.wait_ge(s_const, 16)

            def sums(u, a, b, n, ap):
                step(G.tensor_tensor(ap(a, 0, 1, n), ap(u, 0, 1, n), ap(u, 0, 0, n - 1), ALU.add))
                step(G.tensor_tensor(ap(b, 0, 3, n), ap(a, 0, 3, n), ap(a, 0, 1, n - 2), ALU.add))
                step(G.tensor_tensor(ap(a, 1, 7, n), ap(b, 1, 7, n), ap(b, 1, 3, n - 4), ALU.add))
                step(G.tensor_tensor(ap(b, 1, 15, n), ap(a, 1, 15, n), ap(a, 1, 7, n - 8), ALU.add))

            def prompt_ap(x, t0, lo, hi):
                return x[:, t0:2, lo:hi]

            def sample_ap(x, t0, lo, hi):
                return x[:, t0, :, lo:hi] if t0 else x[:, :, :, lo:hi]

            sums(UP, PA, PBUF, UH + SEQ, prompt_ap)
            for t in range(2):
                for g in range(2):
                    r = slice(64 * g, 64 * g + 64)
                    src = (PA, PBUF)[g]
                    step(G.tensor_tensor(PA[r, t, UH:UH + 16], src[r, t, UH:UH + 16], pool_inv[r, t, 0:16], ALU.mult))
                    step(G.tensor_scalar(PA[r, t, UH + 16:UH + SEQ], src[r, t, UH + 16:UH + SEQ], pool_inv[r, t, 16:17], None, ALU.mult))
            G.tensor_tensor(PA[:, :, UH:UH + SEQ], PA[:, :, UH:UH + SEQ], UP[:, :, UH:UH + SEQ], ALU.subtract).then_inc(s_pool, 1)
            proj_done(pool, n_x - 1)
            sums(US, SA, SBF, PB + DT, sample_ap)
            for t in range(2):
                for g in range(2):
                    r = slice(64 * g, 64 * g + 64)
                    src = (SA, SBF)[g]
                    step(G.tensor_scalar(SA[r, t, :, PB:PB + DT], src[r, t, :, PB:PB + DT], pool_inv[r, t, 16:17], None, ALU.mult))
            G.tensor_tensor(SA[:, :, :, PB:PB + DT], SA[:, :, :, PB:PB + DT], US[:, :, :, PB:PB + DT], ALU.subtract).then_inc(s_pool, 1)
            for u in range(NU):
                pool.wait_ge(s_rd, u + 1)
                if u >= 2:
                    pool.wait_ge(s_O, u - 1)
                for s in range(2):
                    last = G.tensor_scalar(DG[u % 2][:, s, :], ident, RD[:, 2 * u + s:2 * u + s + 1], None, ALU.mult)
                last.then_inc(s_dg, 1)
            for c in range(CH):
                m = rows(c)
                pool.wait_ge(s_z, c + 1)
                if c == 0:
                    pool.wait_ge(s_gb, 64)
                step(G.tensor_tensor(H1[0:m, c, :], H1[0:m, c, :], GB[0:m, 0, :], ALU.mult))
                G.tensor_tensor(H1[0:m, c, :], H1[0:m, c, :], GB[0:m, 1, :], ALU.add).then_inc(s_h1, 1)
            pool.wait_ge(s_idx, 1)
            pool.wait_ge(s_h1d, 16 * CH)

            def await_(sem_, count):
                pool.wait_ge(sem_, count)
                pool.sem_inc(s_past, 1)

            def column(dst, src, count):
                G.tensor_copy(dst, src).then_inc(s_col, 1)
                await_(s_col, count)

            last_token, last_pair = pool.to_reg(TOK - 1), pool.to_reg(NPAIR - 1)

            def gather(e, sl, count):
                column(GI[sl], e, count)
                G.indirect_dma_start(XG[sl], None, h1_d, bass.IndirectOffsetOnAxis(ap=GI[sl], axis=0),
                                     bounds_check=last_token, oob_is_err=False).then_inc(s_gx[sl], 16)

            def scatter(e, sl, count):
                column(SI[sl], e, count)
                G.indirect_dma_start(pair_d, bass.IndirectOffsetOnAxis(ap=SI[sl], axis=0), YS[sl], None,
                                     bounds_check=last_pair, oob_is_err=False).then_inc(s_ys[sl], 16)

            gather(IDX[:, 0:1], 0, 1)
            gather(IDX[:, 1:2], 1, 2)
            for c in range(CH):
                step(G.tensor_scalar(H1[0:rows(c), c, :], H1[0:rows(c), c, :], ALPHA, None, ALU.mult))

            def turn(i, j, last):
                e = i * 4 + j
                to_gather = IDX[:, bass.ds(e + 2, 1)] if last else IDX[:, bass.ds(pool.snap(e + 2), 1)] if not isinstance(i, int) else IDX[:, e + 2:e + 3]
                to_scatter = IDX[:, bass.ds(pool.snap(e + NE), 1)] if not isinstance(i, int) else IDX[:, NE + e:NE + e + 1]
                if not last:
                    pool.wait_ge(s_tp, e * 2 + 2)
                    gather(to_gather, j % 2, e * 2 + 3)
                pool.wait_ge(s_ya, e + 1)
                pool.wait_ge(s_yd, e + 1)
                scatter(to_scatter, j % 2, e * 2 + 4 if not last else NE + e + 1)

            with pool.Fori(0, NE // 4 - 1) as i:
                for j in range(4):
                    turn(i, j, False)
            for j in range(4):
                turn(NE // 4 - 1, j, j >= 2)
            with overflow(pool):
                with pool.Fori(0, BLOCKS) as b:
                    await_(o_idx, b + 1)
                    G.indirect_dma_start(XG[0], None, h1_d, bass.IndirectOffsetOnAxis(ap=OLI[:, 0:1], axis=0),
                                         bounds_check=last_token, oob_is_err=False).then_inc(o_g, 16)
                    await_(o_yd, b + 1)
                    G.indirect_dma_start(pair_d, bass.IndirectOffsetOnAxis(ap=OLI[:, 1:2], axis=0), YS[0], None,
                                         bounds_check=last_pair, oob_is_err=False).then_inc(o_s, 16)
                    pool.wait_ge(o_s, b * 16 + 16)
                    pool.sem_inc(o_free, 1)
            with pool.Else():
                pool.nop()
            pool.wait_ge(s_y, NE)
            for c in range(CH):
                m = rows(c)
                pool.wait_ge(s_yp[c % 3], 16 * (c // 3 + 1))
                if c >= 3:
                    pool.wait_ge(s_out[c % 3], 16 * (c // 3))
                step(G.tensor_tensor(RF[c % 3][0:m, :], YP[c % 3][0:m, 0, :], YP[c % 3][0:m, 1, :], ALU.add))
                G.tensor_tensor(RF[c % 3][0:m, :], RF[c % 3][0:m, :], H1[0:m, c, :], ALU.add).then_inc(s_f1, 1)


_OUT = {"y": (TOK, D), "kT": (D_A, SEQ), "v": (SEQ, D_A), "uT": (D_B, PB), "kmT": (D_C, N_MEM), "vm": (N_MEM, D_C),
        "win_k_s": (DB, WB, D_A), "win_v_s": (DB, WB, D_A), "poolT_s": (P, 2 * DB, PB)}


def laid_out(i):
    a = {n: np.asarray(v) for n, v in i.items()}
    x = np.concatenate([a["x_prompt"].reshape(SEQ, D), a["x_sample"].reshape(SMP, D)])
    wk = a["cache_win_k"][0][:, ROWS].reshape(2, 4, 4, KC, 4, 2, HD)
    wk = wk.transpose(0, 3 - 1, 5, 6, 4, 1, 3).reshape(8, P, 4, 4 * KC)
    mk = a["cache_mem_k"][0].reshape(DB, N_MEM, 2, 2, HD).transpose(3, 4, 2, 0, 1).reshape(P, 2, DB * N_MEM)
    out = {
        "x": x, "xT": x.T, "memT": a["mem_prompt"][0].T, "stateT": a["state_pool"][0].transpose(2, 0, 1).reshape(2, P, DB, PB).transpose(1, 0, 2, 3).reshape(P, 2 * DB, PB),
        "winkT": wk, "memkT": mk,
        "cache_win_k": a["cache_win_k"].reshape(DB, WB, D_A), "cache_win_v": a["cache_win_v"].reshape(DB, WB, D_A),
        "cache_mem_v": a["cache_mem_v"].reshape(DB, N_MEM, D_C),
        "w_in": a["w_in"][0], "w_mem_kv": a["w_mem_kv"][0], "w_pool": a["w_pool"][0], "pool_scale": a["pool_scale"][0].reshape(2, P).T,
        "w_o": a["w_o"][0], "w_r": np.concatenate([a["w_r1"][0], a["w_r2"][0].transpose(1, 0, 2).reshape(D, NE)], axis=1),
        "b_r": np.concatenate([a["b_r1"][0], a["b_r2"][0].reshape(NE)]),
        "w_gate": a["w_gate"].reshape(NE, D, DE), "w_up": a["w_up"].reshape(NE, D, DE), "w_down": a["w_down"].reshape(NE, DE, D),
        **{n: a[n][0] for n in ("ln1_g", "ln1_b", "ln2_g", "ln2_b")}, **shape_constants(),
    }
    return {n: np.ascontiguousarray(v) for n, v in out.items()}


def results(r):
    y = r["y"]
    heads = lambda t, n: t.reshape(1, 1, -1, n, HD)
    return (y[:SEQ].reshape(1, SEQ, D), y[SEQ:].reshape(DB, DT, D),
            heads(np.ascontiguousarray(r["kT"].T), HA), heads(r["v"], HA),
            np.ascontiguousarray(r["uT"].T).reshape(1, 1, PB, D_B),
            heads(np.ascontiguousarray(r["kmT"].T), HC), heads(r["vm"], HC),
            r["win_k_s"].reshape(1, DB, WB, HA, HD), r["win_v_s"].reshape(1, DB, WB, HA, HD),
            np.ascontiguousarray(r["poolT_s"].reshape(P, 2, DB, PB).transpose(2, 3, 1, 0)).reshape(1, DB, PB, D_B))


def kernel(**inputs):
    import concourse.bacc as _bacc
    from concourse.bass_utils import run_bass_kernel_spmd as _run

    nc = _bacc.Bacc("TRN2", target_bir_lowering=False, num_devices=1)
    arrays = laid_out(inputs)
    ins = {n: nc.dram_tensor(n, a.shape, F32, kind="ExternalInput").ap() for n, a in arrays.items()}
    outs = {n: nc.dram_tensor("out_" + n, s, F32, kind="ExternalOutput").ap() for n, s in _OUT.items()}
    build(nc, ins, outs)
    r = _run(nc, [arrays], core_ids=[0])
    return results({n: r.results[0]["out_" + n] for n in _OUT})
```

```python
from contextlib import ExitStack

import concourse.bass as bass
import numpy as np
from concourse import mybir

F32 = mybir.dt.float32
F32R = mybir.dt.float32r
U32 = mybir.dt.uint32
ALU = mybir.AluOpType
ACT = mybir.ActivationFunctionType
AX = mybir.AxisListType

P = 128
D = 1024
KT = D // P
SEQ = 1024
DB, DT = 8, 4
SMP = DB * DT
TOK = SEQ + SMP
CH = SEQ // P + 1
HD = 64
HA, HC = 8, 4
D_A, D_B, D_C = 512, 256, 256
N_MEM = 256
WB = 2048
PB = 15
PATTERNS = ((128, 1), (512, 4), (2048, 16))
NG, EPG = 4, 8
NE = NG * EPG
DE = 256
ALPHA = 2.0 ** 0.25
EPS = 1e-5
QS = -(HD ** -0.5)
MASKED = 1e30

FAR = [16 * j + t for j in range((WB - 512) // 16) for t in range(DT)]
NEAR = list(range(WB - 512, WB))
ROWS = FAR + NEAR
NK = len(ROWS)
KC = NK // 4
NVT = NK // P

ARENA = 51984
COPIES_FIRST = 24

CAP = 112
LN_SPLIT = 128
NPAIR = 2 * TOK
BLOCKS = NPAIR // CAP


def distance_bias(dist):
    dist = np.asarray(dist)
    c = np.zeros(dist.shape)
    for w, d in PATTERNS:
        c += (dist >= 0) & (dist <= w) & (dist % d == 0)
    return np.where(c > 0, -np.log(np.maximum(c, 1)), MASKED)


def shape_constants():
    slopes = 2.0 ** (-8.0 * np.arange(1, HA + 1) / HA)
    p, u = np.arange(P)[:, None], np.arange(SEQ)[None, :]
    dist = p + SEQ - P - u
    table = np.stack([distance_bias(dist) + s * np.maximum(dist, 0) for s in slopes])
    b, h, t = np.meshgrid(np.arange(4), np.arange(HA), np.arange(DT), indexing="ij")
    b, h, t = (x.reshape(P, 1) for x in (b, h, t))
    d_win = WB + t - np.array(ROWS)[None, :]
    win = distance_bias(d_win) + slopes[h] * d_win
    new = []
    for g in range(2):
        kb, kt = np.arange(SMP)[None, :] // DT, np.arange(SMP)[None, :] % DT
        dn = np.where(kb == 4 * g + b, t - kt, -1)
        new.append(distance_bias(dn) + slopes[h] * np.maximum(dn, 0))
    sample = np.concatenate([win] + new, axis=1)
    inv = np.zeros((P, 2, 17))
    for tile in range(2):
        for half in range(2):
            w = 2 ** (2 * tile + half + 1)
            inv[64 * half:64 * half + 64, tile, :16] = 1.0 / np.minimum(w, np.arange(16) + 1)
            inv[64 * half:64 * half + 64, tile, 16] = 1.0 / w
    tri = (np.arange(P)[:, None] < np.arange(P)[None, :]).astype(np.float32)
    iota = np.broadcast_to(np.arange(P), (P, P))
    small = np.concatenate([np.eye(P), tri, np.ones((P, P)), iota, inv.reshape(P, 34),
                            1.0 + np.arange(P)[:, None] + P * np.arange(CH)[None, :],
                            (np.arange(P)[:, None] + P * np.arange(CH)[None, :] < TOK)], axis=1)
    f = np.float32
    return {"c_table": table.astype(f), "c_sample": sample.astype(f), "c_small": small.astype(f)}


class Steps:

    def __init__(self, eng, sem):
        self.eng, self.sem, self.n = eng, sem, 0

    def __call__(self, ins):
        self.n += 1
        ins.then_inc(self.sem, 1)
        self.eng.wait_ge(self.sem, self.n)


def build(nc, I, O):
    ctx = ExitStack()
    with ctx:
        def sem(name):
            return ctx.enter_context(nc.semaphore(name))

        def overlay(name, off, a, b):
            with ExitStack() as place:
                if off:
                    place.enter_context(nc.sbuf_tensor(name + "_before", [P, off], F32))
                t = place.enter_context(nc.sbuf_tensor(name, [P, a * b], F32R))
            return t[:, :].rearrange("p (a b) -> p a b", a=a)

        XH, XL = overlay("x_high", 27024, KT, TOK), overlay("x_low", 18576, KT, TOK)
        WH = [overlay(f"w_high{sl}", 39568 + 8192 * sl, KT, 512) for sl in range(2)]
        WL = [overlay(f"w_low{sl}", 35472 + 8192 * sl, KT, 512) for sl in range(2)]
        WOH, WOL = overlay("wo_high", 0, KT, D), overlay("wo_low", 27024, KT, D)
        CATH, CATL = overlay("cat_high", 8448, KT, TOK), overlay("cat_low", 18576, KT, TOK)
        arenas = [(lo, hi, ctx.enter_context(nc.sbuf_tensor(name, [P, hi - lo], F32))) for name, lo, hi in
                  (("front", 0, 18576), ("middle", 18576, 27024), ("back", 27024, ARENA))]
        PS = ctx.enter_context(nc.psum_tensor("psum", [P, 8 * 512], F32))
        CS = ctx.enter_context(nc.sbuf_tensor("consts", [P, 4 * P + 34 + 2 * CH], F32))
        ST = ctx.enter_context(nc.sbuf_tensor("stats", [P, 420], F32))
        h1_d = nc.dram_tensor("h1_d", [TOK, D], F32, kind="Internal").ap()
        pair_d = nc.dram_tensor("pair_d", [NPAIR, D], F32, kind="Internal").ap()

        def at(off, *dims):
            n = int(np.prod(dims))
            v, = (t[:, off - lo:off - lo + n] for lo, hi, t in arenas if lo <= off and off + n <= hi)
            if len(dims) == 2:
                v = v.rearrange("p (a b) -> p a b", a=dims[0])
            elif len(dims) == 3:
                v = v.rearrange("p (a b c) -> p a b c", a=dims[0], b=dims[1])
            elif len(dims) == 4:
                v = v.rearrange("p (a b c d) -> p a b c d", a=dims[0], b=dims[1], c=dims[2])
            return v

        def bank(n):
            return PS[:, 512 * n:512 * n + 512]

        ident, tri, ones, iota = (CS[:, P * n:P * n + P] for n in range(4))
        pool_inv = CS[:, 4 * P:4 * P + 34].rearrange("p (a b) -> p a b", a=2)
        tok1 = CS[:, 4 * P + 34:4 * P + 34 + CH]
        valid = CS[:, 4 * P + 34 + CH:4 * P + 34 + 2 * CH]

        QT, KTT, QC, UH = at(0, 4, TOK), at(4224, 4, TOK), at(8448, 2, TOK), 16
        V = at(10560, CH, D_A)
        KM, VM = at(15168, 2, N_MEM), at(15680, 2, D_C)
        UP = at(16192, 2, UH + SEQ)
        US = at(16192 + 2 * (UH + SEQ), 2, DB, PB + DT)
        USF = at(16192 + 2 * (UH + SEQ), 2 * DB, PB + DT)
        SS = at(16192, 2, 960)
        CAT = at(18576, KT, TOK)
        PA, PBUF = at(18576 + 6 * TOK, 2, UH + SEQ), at(18576 + 2 * TOK, 2, UH + SEQ)
        XF, WF = at(18576, KT, TOK), [at(35472 + 8192 * s, KT, 512) for s in range(2)]
        MT = at(39568, KT, N_MEM)
        RING = [27024, 27024 + 4096]
        SP = [at(x, 1024) for x in (35472, 36496, 37520, 38544, 41616, 42640)]
        PTB = [at(39568 + 512 * s, 4, P) for s in range(4)]
        PTS = at(18576 + 6 * TOK, 2, 8, P)
        TB = [[at(43664 + 2048 * a + 1024 * b, 1024) for b in range(2)] for a in range(2)]
        QBD = at(47760, 2, 4, 4, 32)
        QBM = at(48784, 2, DB, 32)
        PMS, PTM = at(49296, N_MEM), at(49552, 2, P)
        SBIAS = at(49808, 960)
        DG = [at(50768 + 2 * P * s, 2, P) for s in range(2)]
        KN = at(51280, 512)
        INV = at(51792, P)
        OA = at(51280, 512)
        SA, SBF = at(27024 + 3584, 2, DB, PB + DT), at(31120 + 3584, 2, DB, PB + DT)
        WO = at(27024, KT, D)
        H1 = at(35472, CH, D)
        GB = at(44688, 2, D)
        XR = [at(46736 + D * s, D) for s in range(2)]
        RB = [at(48784 + D * s, D) for s in range(2)]
        H1T = [at(50832, KT, P), at(16896, KT, P)]
        WRT = at(17920, KT, 36)
        LG = at(13600, CH, 36)
        SLOT = [(0, 2048, 4096), (18576, 20624, 22672), (24720, 27024, 6144), (45712, 47760, 49808)]
        WG = [at(g, KT, DE) for g, _, _ in SLOT]
        WU = [at(u, KT, DE) for _, u, _ in SLOT]
        WD = [at(d, 2, D) for _, _, d in SLOT]
        XG = [at(30864 + D * s, D) for s in range(2)]
        XGT = [at(32912 + D * s, KT, P) for s in range(2)]
        SIL = [at(13312 + 2048 + 256 * s, 2, P) for s in range(2)]
        AT = [at(13312 + 2560 + 256 * s, 2, P) for s in range(2)]
        YS = [at(9216 + D * s, D) for s in range(2)]
        GB2 = at(11264, 2, D)
        YP = [at(off, 2, D) for off in (24720, 27024, 29072)]
        RF = [at(18576 + D * s, D) for s in range(3)]

        MN, DEN, RD = ST[:, 0:96], ST[:, 96:192], ST[:, 192:288]
        SMN, SDEN, SRD = ST[:, 288:291], ST[:, 291:294], ST[:, 294:297]
        BN = ST[:, 300:300 + 24].rearrange("p (c s) -> p c s", c=2)
        MV = ST[:, 330:330 + 4 * CH].rearrange("p (c s) -> p c s", c=CH)
        MV2 = ST[:, 370:370 + 4 * CH].rearrange("p (c s) -> p c s", c=CH)
        EPSC = ST[:, 297:298]
        PSC = ST[:, 298:300]
        WPL2 = ctx.enter_context(nc.sbuf_tensor("w_pool2", [P, 2, 64], F32))
        RT = ctx.enter_context(nc.sbuf_tensor("routing", [P, 72], F32))

        FLAG = at(35300, 1).bitcast(U32)
        CNT, NB = at(35301, NE), at(35333, NE)
        EB = at(35365, BLOCKS).bitcast(U32)
        OPOS, OVAL = at(15872 + 512, 2, CH), at(15872 + 530, 2, CH, 4)
        OLF, OLI = at(16500, 4), at(16504, 2).bitcast(U32)
        OPRE = [at(16510, NE), at(16542, NE)]
        OTMP = at(SLOT[1][0], BLOCKS, NE)

        s_const, s_bias = sem("s_const"), sem("s_bias")
        s_xk = [sem(f"s_xk{k}") for k in range(KT)]
        s_w = [sem(f"s_w{g}") for g in range(5)]
        s_mem, s_state = sem("s_mem"), sem("s_state")
        s_proj, s_hi, s_lo = sem("s_proj"), sem("s_hi"), sem("s_lo")
        s_pe_d, s_pe_a = sem("s_pe_d"), sem("s_pe_a")
        s_copy = [sem(f"s_copy{i}") for i in range(2)]
        s_store = sem("s_store")
        s_sum, s_pool = sem("s_sum"), sem("s_pool")
        s_tb = [sem(f"s_tb{i}") for i in range(2)]
        s_ring = [sem(f"s_ring{i}") for i in range(2)]
        s_S, s_min, s_exp = sem("s_S"), sem("s_min"), sem("s_exp")
        s_rd, s_dg, s_inv = sem("s_rd"), sem("s_dg"), sem("s_inv")
        s_T, s_Td, s_Ta, s_PV, s_O, s_OB = sem("s_T"), sem("s_Td"), sem("s_Ta"), sem("s_PV"), sem("s_O"), sem("s_OB")
        s_xp, s_xe, s_sexp, s_smin, s_srd = sem("s_xp"), sem("s_xe"), sem("s_sexp"), sem("s_smin"), sem("s_srd")
        s_dve, s_pl = sem("s_dve"), sem("s_pl")
        s_wo = [sem(f"s_wo{i}") for i in range(2)]
        s_gb, s_mix, s_r = sem("s_gb"), sem("s_mix"), sem("s_r")
        s_x = [sem(f"s_x{i}") for i in range(2)]
        s_std, s_nrm, s_z, s_h1 = sem("s_std"), sem("s_nrm"), sem("s_z"), sem("s_h1")
        s_ht, s_hte, s_rt = sem("s_ht"), sem("s_hte"), sem("s_rt")
        s_h1d = sem("s_h1d")
        s_M, s_rank, s_oh, s_ohx, s_idx = sem("s_M"), sem("s_rank"), sem("s_oh"), sem("s_ohx"), sem("s_idx")
        s_rx, s_ra = sem("s_rx"), sem("s_ra")
        s_g = [sem(f"s_g{i}") for i in range(4)]
        s_wd = [sem(f"s_wd{i}") for i in range(4)]
        s_gx = [sem(f"s_gx{i}") for i in range(2)]
        s_col, s_past = sem("s_col"), sem("s_past")
        s_tp, s_xgt, s_gu, s_sil, s_at, s_y, s_ya, s_yd = (sem(n) for n in
                                                      ("s_tp", "s_xgt", "s_gu", "s_sil", "s_at", "s_y", "s_ya", "s_yd"))
        s_ys = [sem(f"s_ys{i}") for i in range(2)]
        s_gb2 = sem("s_gb2")
        s_yp = [sem(f"s_yp{i}") for i in range(3)]
        s_fp, s_zero = sem("s_fp"), sem("s_zero")
        s_f, s_f1, s_fz, s_fo, s_std2, s_nr2 = (sem(n) for n in ("s_f", "s_f1", "s_fz", "s_fo", "s_std2", "s_nr2"))
        s_out = [sem(f"s_out{i}") for i in range(3)]

        o_pos, o_eb, o_oh, o_ohx, o_idx = (sem(n) for n in ("o_pos", "o_eb", "o_oh", "o_ohx", "o_idx"))
        o_free = sem("o_free")
        o_w, o_g, o_s = sem("o_w"), sem("o_g"), sem("o_s")
        o_tp, o_xgt, o_gu, o_sil, o_at, o_y, o_ya, o_yd = (sem(n) for n in
                                                           ("o_tp", "o_xgt", "o_gu", "o_sil", "o_at", "o_y", "o_ya", "o_yd"))

        block = ctx.enter_context(nc.Block())

        def overflow(eng):
            eng.wait_ge(s_idx, 1)
            return eng.If(eng.value_load(FLAG[0:1, 0:1], min_val=0, max_val=1) > 0)

        def rows(c):
            return P if c < CH - 1 else SMP

        W_G = {"q": 0, "k": 1, "v": 2, "u": 3, "m": 4}
        W_SLOT = [0, 1, 0, 1, 0]
        proj = []

        def parts(high, low, *ix):
            return tuple(t[(slice(None),) + ix] for t in (high, low))

        def proj_tile(dest3, grp, col):
            sl = W_SLOT[W_G[grp]]
            return [(d, lambda k, c=col, sl=sl: parts(WH[sl], WL[sl], k, slice(c, c + P)),
                     lambda k, a=a, n=n: parts(XH, XL, k, slice(a, a + n)), W_G[grp], s, P, n)
                    for d, a, n, s in dest3]

        W3 = TOK // 3
        for dest, grp, scale in ((QT, "q", QS), (KTT, "k", 1.0)):
            for m in range(4):
                proj += proj_tile([(dest[:, m, a:a + W3], a, W3, scale) for a in range(0, TOK, W3)], grp, m * P)
        for c in range(CH):
            proj.append((V[0:rows(c), c, :], lambda k, c=c: parts(XH, XL, k, slice(c * P, c * P + rows(c))),
                         lambda k: parts(WH[0], WL[0], k, slice(0, 512)), W_G["v"], 1.0, rows(c), 512))
        for m in range(2):
            proj += proj_tile([(QC[:, m, a:a + W3], a, W3, QS) for a in range(0, TOK, W3)], "u", D_B + m * P)
        for m in range(2):
            proj += proj_tile([(UP[:, m, UH:UH + W3], 0, W3, 1.0), (UP[:, m, UH + W3:UH + 2 * W3], W3, W3, 1.0),
                               ((UP[:, m, UH + 2 * W3:UH + SEQ], US[:, m, :, PB:PB + DT]), 2 * W3, W3, 1.0)], "u", m * P)
        n_x = len(proj)
        for m in range(2):
            proj.append((KM[:, m, :], lambda k, m=m: WF[0][:, k, m * P:m * P + P], lambda k: MT[:, k, :], W_G["m"], 1.0, P, N_MEM))
        for m in range(2):
            proj.append((VM[:, m, :], lambda k, m=m: MT[:, k, m * P:m * P + P], lambda k: WF[0][:, k, 256:512], W_G["m"], 1.0, P, N_MEM))
        NPROJ = len(proj)
        last_of = {g: max(n for n, t in enumerate(proj) if t[3] == g) for g in range(5)}

        def proj_out(n, copy):
            d, _, _, _, _, m, w = proj[n]
            src = bank(n % 8)[0:m, 0:w]
            if isinstance(d, tuple):
                copy(d[0], src[:, 0:w - SMP])
                return copy(d[1], src[:, w - SMP:w].rearrange("p (b t) -> p b t", t=DT))
            return copy(d, src)

        def proj_done(eng, n):
            eng.wait_ge(s_pe_d, n // 2 + 1)
            if n >= 1:
                eng.wait_ge(s_pe_a, (n + 1) // 2)

        splits = []
        for k in range(KT):
            splits += [(s_xk[k], 32, XF[:, k, :], XH[:, k, :], XL[:, k, :]),
                       (s_xk[k], 32, WF[0][:, k, :], WH[0][:, k, :], WL[0][:, k, :])]
        for g in (1, 2, 3):
            sl = W_SLOT[g]
            splits += [(s_w[g], 16) + tuple(t[sl][:, k:k + 2, :] for t in (WF, WH, WL)) for k in range(0, KT, 2)]
        splits_of = {0: range(0, 2 * KT), 1: range(2 * KT, 2 * KT + 4), 2: range(2 * KT + 4, 2 * KT + 8), 3: range(2 * KT + 8, 2 * KT + 12)}

        def rounded_part(act, j):
            load, count, full, high, _ = splits[j]
            act.wait_ge(load, count)
            nc.scalar.copy(high, full).then_inc(s_hi, 1)

        def rest(dve, j):
            _, _, full, high, low = splits[j]
            dve.wait_ge(s_hi, j + 1)
            nc.vector.tensor_tensor(low, full, high.bitcast(F32), ALU.subtract).then_inc(s_lo, 1)

        def splits_after(n):
            for g in (2, 3):
                q = n // 2 - (last_of[g - 2] // 2 + 1)
                if 0 <= q < 4:
                    return [splits_of[g][q]]
            return []

        def wo_parts(k):
            return WO[:, k, :], WOH[:, k, :], WOL[:, k, :]

        def cat_parts(c):
            return tuple(t[:, :, c * P:c * P + rows(c)] for t in (CAT, CATH, CATL))

        WO_SPLIT_AT = {40: (0,), 41: (1,), 42: (2,), 43: (3,), 44: (4,), 45: (5,), 46: (6,), 47: (7,)}

        units = [("w", hp, i) for hp in range(4) for i in range(8)] + [("c", hp, i) for hp in range(2) for i in range(8)]
        NU = len(units)
        items = []
        unit_items = []
        for u, (kind, hp, i) in enumerate(units):
            nb = i + 1 if kind == "w" else 2
            unit_items.append(list(range(len(items), len(items) + (nb + 1) // 2)))
            items += [(u, list(range(b0, min(b0 + 2, nb))), nb) for b0 in range(0, nb, 2)]
        NI = len(items)

        def item_done(eng, n):
            if n % 2 == 0:
                eng.wait_ge(s_Td, n // 2 + 1)
            else:
                eng.wait_ge(s_Ta, n // 2 + 1)

        extra = {u: [] for u in range(-1, NU)}
        extra[-1] = [("knew",)]
        sample_steps = ([("pool", j) for j in range(5)] + [("ss", s) for s in range(6)] + [("st", 0, 0), ("st", 0, 1)]
                        + [("ss", 6), ("ss", 7), ("pv", 0, 0), ("pv", 0, 1), ("st", 1, 0), ("st", 1, 1)]
                        + [("pv", 0, 2), ("pv", 0, 3), ("ot", 0)] + [("pv", 1, p) for p in range(4)] + [("ot", 1)])
        for j, e in enumerate(sample_steps):
            extra[32 - len(sample_steps) + j].append(e)
        extra[32].append(("ms",))
        extra[34].append(("mt",))
        extra[35].append(("mpv",))
        extra[36].append(("mo",))
        xlist = [e for u in range(-1, NU) for e in extra[u]]
        xnum = {e: n for n, e in enumerate(xlist)}
        xbank = {e: 6 + (u + 1) % 2 for u in range(-1, NU) for e in extra[u]}
        x_before = [sum(len(extra[w]) for w in range(-1, u)) for u in range(NU)]
        ring_user = [e for e in xlist if e[0] in ("ss", "pv", "ms", "mpv")]
        ring_no = {e: n for n, e in enumerate(ring_user)}

        def ring_dmas(e):
            return sum(4 if t < 3 else 1 for t in pv_tiles(e[2])) if e[0] == "pv" else 1

        def pv_tiles(p):
            return range(2 * p, min(2 * p + 2, NVT))

        def ring_ready(eng, e):
            n = ring_no[e]
            eng.wait_ge(s_ring[n % 2], 16 * sum(ring_dmas(f) for f in ring_user[n % 2:n + 1:2]))

        def score_at(u, s):
            return 1024 * s + (512 * (u % 2) if units[u][0] == "c" else 0)

        def load_table(sp, hp):
            if hp >= 2:
                sp.wait_ge(s_min, 2 * 8 * (hp - 1))
            elif hp == 0:
                proj_done(sp, n_x - 1)
            for s in range(2):
                sp.dma_start(TB[hp % 2][s], I["c_table"][2 * hp + s]).then_inc(s_tb[hp % 2], 16)

        def ring_load(n, e):
            off = RING[n % 2]
            if e[0] == "ss":
                return [at(off, 4, 4 * KC)], [I["winkT"][e[1]].rearrange("p a n -> p a n")]
            if e[0] == "pv":
                dst = at(off, 2, 4, 512)
                to, srcs = [], []
                for t in pv_tiles(e[2]):
                    if t < 3:
                        for b in range(4):
                            far = I["cache_win_v"][4 * e[1] + b][0:WB - 512, :].rearrange("(j r) n -> j (r n)", r=16)[:, 0:DT * 512]
                            to.append(dst[:, t % 2, b, :])
                            srcs.append(far[32 * t:32 * t + 32, :].rearrange("j (r n) -> j r n", r=DT))
                    else:
                        r0 = WB - 512 + P * (t - 3)
                        to.append(dst[:, t % 2, :, :])
                        srcs.append(I["cache_win_v"][4 * e[1]:4 * e[1] + 4, r0:r0 + P, :].rearrange("b p n -> p b n"))
                return to, srcs
            if e[0] == "ms":
                return [at(off, 2, DB * N_MEM)], [I["memkT"]]
            return [at(off, DB * 2, D_C)], [I["cache_mem_v"].rearrange("b (t p) n -> p (b t) n", p=P)]

        def load_gu(sp, e, j):
            for w, d in (("w_gate", WG), ("w_up", WU)):
                src = I[w][bass.ds(e, 1)].rearrange("o (k p) n -> p (o k) n", p=P)
                sp.dma_start(d[j], src).then_inc(s_g[j], 16)

        def load_dn(sp, e, j):
            src = I["w_down"][bass.ds(e, 1)].rearrange("o (k p) n -> p (o k) n", p=P)
            sp.dma_start(WD[j], src).then_inc(s_wd[j], 16)

        def load_expert(sp, e, j):
            load_gu(sp, e, j)
            load_dn(sp, e, j)

        R0 = 13600 + 324
        RM, RMP = at(R0, CH, NE), at(R0 + 288, CH, NE)
        RE = [at(R0 + 576, CH, NE), at(R0 + 864, CH, NE)]
        RL = at(R0 + 1152, CH, NE)
        RANK = at(17800, CH, NE)
        RX = at(R0 + 1440, CH, NE)
        RV = at(9216, 2, CH, 96)
        OH = [at(32912 + P * s, P) for s in range(4)]
        IDX = at(34960, 3 * NE).bitcast(U32)
        IDF = at(35056, 3 * NE)

        def transposed_out(eng, copy, n):
            if n >= 4:
                eng.wait_ge(s_PV, n - 3)
            w = 2 * P * len(items[n][1])
            return copy(PTB[n % 4].rearrange("p a b -> p (a b)")[:, 0:w], bank(4 + n % 2)[:, 0:w])

        GI = [at(35296 + n, 1).bitcast(U32) for n in range(2)]
        SI = [at(35298 + n, 1).bitcast(U32) for n in range(2)]
        G1W = at(35152, 12 * CH)
        RX1 = at(35260, CH * 4)
        W2 = G1W[:, 0:CH]
        GS = IDF[:, 2 * NE:3 * NE]

        @block.sync
        def _(sp):
            xv = I["xT"].rearrange("(k p) n -> p k n", p=P)
            wv = I["w_in"].rearrange("(k p) n -> p k n", p=P)
            for k in range(KT):
                sp.dma_start(XF[:, k, :], xv[:, k, :]).then_inc(s_xk[k], 16)
                sp.dma_start(WF[0][:, k, :], wv[:, k, 0:512]).then_inc(s_xk[k], 16)
                if k == 1:
                    sp.dma_start(CS[:, :], I["c_small"]).then_inc(s_const, 16)
            sp.dma_start(WF[1], wv[:, :, 512:1024]).then_inc(s_w[1], 16)
            sp.dma_start(USF[:, :, 0:PB], I["stateT"]).then_inc(s_state, 16)
            sp.dma_start(WPL2[:, :, :], I["w_pool"].rearrange("(m h) c e -> (h c) m e", h=2)).then_inc(s_state, 16)
            sp.dma_start(PSC, I["pool_scale"]).then_inc(s_state, 16)
            copies = [(t, b, r) for t in "kv" for b in range(DB) for r in range(2)]
            half = (WB - DT) // 2

            def copy_cache(n):
                t, b, r = copies[n]
                if n >= 2:
                    sp.wait_ge(s_copy[n % 2], 16 * (n // 2))
                sp.dma_start(O["win_" + t + "_s"][b, r * half:(r + 1) * half, :],
                             I["cache_win_" + t][b, DT + r * half:DT + (r + 1) * half, :]).then_inc(s_copy[n % 2], 16)

            for n in range(COPIES_FIRST):
                copy_cache(n)
            load_table(sp, 0)
            sp.dma_start(SBIAS, I["c_sample"]).then_inc(s_bias, 16)
            for n, e in enumerate(ring_user):
                if n == 0:
                    proj_done(sp, n_x - 1)
                if n >= 2:
                    sp.wait_ge(s_xp, xnum[ring_user[n - 2]] + 1)
                dst, srcs = ring_load(n, e)
                for d, s in zip(dst, srcs):
                    sp.dma_start(d, s).then_inc(s_ring[n % 2], 16)
                if n == 1:
                    load_table(sp, 1)
                if n == 2:
                    load_table(sp, 2)
                if n == 7:
                    load_table(sp, 3)
                if n == 1:
                    proj_done(sp, NPROJ - 1)
                    sp.dma_start(O["kT"].rearrange("(m p) n -> p m n", p=P), KTT[:, :, 0:SEQ]).then_inc(s_store, 16)
                    sp.dma_start(O["v"].rearrange("(c p) n -> p c n", p=P), V[:, 0:CH - 1, :]).then_inc(s_store, 16)
                    sp.dma_start(O["kmT"].rearrange("(m p) n -> p m n", p=P), KM).then_inc(s_store, 16)
                    sp.dma_start(O["vm"].rearrange("(m p) n -> p m n", p=P), VM).then_inc(s_store, 16)
                    sp.dma_start(O["uT"].rearrange("(m p) n -> p m n", p=P), UP[:, :, UH + SEQ - PB:UH + SEQ]).then_inc(s_store, 16)
                    sp.wait_ge(s_state, 48)
                    sp.dma_start(O["poolT_s"], USF[:, :, DT:DT + PB]).then_inc(s_store, 16)
                    for b in range(DB):
                        sp.dma_start(O["win_v_s"][b, WB - DT:WB, :], V[DT * b:DT * b + DT, CH - 1, :]).then_inc(s_store, 16)
                    sp.wait_ge(s_xe, xnum[("knew",)] + 1)
                    for b in range(DB):
                        sp.dma_start(O["win_k_s"][b, WB - DT:WB, :], KN[DT * b:DT * b + DT, :]).then_inc(s_store, 16)
                    for c in range(COPIES_FIRST, len(copies)):
                        copy_cache(c)
            wo = I["w_o"].rearrange("(k p) n -> p k n", p=P)
            sp.wait_ge(s_xp, xnum[("ms",)] + 1)
            sp.dma_start(WO[:, 0:4, :], wo[:, 0:4, :]).then_inc(s_wo[0], 16)
            sp.wait_ge(s_xp, xnum[("mpv",)] + 1)
            sp.dma_start(WO[:, 4:8, :], wo[:, 4:8, :]).then_inc(s_wo[1], 16)
            item_done(sp, NI - 1)
            item_done(sp, NI - 2)
            sp.wait_ge(s_OB, NU)
            sp.wait_ge(s_store, 16 * (6 + 2 * DB))
            for v, n in (("ln1_g", 0), ("ln1_b", 1)):
                sp.dma_start(GB[:, n, :], I[v].unsqueeze(0).broadcast_to([P, D])).then_inc(s_gb, 16)
            sp.dma_start(WRT, I["w_r"].rearrange("(k p) e -> p k e", p=P)).then_inc(s_gb, 16)
            sp.dma_start(RT[:, 0:36], I["b_r"].unsqueeze(0).broadcast_to([P, 36])).then_inc(s_gb, 16)

            def store_h1(c):
                sp.wait_ge(s_h1, c + 1)
                sp.dma_start(h1_d[c * P:c * P + rows(c), :], H1[0:rows(c), c, :]).then_inc(s_h1d, 16)

            for c in range(CH):
                if c >= 2:
                    sp.wait_ge(s_r, c - 1)
                sp.dma_start(XR[c % 2][0:rows(c), :], I["x"][c * P:c * P + rows(c), :]).then_inc(s_x[c % 2], 16)
                if c >= 3:
                    store_h1(c - 3)
            sp.wait_ge(s_mix, CH)
            load_expert(sp, 0, 0)
            for c in range(CH - 3, CH):
                store_h1(c)
            load_expert(sp, 1, 1)
            load_expert(sp, 2, 2)
            sp.wait_ge(s_rt, CH)
            load_expert(sp, 3, 3)
            with sp.Fori(1, NE // 4) as i:
                for j in range(4):
                    sp.wait_ge(s_gu, i * 4 + (j - 3))
                    load_gu(sp, i * 4 + j, j)
                    sp.wait_ge(s_y, i * 4 + (j - 3))
                    load_dn(sp, i * 4 + j, j)
            with overflow(sp):
                sp.wait_ge(s_y, NE)
                sp.wait_ge(o_eb, 1)
                with sp.Fori(0, BLOCKS) as b:
                    e = sp.value_load(EB[0:1, bass.ds(b, 1)], min_val=0, max_val=NE - 1)
                    sp.wait_ge(o_free, b + 1)
                    for w, d in (("w_gate", WG), ("w_up", WU), ("w_down", WD)):
                        sp.dma_start(d[0], I[w][bass.ds(e, 1)].rearrange("o (k p) n -> p (o k) n", p=P)).then_inc(o_w, 16)
                sp.wait_ge(o_s, 16 * BLOCKS)
            with sp.Else():
                sp.nop()
            for v, n in (("ln2_g", 0), ("ln2_b", 1)):
                sp.dma_start(GB2[:, n, :], I[v].unsqueeze(0).broadcast_to([P, D])).then_inc(s_gb2, 16)
            sp.wait_ge(s_ys[0], 16 * (NE // 2))
            sp.wait_ge(s_ys[1], 16 * (NE // 2))
            pr = pair_d.rearrange("(k n) d -> n k d", k=2)

            def store_y(c):
                sp.wait_ge(s_fo, c + 1)
                sp.wait_ge(s_fp, c + 1)
                sp.dma_start(O["y"][c * P:c * P + rows(c), :], RF[c % 3][0:rows(c), :]).then_inc(s_out[c % 3], 16)

            for c in range(CH):
                if c == 0:
                    sp.wait_ge(s_y, NE)
                if c >= 3:
                    sp.wait_ge(s_f1, c - 2)
                sp.dma_start(YP[c % 3][0:rows(c), :, :], pr[c * P:c * P + rows(c), :, :]).then_inc(s_yp[c % 3], 16)
                if c >= 3:
                    store_y(c - 3)
            for c in range(CH - 3, CH):
                store_y(c)
            for i in range(3):
                sp.wait_ge(s_out[i], 16 * (CH // 3))
            for i in range(2):
                sp.wait_ge(s_copy[i], 16 * DB * 2)

        @block.tensor
        def _(pe):
            def mm(out, lhsT, rhs, start, stop):
                return nc.tensor.matmul(out, lhsT, rhs, start=start, stop=stop, skip_group_check=True)

            def product(n, k):
                _, lt, rh, g, _, m, w = proj[n]
                out, l, r = bank(n % 8)[0:m, 0:w], lt(k), rh(k)
                if g == 4:
                    return mm(out, l, r, k == 0, k == KT - 1)
                mm(out, l[0], r[0], k == 0, False)
                mm(out, l[0], r[1], False, False)
                return mm(out, l[1], r[0], False, k == KT - 1)

            for k in range(KT):
                pe.wait_ge(s_lo, 2 * k + 2)
                for n in range(8):
                    last = product(n, k)
                    if k == KT - 1:
                        last.then_inc(s_proj, 1)
            for n in range(8, NPROJ):
                g = proj[n][3]
                if 1 <= g < 4:
                    pe.wait_ge(s_lo, splits_of[g][-1] + 1)
                if g == 4:
                    pe.wait_ge(s_w[4], 16)
                    pe.wait_ge(s_mem, 16)
                proj_done(pe, n - 8)
                for k in range(KT):
                    last = product(n, k)
                last.then_inc(s_proj, 1)
            proj_done(pe, NPROJ - 1)
            pe.wait_ge(s_const, 16)

            def scores(u):
                kind, hp, i = units[u]
                if u and units[u - 1][0] == "w":
                    pe.wait_ge(s_min, 2 * u)
                if kind == "c" and units[u - 2][0] == "c":
                    pe.wait_ge(s_exp, 2 * (u - 1))
                width = P * (i + 1) if kind == "w" else N_MEM
                for a in range(0, width, 512):
                    w = min(512, width - a)
                    for s in range(2):
                        h = slice(64 * s, 64 * s + 64)
                        q = (QT if kind == "w" else QC)[h, hp, i * P:i * P + P]
                        k = (KTT if kind == "w" else KM)[h, hp, a:a + w]
                        o = score_at(u, s) + a
                        last = mm(PS[:, o:o + w], q, k, True, True)
                        if a + w == width:
                            last.then_inc(s_S, 1)

            def transposes(n):
                u, blocks, _ = items[n]
                if n >= 2:
                    item_done(pe, n - 2)
                if blocks[0] == 0:
                    pe.wait_ge(s_exp, 2 * u + 2)
                b = bank(4 + n % 2)
                for j, kb in enumerate(blocks):
                    for s in range(2):
                        last = nc.tensor.transpose(b[:, (2 * j + s) * P:(2 * j + s) * P + P], SP[(u % 3) * 2 + s][:, kb * P:kb * P + P], ident)
                last.then_inc(s_T, 1)

            def values(n):
                u, blocks, nb = items[n]
                kind, hp, i = units[u]
                item_done(pe, n)
                if blocks[0] == 0:
                    if u >= 2:
                        pe.wait_ge(s_OB, u - 1)
                    pe.wait_ge(s_xe, x_before[u])
                b = bank(6 + u % 2)
                for j, kb in enumerate(blocks):
                    for s in range(2):
                        c = (2 * hp + s) * HD
                        v = (V if kind == "w" else VM)[:, kb, c:c + HD]
                        last = mm(b[64 * s:64 * s + 64, 0:P], v, PTB[n % 4][:, 2 * j + s, :], kb == 0, kb == nb - 1)
                last.then_inc(s_PV, 1)
                if blocks[-1] == nb - 1:
                    pe.wait_ge(s_dg, u + 1)
                    for s in range(2):
                        last = mm(b[64 * s:64 * s + 64, P:2 * P], ones[:, 0:HD], DG[u % 2][:, s, :], True, True)
                    last.then_inc(s_O, 1)

            def x_step(e, u):
                x = xnum[e]
                if x:
                    pe.wait_ge(s_xe, x)
                if u >= 1:
                    pe.wait_ge(s_OB, u)
                bx = bank(xbank[e])
                if e[0] == "knew":
                    for m in range(4):
                        last = nc.tensor.transpose(bx[0:SMP, m * P:m * P + P], KTT[:, m, SEQ:TOK], ident)
                elif e[0] == "pool":
                    pe.wait_ge(s_pool, e[1] // 2 + 1)
                    if e[1] < 4:
                        t, hf = e[1] // 2, e[1] % 2
                        for g in range(2):
                            r = slice(64 * g, 64 * g + 64)
                            last = mm(bx[r, 0:512], WPL2[r, t, :], PA[r, t, UH + 512 * hf:UH + 512 * hf + 512], True, True)
                    else:
                        for t in range(2):
                            for g in range(2):
                                r = slice(64 * g, 64 * g + 64)
                                last = mm(bx[r, t * SMP:t * SMP + SMP], WPL2[r, t, :], SA[r, t, :, PB:PB + DT], True, True)
                elif e[0] == "ss":
                    g, kc = e[1] // 4, e[1] % 4
                    ring_ready(pe, e)
                    if e[1] == 0:
                        pe.wait_ge(s_srd, 1)
                    kt = at(RING[ring_no[e] % 2], 4, 4, KC)
                    for hp in range(4):
                        for b in range(4):
                            last = mm(bx[32 * b:32 * b + 32, 0:KC], QBD[:, g, hp, b, :], kt[:, hp, b, :], hp == 0, hp == 3)
                    if kc == 3:
                        for hp in range(4):
                            for b in range(4):
                                last = mm(bx[32 * b:32 * b + 32, KC:KC + SMP], QBD[:, g, hp, b, :], KTT[:, hp, SEQ:TOK], hp == 0, hp == 3)
                elif e[0] == "st":
                    _, g, hf = e
                    pe.wait_ge(s_srd, 2 + g)
                    for j in range(4):
                        t = 4 * hf + j
                        m = P if t < NVT else SMP
                        last = nc.tensor.transpose(bx[0:m, j * P:j * P + P], SS[:, g, t * P:t * P + m], ident)
                elif e[0] == "pv":
                    _, g, p = e
                    ring_ready(pe, e)
                    vt = at(RING[ring_no[e] % 2], 2, 4, 512)
                    for t in pv_tiles(p):
                        for b in range(4):
                            last = mm(bx[32 * b:32 * b + 32, :], PTS[:, g, t, 32 * b:32 * b + 32], vt[:, t % 2, b, :],
                                      t == 2 * p, p < 3 and t == 2 * p + 1)
                    if p == 3:
                        for b in range(4):
                            last = mm(bx[32 * b:32 * b + 32, :], PTS[0:SMP, g, NVT, 32 * b:32 * b + 32], V[0:SMP, CH - 1, :], False, True)
                elif e[0] in ("ot", "mo"):
                    for hp in range(4):
                        last = nc.tensor.transpose(bx[:, hp * P:hp * P + P], OA[:, hp * P:hp * P + P], ident)
                elif e[0] == "ms":
                    ring_ready(pe, e)
                    km = at(RING[ring_no[e] % 2], 2, DB, N_MEM)
                    for j in range(4):
                        for n in range(4):
                            hp, b = n // 2, 2 * j + n % 2
                            last = mm(bx[32 * j:32 * j + 32, 0:N_MEM], QBM[:, hp, b, :], km[:, hp, b, :], n == 0, n == 3)
                elif e[0] == "mt":
                    pe.wait_ge(s_srd, 4)
                    for t in range(2):
                        last = nc.tensor.transpose(bx[:, t * P:t * P + P], PMS[:, t * P:t * P + P], ident)
                else:
                    ring_ready(pe, e)
                    vm = at(RING[ring_no[e] % 2], DB, 2, D_C)
                    for o in range(2):
                        for t in range(2):
                            for j in range(4):
                                last = mm(bx[32 * j:32 * j + 32, D_C * o:D_C * o + D_C], PTM[:, t, 32 * j:32 * j + 32],
                                          vm[:, 2 * j + o, t, :], t == 0, t == 1)
                last.then_inc(s_xp, 1)

            for e in extra[-1]:
                x_step(e, -1)
            scores(0)
            scores(1)
            for u in range(NU):
                if u + 2 < NU:
                    scores(u + 2)
                for n in unit_items[u]:
                    transposes(n)
                    if n:
                        values(n - 1)
                for e in extra[u]:
                    x_step(e, u)
            values(NI - 1)
            pe.wait_ge(s_OB, NU)

            def mix(c):
                if c >= 2:
                    pe.wait_ge(s_r, c - 1)
                m = rows(c)
                pe.wait_ge(s_lo, len(splits) + KT + c + 1)
                for n in range(2):
                    o = PS[0:m, 1024 * (c % 2) + 512 * n:1024 * (c % 2) + 512 * n + 512]
                    for k in range(KT):
                        cat_h, cat_l = (t[:, k, :] for t in cat_parts(c)[1:])
                        wo_h, wo_l = (t[:, 512 * n:512 * n + 512] for t in wo_parts(k)[1:])
                        mm(o, cat_h, wo_h, k == 0, False)
                        mm(o, cat_h, wo_l, False, False)
                        last = mm(o, cat_l, wo_h, False, k == KT - 1)
                last.then_inc(s_mix, 1)

            def h1_transposes(c):
                pe.wait_ge(s_h1, c + 1)
                m = rows(c)
                for hf in range(2):
                    if c >= 1:
                        pe.wait_ge(s_hte, 2 * (c - 1) + hf + 1)
                    for j in range(4):
                        k = 4 * hf + j
                        last = nc.tensor.transpose(bank(4 + hf)[:, j * P:j * P + m], H1[0:m, c, k * P:k * P + P], ident[0:m, 0:m])
                    last.then_inc(s_ht, 1)

            def router(c):
                m = rows(c)
                if c == 0:
                    pe.wait_ge(s_gb, 64)
                pe.wait_ge(s_hte, 2 * c + 2)
                for k in range(KT):
                    last = mm(bank(6)[0:m, 36 * c:36 * c + 36], H1T[c % 2][:, k, 0:m], WRT[:, k, :], k == 0, k == KT - 1)
                last.then_inc(s_rt, 1)

            for c in range(CH):
                mix(c)
                if c >= 1:
                    h1_transposes(c - 1)
                if c >= 2:
                    router(c - 2)
            h1_transposes(CH - 1)
            router(CH - 2)
            router(CH - 1)
            pe.wait_ge(s_M, 1)
            mm(bank(0)[:, 0:CH * NE], tri, RM.rearrange("p c e -> p (c e)"), True, False)
            mm(bank(0)[:, 0:CH * NE], ones, RMP.rearrange("p c e -> p (c e)"), False, True)
            mm(bank(0)[:, CH * NE:CH * NE + NE], ones, CNT, True, True).then_inc(s_rank, 1)
            for n in range(2 * CH):
                c, k = n // 2, n % 2
                pe.wait_ge(s_oh, n + 1)
                last = mm(bank(1)[:, 0:3 * NE], OH[n % 4], RV[:, k, c, :], n == 0, n == 2 * CH - 1)
                last.then_inc(s_ohx, 1)
            def gather_transposes(e, sl):
                for hf in range(2):
                    for j in range(4):
                        k = 4 * hf + j
                        last = nc.tensor.transpose(bank(hf)[:, j * P:j * P + CAP], XG[sl][0:CAP, k * P:k * P + P], ident[0:CAP, 0:CAP])
                    last.then_inc(s_tp, 1)

            def gate_up(j):
                b = bank(2 + j % 2)
                for n in range(4):
                    w = (WG, WU)[n // 2][j]
                    for k in range(KT):
                        last = mm(b[:, n * P:n * P + CAP], w[:, k, (n % 2) * P:(n % 2) * P + P], XGT[j % 2][:, k, 0:CAP], k == 0, k == KT - 1)
                last.then_inc(s_gu, 1)

            def down(j):
                for n in range(2):
                    for f in range(2):
                        last = mm(PS[0:CAP, 2048 + 1024 * (j % 2) + 512 * n:2048 + 1024 * (j % 2) + 512 * n + 512],
                                  AT[j % 2][:, f, 0:CAP], WD[j][:, f, 512 * n:512 * n + 512], f == 0, f == 1)
                last.then_inc(s_y, 1)

            pe.wait_ge(s_idx, 1)
            pe.wait_ge(s_gx[0], 16)
            gather_transposes(0, 0)

            def expert(i, j, first, last):
                e = i * 4 + j
                pe.wait_ge(s_g[j], i * 32 + 32)
                pe.wait_ge(s_xgt, e * 2 + 2)
                if not first:
                    pe.wait_ge(s_at, e - 1)
                gate_up(j)
                if not last:
                    pe.wait_ge(s_gx[(j + 1) % 2], (e + 1 - (j + 1) % 2) * 8 + 16)
                    gather_transposes(e + 1, (j + 1) % 2)
                pe.wait_ge(s_at, e + 1)
                pe.wait_ge(s_wd[j], i * 16 + 16)
                if not first:
                    pe.wait_ge(s_ya, e - 1)
                    pe.wait_ge(s_yd, e - 1)
                down(j)

            for j in range(4):
                expert(0, j, j < 2, False)
            with pe.Fori(1, NE // 4 - 1) as i:
                for j in range(4):
                    expert(i, j, False, False)
            for j in range(4):
                expert(NE // 4 - 1, j, False, j == 3)
            with overflow(pe):
                pe.wait_ge(s_yd, NE)
                pe.wait_ge(s_ya, NE)
                with pe.Fori(0, BLOCKS) as b:
                    for n in range(2 * CH):
                        pe.wait_ge(o_oh, b * 2 * CH + (n + 1))
                        mm(bank(1)[:, 0:4], OH[n % 4], OVAL[:, n % 2, n // 2, :], n == 0, n == 2 * CH - 1).then_inc(o_ohx, 1)
                    pe.wait_ge(o_g, b * 16 + 16)
                    for hf in range(2):
                        for j in range(4):
                            k = 4 * hf + j
                            last = nc.tensor.transpose(bank(hf)[:, j * P:j * P + P], XG[0][:, k * P:k * P + P], ident)
                        last.then_inc(o_tp, 1)
                    pe.wait_ge(o_w, b * 48 + 48)
                    pe.wait_ge(o_xgt, b * 2 + 2)
                    for n in range(4):
                        w = (WG, WU)[n // 2][0]
                        for k in range(KT):
                            last = mm(bank(2)[:, n * P:n * P + P], w[:, k, (n % 2) * P:(n % 2) * P + P], XGT[0][:, k, :], k == 0, k == KT - 1)
                    last.then_inc(o_gu, 1)
                    pe.wait_ge(o_at, b + 1)
                    for n in range(2):
                        for f in range(2):
                            last = mm(bank(4 + n), AT[0][:, f, :], WD[0][:, f, 512 * n:512 * n + 512], f == 0, f == 1)
                    last.then_inc(o_y, 1)
            with pe.Else():
                pe.nop()

        @block.scalar
        def _(act):
            for j in range(splits_of[1][-1] + 1):
                rounded_part(act, j)
            for n in range(1, NPROJ, 2):
                act.wait_ge(s_proj, n + 1)
                proj_out(n, lambda to, src: nc.scalar.activation(to, src, ACT.Copy, scale=proj[n][4])).then_inc(s_pe_a, 1)
                for j in splits_after(n):
                    rounded_part(act, j)

            def evac(n):
                if n % 2:
                    act.wait_ge(s_T, n + 1)
                    transposed_out(act, nc.scalar.copy, n).then_inc(s_Ta, 1)

            def exps(u, s):
                kind, hp, i = units[u]
                w = P * (i + 1) if kind == "w" else N_MEM
                x = 2 * u + s
                act.wait_ge(s_min, x + 1)
                sp = SP[(u % 3) * 2 + s]
                if kind == "c":
                    act.wait_ge(s_T, unit_items[u - 3][-1] + 1)
                src = sp[:, 0:w] if kind == "w" else PS[:, score_at(u, s):score_at(u, s) + w]
                nc.scalar.activation(sp[:, 0:w], src, ACT.Exp, scale=-1.0, bias=MN[:, x:x + 1],
                                     accum_out=DEN[:, x:x + 1]).then_inc(s_exp, 1)

            def x_act(e):
                if e in (("ss", 3), ("ss", 7)):
                    g = e[1] // 4
                    act.wait_ge(s_smin, g + 1)
                    nc.scalar.activation(SS[:, g, 0:NK + SMP], SS[:, g, 0:NK + SMP], ACT.Exp, scale=-1.0,
                                         bias=SMN[:, g:g + 1], accum_out=SDEN[:, g:g + 1]).then_inc(s_sexp, 1)
                if e == ("ms",):
                    act.wait_ge(s_smin, 3)
                    nc.scalar.activation(PMS, bank(xbank[e])[:, 0:N_MEM], ACT.Exp, scale=-1.0,
                                         bias=SMN[:, 2:3], accum_out=SDEN[:, 2:3]).then_inc(s_sexp, 1)

            def spread(u):
                act.wait_ge(s_O, u + 1)
                if u:
                    act.wait_ge(s_OB, u)
                nc.scalar.copy(INV, bank(6 + u % 2)[:, P:2 * P]).then_inc(s_inv, 1)

            exps(0, 0)
            exps(0, 1)
            for u in range(NU):
                mine = unit_items[u]
                small = len(mine) == 1
                for s in range(2):
                    if small and u + 1 < NU:
                        exps(u + 1, s)
                for j, n in enumerate(mine):
                    evac(n)
                    if j == 0 and u:
                        spread(u - 1)
                    for s in range(2):
                        if not small and j == min(2 * s, len(mine) - 1):
                            exps(u + 1, s)
                for e in extra[u]:
                    x_act(e)
                for k in WO_SPLIT_AT.get(u, ()):
                    act.wait_ge(s_wo[k // 4], 16)
                    act.wait_ge(s_S, 2 * 32)
                    act.wait_ge(s_store, 16 * (6 + 2 * DB))
                    full, high, _ = wo_parts(k)
                    nc.scalar.copy(high, full).then_inc(s_hi, 1)
            spread(NU - 1)

            def cat_rounded(c):
                act.wait_ge(s_OB, NU)
                act.wait_ge(s_xe, len(xlist))
                full, high, _ = cat_parts(c)
                nc.scalar.copy(high, full).then_inc(s_hi, 1)

            cat_rounded(0)
            cat_rounded(1)
            def h1t_copy(c):
                m = rows(c)
                for hf in range(2):
                    act.wait_ge(s_ht, 2 * c + hf + 1)
                    if c >= 2:
                        act.wait_ge(s_rt, c - 1)
                    nc.scalar.copy(H1T[c % 2][:, 4 * hf:4 * hf + 4, 0:m],
                                   bank(4 + hf).rearrange("p (j n) -> p j n", j=4)[:, :, 0:m]).then_inc(s_hte, 1)

            for c in range(CH):
                m = rows(c)
                act.wait_ge(s_r, c + 1)
                nc.scalar.activation(MV[0:m, c, 2:3], MV[0:m, c, 1:2], ACT.Sqrt, bias=EPSC[0:m, :]).then_inc(s_std, 1)
                act.wait_ge(s_nrm, c + 1)
                nc.scalar.activation(H1[0:m, c, :], RB[c % 2][0:m, :], ACT.Identity, scale=MV[0:m, c, 2:3],
                                     bias=MV[0:m, c, 3:4]).then_inc(s_z, 1)
                if c + 2 < CH:
                    cat_rounded(c + 2)
                if c >= 1:
                    h1t_copy(c - 1)
            h1t_copy(CH - 1)
            act.wait_ge(s_rx, 1)
            nc.scalar.activation(RX1, RX1, ACT.Exp).then_inc(s_ra, 1)
            act.wait_ge(s_rx, 2)
            nc.scalar.activation(W2, W2, ACT.Exp).then_inc(s_ra, 1)

            def expert(i, j, first):
                e = i * 4 + j
                for hf in range(2):
                    act.wait_ge(s_tp, e * 2 + (hf + 1))
                    if not first:
                        act.wait_ge(s_gu, e - 1)
                    nc.scalar.copy(XGT[j % 2][:, 4 * hf:4 * hf + 4, 0:CAP],
                                   bank(hf).rearrange("p (j n) -> p j n", j=4)[:, :, 0:CAP]).then_inc(s_xgt, 1)

            def silu(i, j, first):
                e = i * 4 + j
                act.wait_ge(s_gu, e + 1)
                if not first:
                    act.wait_ge(s_at, e - 1)
                nc.scalar.activation(SIL[j % 2][:, :, 0:CAP], bank(2 + j % 2)[:, 0:256].rearrange("p (a n) -> p a n", a=2)[:, :, 0:CAP],
                                     ACT.Silu).then_inc(s_sil, 1)

            def y_half(i, j, first):
                e = i * 4 + j
                act.wait_ge(s_y, e + 1)
                if not first:
                    act.wait_ge(s_ys[j % 2], (e - j % 2) * 8)
                nc.scalar.activation(YS[j % 2][0:CAP, 0:512], PS[0:CAP, 2048 + 1024 * (j % 2):2048 + 1024 * (j % 2) + 512], ACT.Copy,
                                     scale=GS[0:CAP, bass.ds(e, 1)]).then_inc(s_ya, 1)

            act.wait_ge(s_idx, 1)
            expert(0, 0, True)
            def turn(i, j, first, last):
                silu(i, j, first)
                if not last:
                    expert(i + (j + 1) // 4, (j + 1) % 4, first and j == 0)
                y_half(i, j, first)
            for j in range(4):
                turn(0, j, j < 2, False)
            with act.Fori(1, NE // 4 - 1) as i:
                for j in range(4):
                    turn(i, j, False, False)
            for j in range(4):
                turn(NE // 4 - 1, j, False, j == 3)
            with overflow(act):
                with act.Fori(0, BLOCKS) as b:
                    for hf in range(2):
                        act.wait_ge(o_tp, b * 2 + (hf + 1))
                        nc.scalar.copy(XGT[0][:, 4 * hf:4 * hf + 4, :], bank(hf).rearrange("p (j n) -> p j n", j=4)).then_inc(o_xgt, 1)
                    act.wait_ge(o_gu, b + 1)
                    nc.scalar.activation(SIL[0].rearrange("p a n -> p (a n)"), bank(2)[:, 0:256], ACT.Silu).then_inc(o_sil, 1)
                    act.wait_ge(o_y, b + 1)
                    nc.scalar.activation(YS[0][:, 0:512], bank(4), ACT.Copy, scale=OLF[:, 2:3]).then_inc(o_ya, 1)
            with act.Else():
                act.nop()
            for c in range(CH):
                m = rows(c)
                act.wait_ge(s_f, c + 1)
                nc.scalar.activation(MV2[0:m, c, 2:3], MV2[0:m, c, 1:2], ACT.Sqrt, bias=EPSC[0:m, :]).then_inc(s_std2, 1)
                act.wait_ge(s_nr2, c + 1)
                nc.scalar.activation(RF[c % 3][0:m, :], RF[c % 3][0:m, :], ACT.Identity, scale=MV2[0:m, c, 2:3],
                                     bias=MV2[0:m, c, 3:4]).then_inc(s_fz, 1)

        @block.vector
        def _(dve):
            step = Steps(dve, s_dve)
            V_ = nc.vector
            step(V_.memset(EPSC, EPS))
            step(V_.memset(UP[:, :, 0:UH], 0.0))
            for j in range(splits_of[1][-1] + 1):
                rest(dve, j)
            for n in range(0, NPROJ, 2):
                dve.wait_ge(s_proj, n + 1)
                proj_out(n, lambda to, src: V_.tensor_scalar(to, src, proj[n][4], None, ALU.mult)).then_inc(s_pe_d, 1)
                for j in splits_after(n):
                    rest(dve, j)
            proj_done(dve, NPROJ - 1)

            def pool_differences(t):
                dve.wait_ge(s_sum, 1)
                for g in range(2):
                    r = slice(64 * g, 64 * g + 64)
                    src = (PA, PBUF)[g]
                    step(V_.tensor_tensor(PA[r, t, UH:UH + 16], src[r, t, UH:UH + 16], pool_inv[r, t, 0:16], ALU.mult))
                    step(V_.tensor_tensor(PA[r, t, UH:UH + 16], PA[r, t, UH:UH + 16], UP[r, t, UH:UH + 16], ALU.subtract))
                    last = V_.scalar_tensor_tensor(PA[r, t, UH + 16:UH + SEQ], src[r, t, UH + 16:UH + SEQ], pool_inv[r, t, 16:17],
                                                   UP[r, t, UH + 16:UH + SEQ], ALU.mult, ALU.subtract)
                last.then_inc(s_pool, 1)
                if t == 0:
                    return
                dve.wait_ge(s_sum, 2)
                for t in range(2):
                    for g in range(2):
                        r = slice(64 * g, 64 * g + 64)
                        src = (SA, SBF)[g]
                        last = V_.scalar_tensor_tensor(SA[r, t, :, PB:PB + DT], src[r, t, :, PB:PB + DT], pool_inv[r, t, 16:17],
                                                       US[r, t, :, PB:PB + DT], ALU.mult, ALU.subtract)
                last.then_inc(s_pool, 1)

            def sample_queries():
                step(V_.memset(at(47760, 1536), 0.0))
                for g in range(2):
                    for hp in range(4):
                        for s in range(2):
                            r = slice(64 * s, 64 * s + 64)
                            last = V_.tensor_copy(QBD[r, g, hp, :, (2 * hp + s) * DT:(2 * hp + s) * DT + DT],
                                                  QT[r, hp, SEQ + 16 * g:SEQ + 16 * g + 16].rearrange("p (b t) -> p b t", t=DT))
                for hp in range(2):
                    for s in range(2):
                        for o in range(2):
                            r = slice(64 * s, 64 * s + 64)
                            c = o * 16 + (2 * hp + s) * DT
                            last = V_.tensor_copy(QBM[r, hp, :, c:c + DT].rearrange("p (b o) t -> p b o t", o=2)[:, :, o, :],
                                                  QC[r, hp, SEQ:TOK].rearrange("p (b o t) -> p b o t", o=2, t=DT)[:, :, o, :])
                last.then_inc(s_srd, 1)

            def mins(u, s):
                kind, hp, i = units[u]
                x = 2 * u + s
                dve.wait_ge(s_S, x + 1)
                ps = PS[:, score_at(u, s):]
                if kind == "w":
                    if i == 0:
                        dve.wait_ge(s_tb[hp % 2], 32 * (hp // 2 + 1))
                    if u >= 3 and s == 0:
                        dve.wait_ge(s_T, unit_items[u - 3][-1] + 1)
                    w = P * (i + 1)
                    V_.tensor_tensor_reduce(SP[(u % 3) * 2 + s][:, 0:w], ps[:, 0:w], TB[hp % 2][s][:, SEQ - w:SEQ],
                                            1.0, 3e38, ALU.add, ALU.min, MN[:, x:x + 1]).then_inc(s_min, 1)
                else:
                    V_.tensor_reduce(MN[:, x:x + 1], ps[:, 0:N_MEM], AX.X, ALU.min).then_inc(s_min, 1)

            def evac(n):
                if n % 2 == 0:
                    dve.wait_ge(s_T, n + 1)
                    transposed_out(dve, V_.tensor_copy, n).then_inc(s_Td, 1)

            def inverse(u):
                dve.wait_ge(s_exp, 2 * u + 2)
                V_.reciprocal(RD[:, 2 * u:2 * u + 2], DEN[:, 2 * u:2 * u + 2]).then_inc(s_rd, 1)

            def o_out(u):
                kind, hp, i = units[u]
                dve.wait_ge(s_inv, u + 1)
                if (kind, hp, i) in (("w", 2, 0), ("c", 0, 0)):
                    dve.wait_ge(s_xp, xnum[("pool", 4) if kind == "w" else ("pv", 1, 3)] + 1)
                b = bank(6 + u % 2)
                V_.tensor_tensor(CAT[:, hp + (0 if kind == "w" else 6), i * P:i * P + P], b[:, 0:P], INV,
                                 ALU.mult).then_inc(s_OB, 1)

            def affine2(c):
                r = RF[c % 3][0:rows(c), 0:LN_SPLIT]
                dve.wait_ge(s_fz, c + 1)
                if c == 0:
                    dve.wait_ge(s_gb2, 32)
                step(V_.tensor_tensor(r, r, GB2[0:rows(c), 0, 0:LN_SPLIT], ALU.mult))
                V_.tensor_tensor(r, r, GB2[0:rows(c), 1, 0:LN_SPLIT], ALU.add).then_inc(s_fo, 1)

            def normalise(g, w, p):
                dve.wait_ge(s_sexp, g + 1)
                step(V_.reciprocal(SRD[:, g:g + 1], SDEN[:, g:g + 1]))
                V_.tensor_scalar(p[:, 0:w], p[:, 0:w], SRD[:, g:g + 1], None, ALU.mult).then_inc(s_srd, 1)

            def x_out(e):
                x = xnum[e]
                dve.wait_ge(s_xp, x + 1)
                bx = bank(xbank[e])
                if e[0] == "knew":
                    V_.tensor_copy(KN[0:SMP, :], bx[0:SMP, :]).then_inc(s_xe, 1)
                elif e[0] == "pool":
                    if e[1] < 4:
                        t, hf = e[1] // 2, e[1] % 2
                        V_.tensor_scalar(CAT[:, 4 + t, 512 * hf:512 * hf + 512], bx, PSC[:, t:t + 1], None, ALU.mult).then_inc(s_xe, 1)
                    else:
                        step(V_.tensor_scalar(CAT[:, 4, SEQ:TOK], bx[:, 0:SMP], PSC[:, 0:1], None, ALU.mult))
                        V_.tensor_scalar(CAT[:, 5, SEQ:TOK], bx[:, SMP:2 * SMP], PSC[:, 1:2], None, ALU.mult).then_inc(s_xe, 1)
                elif e[0] == "ss":
                    g, kc = e[1] // 4, e[1] % 4
                    if e[1] == 0:
                        dve.wait_ge(s_bias, 16)
                        dve.wait_ge(s_pool, 3)
                        dve.wait_ge(s_store, 16 * (6 + 2 * DB))
                    if kc < 3:
                        V_.tensor_tensor(SS[:, g, kc * KC:kc * KC + KC], bx[:, 0:KC], SBIAS[:, kc * KC:kc * KC + KC], ALU.add).then_inc(s_xe, 1)
                    else:
                        step(V_.tensor_tensor(SS[:, g, 3 * KC:4 * KC], bx[:, 0:KC], SBIAS[:, 3 * KC:4 * KC], ALU.add))
                        V_.tensor_tensor(SS[:, g, NK:NK + SMP], bx[:, KC:KC + SMP], SBIAS[:, NK + SMP * g:NK + SMP * g + SMP], ALU.add).then_inc(s_xe, 1)
                        dve.wait_ge(s_xe, x + 1)
                        V_.tensor_reduce(SMN[:, g:g + 1], SS[:, g, 0:NK + SMP], AX.X, ALU.min).then_inc(s_smin, 1)
                        pending.append((g, NK + SMP, SS[:, g, :]))
                elif e[0] == "st":
                    _, g, hf = e
                    if hf == 0:
                        V_.tensor_copy(PTS[:, g, 0:4, :].rearrange("p a b -> p (a b)"), bx).then_inc(s_xe, 1)
                    else:
                        step(V_.tensor_copy(PTS[:, g, 4:7, :].rearrange("p a b -> p (a b)"), bx[:, 0:3 * P]))
                        V_.tensor_copy(PTS[0:SMP, g, 7, :], bx[0:SMP, 3 * P:4 * P]).then_inc(s_xe, 1)
                elif e[0] == "pv":
                    if e[2] == 0:
                        V_.tensor_copy(OA, bx).then_inc(s_xe, 1)
                    else:
                        V_.tensor_tensor(OA, OA, bx, ALU.add).then_inc(s_xe, 1)
                elif e[0] == "ot":
                    g = e[1]
                    for hp in range(4):
                        for s in range(2):
                            r = slice(64 * s, 64 * s + 64)
                            last = V_.tensor_copy(CAT[r, hp, SEQ + 16 * g:SEQ + 16 * g + 16].rearrange("p (b t) -> p b t", t=DT),
                                                  bx[r, hp * P:hp * P + P].rearrange("p (b h t) -> p b h t", b=4, t=DT)[:, :, 2 * hp + s, :])
                    last.then_inc(s_xe, 1)
                elif e[0] == "ms":
                    V_.tensor_reduce(SMN[:, 2:3], bx[:, 0:N_MEM], AX.X, ALU.min).then_inc(s_smin, 1)
                    normalise(2, N_MEM, PMS)
                    dve.wait_ge(s_srd, 4)
                    dve.sem_inc(s_xe, 1)
                elif e[0] == "mt":
                    V_.tensor_copy(PTM.rearrange("p a b -> p (a b)"), bx[:, 0:2 * P]).then_inc(s_xe, 1)
                elif e[0] == "mpv":
                    V_.tensor_copy(OA, bx).then_inc(s_xe, 1)
                else:
                    for o in range(2):
                        for hp in range(2):
                            for s in range(2):
                                r = slice(64 * s, 64 * s + 64)
                                last = V_.tensor_copy(
                                    CAT[r, 6 + hp, SEQ:TOK].rearrange("p (j o t) -> p o j t", o=2, t=DT)[:, o],
                                    bx[r, (2 * o + hp) * P:(2 * o + hp) * P + P].rearrange("p (j o h t) -> p o h j t", j=4, o=2, t=DT)[:, o, 2 * hp + s])
                    last.then_inc(s_xe, 1)

            pending = []
            for e in extra[-1]:
                x_out(e)
            for u in range(2):
                for s in range(2):
                    mins(u, s)
            for u in range(NU):
                for e in pending:
                    normalise(*e)
                pending.clear()
                mine = unit_items[u]
                for j, n in enumerate(mine):
                    evac(n)
                    if j == 0:
                        inverse(u)
                    for s in range(2):
                        if u + 2 < NU and j == min(2 * s, len(mine) - 1):
                            mins(u + 2, s)
                        if u and j == s == 0:
                            o_out(u - 1)
                if u == 2:
                    sample_queries()
                if u == 3:
                    pool_differences(0)
                if u == 4:
                    pool_differences(1)
                for e in extra[u]:
                    x_out(e)
                for k in WO_SPLIT_AT.get(u, ()):
                    full, high, low = wo_parts(k)
                    dve.wait_ge(s_hi, len(splits) + k + 1)
                    V_.tensor_tensor(low, full, high.bitcast(F32), ALU.subtract).then_inc(s_lo, 1)
            o_out(NU - 1)

            def cat_rest(c):
                full, high, low = cat_parts(c)
                dve.wait_ge(s_hi, len(splits) + KT + c + 1)
                V_.tensor_tensor(low, full, high.bitcast(F32), ALU.subtract).then_inc(s_lo, 1)

            cat_rest(0)
            cat_rest(1)
            def affine(c):
                h = H1[0:rows(c), c, :]
                dve.wait_ge(s_z, c + 1)
                if c == 0:
                    dve.wait_ge(s_gb, 64)
                step(V_.tensor_tensor(h, h, GB[0:rows(c), 0, :], ALU.mult))
                V_.tensor_tensor(h, h, GB[0:rows(c), 1, :], ALU.add).then_inc(s_h1, 1)

            for c in range(CH):
                m = rows(c)
                dve.wait_ge(s_mix, c + 1)
                dve.wait_ge(s_x[c % 2], 16 * (c // 2 + 1))
                if c >= 2:
                    dve.wait_ge(s_z, c - 1)
                step(V_.scalar_tensor_tensor(RB[c % 2][0:m, :], XR[c % 2][0:m, :], ALPHA,
                                             PS[0:m, 1024 * (c % 2):1024 * (c % 2) + 1024], ALU.mult, ALU.add))
                for hf in range(2):
                    last = V_.bn_stats(BN[0:m, 0, 6 * hf:6 * hf + 6], RB[c % 2][0:m, 512 * hf:512 * hf + 512])
                step(last)
                V_.bn_aggr(MV[0:m, c, 0:2], BN[0:m, 0, :]).then_inc(s_r, 1)
                dve.wait_ge(s_std, c + 1)
                step(V_.reciprocal(MV[0:m, c, 2:3], MV[0:m, c, 2:3]))
                V_.scalar_tensor_tensor(MV[0:m, c, 3:4], MV[0:m, c, 0:1], -1.0, MV[0:m, c, 2:3], ALU.mult, ALU.mult).then_inc(s_nrm, 1)
                affine(c)
                if c + 2 < CH:
                    cat_rest(c + 2)
            step(V_.memset(LG, 0.0))
            dve.wait_ge(s_rt, CH)
            step(V_.tensor_copy(LG[:, 0:8, :].rearrange("p c e -> p (c e)"), bank(6)[:, 0:288]))
            step(V_.tensor_copy(LG[0:SMP, 8, :], bank(6)[0:SMP, 288:324]))
            dve.wait_ge(s_gb, 64)
            step(V_.tensor_tensor(LG, LG, RT[:, 0:36].unsqueeze(1).broadcast_to([P, CH, 36]), ALU.add))
            L1 = LG[:, :, 0:NG]
            rx1 = RX1.rearrange("p (c e) -> p c e", c=CH)
            m1, p1, v1, v2, r1, r2 = (G1W[:, CH * n:CH * n + CH] for n in range(1, 7))
            g4 = [at(R0 + 1728, CH, 4), at(R0 + 1764, CH, 4)]

            def wide(x, n):
                return x.unsqueeze(2).broadcast_to([P, CH, n])

            def first_max(out, vals, top, n, scratch):
                down_ = CS[:, 3 * P:3 * P + n].unsqueeze(1).broadcast_to([P, CH, n])
                step(V_.tensor_reduce(top, vals, AX.X, ALU.max))
                step(V_.tensor_tensor(scratch, vals, wide(top, n), ALU.is_equal))
                step(V_.tensor_scalar(out, scratch, -1000.0, 1000.0, ALU.mult, ALU.add))
                step(V_.tensor_tensor(out, out, down_, ALU.add))
                step(V_.tensor_reduce(p1, out, AX.X, ALU.min))
                step(V_.tensor_tensor(out, out, wide(p1, n), ALU.is_equal))

            first_max(g4[0], L1, m1, NG, g4[1])
            step(V_.tensor_tensor(rx1, L1, wide(m1, NG), ALU.subtract))
            dve.sem_inc(s_rx, 1)
            step(V_.tensor_scalar(g4[0], g4[0], 1.0, MASKED, ALU.subtract, ALU.mult))
            step(V_.tensor_tensor(RL.rearrange("p c (g e) -> p c g e", g=NG), LG[:, :, NG:36].rearrange("p c (g e) -> p c g e", g=NG),
                                  g4[0].unsqueeze(3).broadcast_to([P, CH, NG, EPG]), ALU.add))
            first_max(RE[0], RL, v1, NE, RX)
            step(V_.tensor_scalar(RX, RE[0], -2.0 * MASKED, None, ALU.mult))
            step(V_.tensor_tensor(RL, RL, RX, ALU.add))
            first_max(RE[1], RL, v2, NE, RX)
            for k in range(2):
                step(V_.tensor_tensor(RE[k], RE[k], wide(valid, NE), ALU.mult))
            step(V_.tensor_tensor(RM, RE[0], RE[1], ALU.add))
            step(V_.memset(RMP[:, 0, :], 0.0))
            for c in range(1, CH):
                step(V_.tensor_tensor(RMP[:, c, :], RMP[:, c - 1, :], RM[:, c - 1, :], ALU.add))
            step(V_.tensor_tensor(CNT, RMP[:, CH - 1, :], RM[:, CH - 1, :], ALU.add))
            dve.sem_inc(s_M, 1)
            step(V_.tensor_tensor(W2, v2, v1, ALU.subtract))
            dve.sem_inc(s_rx, 1)
            dve.wait_ge(s_ra, 1)
            step(V_.tensor_reduce(p1, rx1, AX.X, ALU.add))
            step(V_.reciprocal(p1, p1))
            dve.wait_ge(s_ra, 2)
            step(V_.tensor_scalar(v1, W2, 1.0, None, ALU.add))
            step(V_.reciprocal(v1, v1))
            step(V_.tensor_tensor(v1, v1, p1, ALU.mult))
            step(V_.tensor_tensor(v2, v1, W2, ALU.mult))
            for k in range(2):
                step(V_.tensor_tensor(RV[:, k, :, 0:NE], RE[k], wide(tok1, NE), ALU.mult))
                step(V_.scalar_tensor_tensor(RV[:, k, :, NE:2 * NE], RE[k], float(k * TOK), RV[:, k, :, 0:NE], ALU.mult, ALU.add))
                step(V_.tensor_tensor(RV[:, k, :, 2 * NE:3 * NE], RE[k], wide((v1, v2)[k], NE), ALU.mult))
            dve.wait_ge(s_rank, 1)
            for k in range(2):
                step(V_.tensor_tensor(RX, RE[k], bank(0)[:, 0:CH * NE].rearrange("p (c e) -> p c e", c=CH), ALU.mult))
                step(V_.tensor_reduce((r1, r2)[k], RX, AX.X, ALU.add))
            if CAP < P:
                for x in (r1, r2):
                    step(V_.tensor_scalar(m1, x, float(CAP), 1e6, ALU.is_ge, ALU.mult))
                    step(V_.tensor_tensor(x, x, m1, ALU.add))
            for n in range(2 * CH):
                c, k = n // 2, n % 2
                if n >= 4:
                    dve.wait_ge(s_ohx, n - 3)
                V_.tensor_scalar(OH[n % 4], iota, (r1, r2)[k][:, c:c + 1], None, ALU.is_equal).then_inc(s_oh, 1)
            step(V_.tensor_copy(RANK.rearrange("p c e -> p (c e)"), bank(0)[:, 0:CH * NE]))
            step(V_.tensor_copy(CNT, bank(0)[:, CH * NE:CH * NE + NE]))
            step(V_.tensor_reduce(NB[:, 0:1], CNT, AX.X, ALU.max))
            step(V_.tensor_scalar(FLAG, NB[:, 0:1], float(CAP), None, ALU.is_gt))
            dve.wait_ge(s_ohx, 2 * CH)
            step(V_.tensor_copy(IDF[:, :], bank(1)[:, 0:3 * NE]))
            step(V_.tensor_scalar(RX[:, 0:2, :].rearrange("p a b -> p (a b)"), IDF[:, 0:2 * NE], 0.0, 1e6, ALU.is_equal, ALU.mult))
            step(V_.scalar_tensor_tensor(IDF[:, 0:2 * NE], IDF[:, 0:2 * NE], -1.0, RX[:, 0:2, :].rearrange("p a b -> p (a b)"), ALU.add, ALU.add))
            step(V_.tensor_copy(IDX[:, 0:2 * NE], IDF[:, 0:2 * NE]))
            dve.sem_inc(s_idx, 1)

            def turn(i, j, first):
                e = i * 4 + j
                dve.wait_ge(s_sil, e + 1)
                if not first:
                    dve.wait_ge(s_y, e - 1)
                V_.tensor_tensor(AT[j % 2][:, :, 0:CAP], SIL[j % 2][:, :, 0:CAP],
                                 bank(2 + j % 2)[:, 256:512].rearrange("p (a n) -> p a n", a=2)[:, :, 0:CAP], ALU.mult).then_inc(s_at, 1)
                dve.wait_ge(s_y, e + 1)
                if not first:
                    dve.wait_ge(s_ys[j % 2], (e - j % 2) * 8)
                V_.tensor_scalar(YS[j % 2][0:CAP, 512:1024], PS[0:CAP, 2048 + 1024 * (j % 2) + 512:2048 + 1024 * (j % 2) + 1024],
                                 GS[0:CAP, bass.ds(e, 1)], None, ALU.mult).then_inc(s_yd, 1)

            for j in range(4):
                turn(0, j, j < 2)
            with dve.Fori(1, NE // 4) as i:
                for j in range(4):
                    turn(i, j, False)
            with overflow(dve):
                dve.wait_ge(s_ys[0], 8 * NE)
                dve.wait_ge(s_ys[1], 8 * NE)
                n_o = [0]

                def ostep(ins):
                    n_o[0] += 1
                    ins.then_inc(o_pos, 1)
                    dve.wait_ge(o_pos, n_o[0])

                ostep(V_.memset(NB, 0.0))
                for j in range(1, -(-TOK // CAP)):
                    ostep(V_.scalar_tensor_tensor(NB, CNT, float(j * CAP), NB, ALU.is_gt, ALU.add))
                ostep(V_.tensor_copy(OPRE[0], NB))
                for j in range(5):
                    a, b = OPRE[j % 2], OPRE[(j + 1) % 2]
                    ostep(V_.tensor_copy(b[:, 0:2 ** j], a[:, 0:2 ** j]))
                    ostep(V_.tensor_tensor(b[:, 2 ** j:NE], a[:, 2 ** j:NE], a[:, 0:NE - 2 ** j], ALU.add))
                ostep(V_.tensor_tensor(OTMP, OPRE[1].unsqueeze(1).broadcast_to([P, BLOCKS, NE]),
                                       iota[:, 0:BLOCKS].unsqueeze(2).broadcast_to([P, BLOCKS, NE]), ALU.is_le))
                ostep(V_.tensor_reduce(RX[:, 0, 0:BLOCKS] if BLOCKS <= NE else RX.rearrange("p c e -> p (c e)")[:, 0:BLOCKS], OTMP, AX.X, ALU.add))
                ostep(V_.tensor_scalar(EB, RX.rearrange("p c e -> p (c e)")[:, 0:BLOCKS], float(NE - 1), None, ALU.min))
                dve.sem_inc(o_eb, 1)
                dve.sem_inc(o_free, 1)
                ostep(V_.tensor_tensor(OPRE[0], OPRE[1], NB, ALU.subtract))
                for k in range(2):
                    ostep(V_.tensor_tensor(RX, RE[k], OPRE[0].unsqueeze(1).broadcast_to([P, CH, NE]), ALU.mult))
                    ostep(V_.tensor_reduce(m1, RX, AX.X, ALU.add))
                    ostep(V_.tensor_tensor(RX, RE[k], RANK, ALU.mult))
                    ostep(V_.tensor_reduce(p1, RX, AX.X, ALU.add))
                    ostep(V_.scalar_tensor_tensor(OPOS[:, k, :], m1, float(CAP), p1, ALU.mult, ALU.add))
                    ostep(V_.tensor_scalar(p1, p1, float(CAP), -1e6, ALU.is_lt, ALU.mult))
                    ostep(V_.tensor_tensor(OPOS[:, k, :], OPOS[:, k, :], p1, ALU.add))
                    ostep(V_.tensor_tensor(OVAL[:, k, :, 0], tok1, valid, ALU.mult))
                    ostep(V_.scalar_tensor_tensor(OVAL[:, k, :, 1], valid, float(k * TOK), OVAL[:, k, :, 0], ALU.mult, ALU.add))
                    ostep(V_.tensor_tensor(OVAL[:, k, :, 2], (v1, v2)[k], valid, ALU.mult))
                    ostep(V_.memset(OVAL[:, k, :, 3], 0.0))
                per_block = 5
                with dve.Fori(0, BLOCKS) as b:
                    def bstep(ins, n):
                        ins.then_inc(o_pos, 1)
                        dve.wait_ge(o_pos, b * per_block + (n_o[0] + n))

                    dve.wait_ge(o_free, b + 1)
                    bstep(V_.tensor_scalar(OPOS, OPOS, float(CAP), None, ALU.subtract), 1)
                    for n in range(2 * CH):
                        if n >= 4:
                            dve.wait_ge(o_ohx, b * 2 * CH + (n - 3))
                        V_.tensor_scalar(OH[n % 4], iota, OPOS[:, n % 2, n // 2:n // 2 + 1], None, ALU.is_equal).then_inc(o_oh, 1)
                    dve.wait_ge(o_ohx, b * 2 * CH + 2 * CH)
                    bstep(V_.tensor_copy(OLF, bank(1)[:, 0:4]), 2)
                    bstep(V_.tensor_scalar(OPRE[0][:, 0:2], OLF[:, 0:2], 0.0, 1e6, ALU.is_equal, ALU.mult), 3)
                    bstep(V_.scalar_tensor_tensor(OPRE[0][:, 0:2], OLF[:, 0:2], -1.0, OPRE[0][:, 0:2], ALU.add, ALU.add), 4)
                    bstep(V_.tensor_copy(OLI, OPRE[0][:, 0:2]), 5)
                    dve.sem_inc(o_idx, 1)
                    dve.wait_ge(o_sil, b + 1)
                    V_.tensor_tensor(AT[0].rearrange("p a n -> p (a n)"), SIL[0].rearrange("p a n -> p (a n)"),
                                     bank(2)[:, 256:512], ALU.mult).then_inc(o_at, 1)
                    dve.wait_ge(o_ya, b + 1)
                    V_.tensor_scalar(YS[0][:, 512:1024], bank(5), OLF[:, 2:3], None, ALU.mult).then_inc(o_yd, 1)
            with dve.Else():
                dve.nop()
            dve.wait_ge(s_y, NE)
            for c in range(CH):
                m = rows(c)
                r = RF[c % 3][0:m, :]
                dve.wait_ge(s_yp[c % 3], 16 * (c // 3 + 1))
                if c >= 3:
                    dve.wait_ge(s_out[c % 3], 16 * (c // 3))
                step(V_.scalar_tensor_tensor(r, H1[0:m, c, :], ALPHA, YP[c % 3][0:m, 0, :], ALU.mult, ALU.add))
                V_.tensor_tensor(r, r, YP[c % 3][0:m, 1, :], ALU.add).then_inc(s_f1, 1)
                dve.wait_ge(s_f1, c + 1)
                for hf in range(2):
                    last = V_.bn_stats(BN[0:m, 1, 6 * hf:6 * hf + 6], r[:, 512 * hf:512 * hf + 512])
                step(last)
                V_.bn_aggr(MV2[0:m, c, 0:2], BN[0:m, 1, :]).then_inc(s_f, 1)
                if c:
                    affine2(c - 1)
                dve.wait_ge(s_std2, c + 1)
                step(V_.reciprocal(MV2[0:m, c, 2:3], MV2[0:m, c, 2:3]))
                V_.scalar_tensor_tensor(MV2[0:m, c, 3:4], MV2[0:m, c, 0:1], -1.0, MV2[0:m, c, 2:3], ALU.mult, ALU.mult).then_inc(s_nr2, 1)
            affine2(CH - 1)

        @block.gpsimd
        def _(pool):
            step = Steps(pool, s_pl)
            G = nc.gpsimd
            wv = I["w_in"].rearrange("(k p) n -> p k n", p=P)
            proj_done(pool, last_of[0])
            G.dma_start(WF[0], wv[:, :, 1024:1536]).then_inc(s_w[2], 16)
            proj_done(pool, last_of[1])
            G.dma_start(WF[1], wv[:, :, 1536:2048]).then_inc(s_w[3], 16)
            proj_done(pool, last_of[2])
            G.dma_start(WF[0], I["w_mem_kv"].rearrange("(k p) n -> p k n", p=P)).then_inc(s_w[4], 16)
            G.dma_start(MT, I["memT"].rearrange("(k p) n -> p k n", p=P)).then_inc(s_mem, 16)
            proj_done(pool, n_x - 1)
            pool.wait_ge(s_state, 48)
            pool.wait_ge(s_dve, 2)
            pool.wait_ge(s_const, 16)

            def sums(u, a, b, n, ap):
                step(G.tensor_tensor(ap(a, 0, 1, n), ap(u, 0, 1, n), ap(u, 0, 0, n - 1), ALU.add))
                step(G.tensor_tensor(ap(b, 0, 3, n), ap(a, 0, 3, n), ap(a, 0, 1, n - 2), ALU.add))
                step(G.tensor_tensor(ap(a, 1, 7, n), ap(b, 1, 7, n), ap(b, 1, 3, n - 4), ALU.add))
                step(G.tensor_tensor(ap(b, 1, 15, n), ap(a, 1, 15, n), ap(a, 1, 7, n - 8), ALU.add))

            def prompt_ap(x, t0, lo, hi):
                return x[:, t0:2, lo:hi]

            def sample_ap(x, t0, lo, hi):
                return x[:, t0, :, lo:hi] if t0 else x[:, :, :, lo:hi]

            sums(UP, PA, PBUF, UH + SEQ, prompt_ap)
            pool.sem_inc(s_sum, 1)
            sums(US, SA, SBF, PB + DT, sample_ap)
            pool.sem_inc(s_sum, 1)
            for u in range(NU):
                pool.wait_ge(s_rd, u + 1)
                if u >= 2:
                    pool.wait_ge(s_O, u - 1)
                for s in range(2):
                    last = G.tensor_scalar(DG[u % 2][:, s, :], ident, RD[:, 2 * u + s:2 * u + s + 1], None, ALU.mult)
                last.then_inc(s_dg, 1)
            pool.wait_ge(s_mix, CH)
            for sl in range(2):
                last = G.memset(XG[sl], 0.0)
            last.then_inc(s_zero, 1)
            pool.wait_ge(s_zero, 1)
            pool.wait_ge(s_idx, 1)
            pool.wait_ge(s_h1d, 16 * CH)

            def await_(sem_, count):
                pool.wait_ge(sem_, count)
                pool.sem_inc(s_past, 1)

            def column(dst, src, count):
                G.tensor_copy(dst, src).then_inc(s_col, 1)
                await_(s_col, count)

            last_token, last_pair = pool.to_reg(TOK - 1), pool.to_reg(NPAIR - 1)

            def gather(e, sl, count):
                column(GI[sl], e, count)
                G.indirect_dma_start(XG[sl][0:CAP, :], None, h1_d, bass.IndirectOffsetOnAxis(ap=GI[sl][0:CAP, :], axis=0),
                                     bounds_check=last_token, oob_is_err=False).then_inc(s_gx[sl], 16)

            def scatter(e, sl, count):
                column(SI[sl], e, count)
                G.indirect_dma_start(pair_d, bass.IndirectOffsetOnAxis(ap=SI[sl][0:CAP, :], axis=0), YS[sl][0:CAP, :], None,
                                     bounds_check=last_pair, oob_is_err=False).then_inc(s_ys[sl], 16)

            gather(IDX[:, 0:1], 0, 1)
            gather(IDX[:, 1:2], 1, 2)
            def turn(i, j, last):
                e = i * 4 + j
                to_gather = IDX[:, bass.ds(e + 2, 1)] if last else IDX[:, bass.ds(pool.snap(e + 2), 1)] if not isinstance(i, int) else IDX[:, e + 2:e + 3]
                to_scatter = IDX[:, bass.ds(pool.snap(e + NE), 1)] if not isinstance(i, int) else IDX[:, NE + e:NE + e + 1]
                if not last:
                    pool.wait_ge(s_tp, e * 2 + 2)
                    gather(to_gather, j % 2, e * 2 + 3)
                pool.wait_ge(s_ya, e + 1)
                pool.wait_ge(s_yd, e + 1)
                scatter(to_scatter, j % 2, e * 2 + 4 if not last else NE + e + 1)

            with pool.Fori(0, NE // 4 - 1) as i:
                for j in range(4):
                    turn(i, j, False)
            for j in range(4):
                turn(NE // 4 - 1, j, j >= 2)
            with overflow(pool):
                with pool.Fori(0, BLOCKS) as b:
                    await_(o_idx, b + 1)
                    G.indirect_dma_start(XG[0], None, h1_d, bass.IndirectOffsetOnAxis(ap=OLI[:, 0:1], axis=0),
                                         bounds_check=last_token, oob_is_err=False).then_inc(o_g, 16)
                    await_(o_yd, b + 1)
                    G.indirect_dma_start(pair_d, bass.IndirectOffsetOnAxis(ap=OLI[:, 1:2], axis=0), YS[0], None,
                                         bounds_check=last_pair, oob_is_err=False).then_inc(o_s, 16)
                    pool.wait_ge(o_s, b * 16 + 16)
                    pool.sem_inc(o_free, 1)
            with pool.Else():
                pool.nop()
            for c in range(CH):
                r = RF[c % 3][0:rows(c), LN_SPLIT:D]
                pool.wait_ge(s_fz, c + 1)
                if c == 0:
                    pool.wait_ge(s_gb2, 32)
                step(G.tensor_tensor(r, r, GB2[0:rows(c), 0, LN_SPLIT:D], ALU.mult))
                G.tensor_tensor(r, r, GB2[0:rows(c), 1, LN_SPLIT:D], ALU.add).then_inc(s_fp, 1)


_OUT = {"y": (TOK, D), "kT": (D_A, SEQ), "v": (SEQ, D_A), "uT": (D_B, PB), "kmT": (D_C, N_MEM), "vm": (N_MEM, D_C),
        "win_k_s": (DB, WB, D_A), "win_v_s": (DB, WB, D_A), "poolT_s": (P, 2 * DB, PB)}


def laid_out(i):
    a = {n: np.asarray(v) for n, v in i.items()}
    x = np.concatenate([a["x_prompt"].reshape(SEQ, D), a["x_sample"].reshape(SMP, D)])
    wk = a["cache_win_k"][0][:, ROWS].reshape(2, 4, 4, KC, 4, 2, HD)
    wk = wk.transpose(0, 3 - 1, 5, 6, 4, 1, 3).reshape(8, P, 4, 4 * KC)
    mk = a["cache_mem_k"][0].reshape(DB, N_MEM, 2, 2, HD).transpose(3, 4, 2, 0, 1).reshape(P, 2, DB * N_MEM)
    out = {
        "x": x, "xT": x.T, "memT": a["mem_prompt"][0].T, "stateT": a["state_pool"][0].transpose(2, 0, 1).reshape(2, P, DB, PB).transpose(1, 0, 2, 3).reshape(P, 2 * DB, PB),
        "winkT": wk, "memkT": mk,
        "cache_win_k": a["cache_win_k"].reshape(DB, WB, D_A), "cache_win_v": a["cache_win_v"].reshape(DB, WB, D_A),
        "cache_mem_v": a["cache_mem_v"].reshape(DB, N_MEM, D_C),
        "w_in": a["w_in"][0], "w_mem_kv": a["w_mem_kv"][0], "w_pool": a["w_pool"][0], "pool_scale": a["pool_scale"][0].reshape(2, P).T,
        "w_o": a["w_o"][0], "w_r": np.concatenate([a["w_r1"][0], a["w_r2"][0].transpose(1, 0, 2).reshape(D, NE)], axis=1),
        "b_r": np.concatenate([a["b_r1"][0], a["b_r2"][0].reshape(NE)]),
        "w_gate": a["w_gate"].reshape(NE, D, DE), "w_up": a["w_up"].reshape(NE, D, DE), "w_down": a["w_down"].reshape(NE, DE, D),
        **{n: a[n][0] for n in ("ln1_g", "ln1_b", "ln2_g", "ln2_b")}, **shape_constants(),
    }
    return {n: np.ascontiguousarray(v) for n, v in out.items()}


def results(r):
    y = r["y"]
    heads = lambda t, n: t.reshape(1, 1, -1, n, HD)
    return (y[:SEQ].reshape(1, SEQ, D), y[SEQ:].reshape(DB, DT, D),
            heads(np.ascontiguousarray(r["kT"].T), HA), heads(r["v"], HA),
            np.ascontiguousarray(r["uT"].T).reshape(1, 1, PB, D_B),
            heads(np.ascontiguousarray(r["kmT"].T), HC), heads(r["vm"], HC),
            r["win_k_s"].reshape(1, DB, WB, HA, HD), r["win_v_s"].reshape(1, DB, WB, HA, HD),
            np.ascontiguousarray(r["poolT_s"].reshape(P, 2, DB, PB).transpose(2, 3, 1, 0)).reshape(1, DB, PB, D_B))


def kernel(**inputs):
    import concourse.bacc as _bacc
    from concourse.bass_utils import run_bass_kernel_spmd as _run

    nc = _bacc.Bacc("TRN2", target_bir_lowering=False, num_devices=1)
    arrays = laid_out(inputs)
    ins = {n: nc.dram_tensor(n, a.shape, F32, kind="ExternalInput").ap() for n, a in arrays.items()}
    outs = {n: nc.dram_tensor("out_" + n, s, F32, kind="ExternalOutput").ap() for n, s in _OUT.items()}
    build(nc, ins, outs)
    r = _run(nc, [arrays], core_ids=[0])
    return results({n: r.results[0]["out_" + n] for n in _OUT})
```
